# Optimizing a Trainium2 kernel written in Bass

```python
import math
import jax, jax.numpy as jnp
from jax import lax
import numpy as np

D_MODEL = 1024
BATCH = 1
SEQ = 256
DEPTH = 2

DA_HEADS = 4
DA_HEAD_DIM = 64
DA_WIDTH = DA_HEADS * 2 * DA_HEAD_DIM
CONV_CH = 512
CONV_WIDTH = 31
SB_HEADS = 8
SB_HEAD_DIM = 64
SB_WIDTH = SB_HEADS * SB_HEAD_DIM
N_BRANCH = 3
Q_BLOCK = 128
ROPE_THETA = 10000.0
MAX_POS_OFFSET = 1024
EPS = 1e-6
NEG_INF = -1e30
IN_SIZES = (DA_WIDTH, DA_WIDTH, DA_WIDTH, 2 * CONV_CH, SB_WIDTH, SB_WIDTH, SB_WIDTH, N_BRANCH * D_MODEL)
IN_COLS = sum(IN_SIZES)
IN_SPLITS = tuple(int(v) for v in np.cumsum(IN_SIZES)[:-1])
N_EXPERTS = 64
TOP_K = 8
N_GROUPS = 8
TOPK_GROUPS = 4
EXPERT_FF = 256
SHARED_FF = 256
ROUTED_SCALE = 2.5
EXPERT_BLOCK = 128


def rms_norm(x, g):
    xf = x.astype(jnp.float32)
    y = xf * lax.rsqrt(jnp.mean(xf * xf, axis=-1, keepdims=True) + EPS)
    return (y * g.astype(jnp.float32)).astype(x.dtype)

def layer_norm(x, g, b):
    xf = x.astype(jnp.float32)
    mu = jnp.mean(xf, axis=-1, keepdims=True)
    var = jnp.mean(jnp.square(xf - mu), axis=-1, keepdims=True)
    y = (xf - mu) * lax.rsqrt(var + EPS) * g.astype(jnp.float32) + b.astype(jnp.float32)
    return y.astype(x.dtype)

def rope_tables(positions, dim):
    inv = ROPE_THETA ** (-jnp.arange(0, dim, 2, dtype=jnp.float32) / dim)
    ang = positions.astype(jnp.float32)[..., None] * inv
    return jnp.cos(ang)[:, :, None, :], jnp.sin(ang)[:, :, None, :]

def apply_rope(x, cos, sin):
    x1, x2 = jnp.split(x, 2, axis=-1)
    c = cos.astype(x.dtype)
    s = sin.astype(x.dtype)
    return jnp.concatenate([x1 * c - x2 * s, x2 * c + x1 * s], axis=-1)

def to_blocks(x):
    b, s = x.shape[:2]
    x = x.reshape((b, s // Q_BLOCK, Q_BLOCK) + x.shape[2:])
    return jnp.moveaxis(x, 1, 0)

def from_blocks(y):
    y = jnp.moveaxis(y, 0, 1)
    return y.reshape((y.shape[0], y.shape[1] * y.shape[2]) + y.shape[3:])

def diff_attention(q, k, v, lam, lambda_init, subln_g):
    S = k.shape[1]
    n_blocks = S // Q_BLOCK
    scale = DA_HEAD_DIM ** -0.5
    kpos = jnp.arange(S)

    def block(args):
        qb, start = args
        s = jnp.einsum('bqhmd,bkhmd->bhmqk', qb, k).astype(jnp.float32) * scale
        qpos = start + jnp.arange(Q_BLOCK)
        causal = kpos[None, :] <= qpos[:, None]
        p = jax.nn.softmax(jnp.where(causal, s, NEG_INF), axis=-1)
        a = p[:, :, 0] - lam * p[:, :, 1]
        return jnp.einsum('bhqk,bkhe->bqhe', a.astype(v.dtype), v)

    starts = jnp.arange(n_blocks, dtype=jnp.int32) * Q_BLOCK
    o = from_blocks(lax.map(block, (to_blocks(q), starts)))
    o = rms_norm(o, subln_g) * (1.0 - lambda_init)
    return o.reshape(o.shape[0], S, DA_WIDTH)

def stick_breaking(q, k, v):
    S = k.shape[1]
    n_blocks = S // Q_BLOCK
    scale = SB_HEAD_DIM ** -0.5
    kpos = jnp.arange(S)

    def block(args):
        qb, start = args
        z = jnp.einsum('bqhd,bkhd->bhqk', qb, k).astype(jnp.float32) * scale
        qpos = start + jnp.arange(Q_BLOCK)
        before = kpos[None, :] < qpos[:, None]
        log_beta = jax.nn.log_sigmoid(z)
        log_one_minus = jnp.where(before, jax.nn.log_sigmoid(-z), 0.0)
        key_axis = log_one_minus.ndim - 1
        suffix = lax.cumsum(log_one_minus, axis=key_axis, reverse=True) - log_one_minus
        a = jnp.where(before, jnp.exp(log_beta + suffix), 0.0)
        return jnp.einsum('bhqk,bkhd->bqhd', a.astype(v.dtype), v)

    starts = jnp.arange(n_blocks, dtype=jnp.int32) * Q_BLOCK
    o = from_blocks(lax.map(block, (to_blocks(q), starts)))
    return o.reshape(o.shape[0], S, SB_WIDTH)

def conformer_conv(u, w_dw, b_dw, ln_g, ln_b):
    a, g = jnp.split(u, 2, axis=-1)
    h = a * jax.nn.sigmoid(g)
    h = lax.conv_general_dilated(
        h, w_dw[:, None, :].astype(h.dtype), window_strides=(1,),
        padding=[(CONV_WIDTH - 1, 0)], dimension_numbers=('NWC', 'WIO', 'NWC'),
        feature_group_count=CONV_CH) + b_dw
    return jax.nn.silu(layer_norm(h, ln_g, ln_b))

def mixer(h, cos, sin, lambda_init, w_in, qn_g, kn_g, lam_q1, lam_k1, lam_q2, lam_k2, subln_g,
          w_proj_a, w_dw, b_dw, conv_ln_g, conv_ln_b, w_proj_b, b_proj_b, w_proj_c, w_out):
    B, S, _ = h.shape
    proj = h @ w_in
    qa, ka, va, ub, qc, kc, vc, gates = jnp.split(proj, IN_SPLITS, axis=-1)

    qa = apply_rope(rms_norm(qa.reshape(B, S, 2 * DA_HEADS, DA_HEAD_DIM), qn_g), cos, sin)
    ka = apply_rope(rms_norm(ka.reshape(B, S, 2 * DA_HEADS, DA_HEAD_DIM), kn_g), cos, sin)
    qa = qa.reshape(B, S, DA_HEADS, 2, DA_HEAD_DIM)
    ka = ka.reshape(B, S, DA_HEADS, 2, DA_HEAD_DIM)
    va = va.reshape(B, S, DA_HEADS, 2 * DA_HEAD_DIM)
    lam = (jnp.exp(jnp.sum(lam_q1.astype(jnp.float32) * lam_k1.astype(jnp.float32)))
           - jnp.exp(jnp.sum(lam_q2.astype(jnp.float32) * lam_k2.astype(jnp.float32)))
           + lambda_init)
    y_a = diff_attention(qa, ka, va, lam, lambda_init, subln_g) @ w_proj_a

    y_b = conformer_conv(ub, w_dw, b_dw, conv_ln_g, conv_ln_b) @ w_proj_b + b_proj_b

    y_c = stick_breaking(qc.reshape(B, S, SB_HEADS, SB_HEAD_DIM),
                         kc.reshape(B, S, SB_HEADS, SB_HEAD_DIM),
                         vc.reshape(B, S, SB_HEADS, SB_HEAD_DIM)) @ w_proj_c

    g = jax.nn.sigmoid(gates.reshape(B, S, N_BRANCH, D_MODEL))
    merged = g[:, :, 0] * y_a + g[:, :, 1] * y_b + g[:, :, 2] * y_c
    return merged @ w_out

def swiglu(x, w1, w3, w2):
    return (jax.nn.silu(x @ w1) * (x @ w3)) @ w2

def moe_ffn(u, w_router, b_router, w1, w3, w2, ws1, ws3, ws2):
    B, S, D = u.shape
    T = B * S
    xf = u.reshape(T, D)
    scores = jax.nn.sigmoid((xf @ w_router).astype(jnp.float32))
    biased = scores + b_router.astype(jnp.float32)
    grouped = biased.reshape(T, N_GROUPS, N_EXPERTS // N_GROUPS)
    group_score = jnp.sum(lax.top_k(grouped, 2)[0], axis=-1)
    _, top_groups = lax.top_k(group_score, TOPK_GROUPS)
    group_mask = jnp.any(top_groups[..., None] == jnp.arange(N_GROUPS), axis=-2)
    expert_mask = jnp.repeat(group_mask, N_EXPERTS // N_GROUPS, axis=-1)
    _, idx = lax.top_k(jnp.where(expert_mask, biased, NEG_INF), TOP_K)
    w = jnp.take_along_axis(scores, idx, axis=-1)
    w = w / (jnp.sum(w, axis=-1, keepdims=True) + 1e-20) * ROUTED_SCALE

    TK = T * TOP_K
    flat_e = idx.reshape(TK).astype(jnp.int32)
    flat_tok = jnp.arange(TK, dtype=jnp.int32) // TOP_K
    flat_w = w.reshape(TK)
    order = jnp.argsort(flat_e)
    se, st, sw = flat_e[order], flat_tok[order], flat_w[order]
    counts = jnp.bincount(flat_e, length=N_EXPERTS).astype(jnp.int32)
    starts = jnp.cumsum(counts) - counts
    padded = (counts + EXPERT_BLOCK - 1) // EXPERT_BLOCK * EXPERT_BLOCK
    pad_ends = jnp.cumsum(padded)
    pad_starts = pad_ends - padded
    dest = pad_starts[se] + (jnp.arange(TK, dtype=jnp.int32) - starts[se])
    n_blocks = (TK + N_EXPERTS * (EXPERT_BLOCK - 1) + EXPERT_BLOCK - 1) // EXPERT_BLOCK
    n_slots = n_blocks * EXPERT_BLOCK
    slot_tok = jnp.full((n_slots,), T, jnp.int32).at[dest].set(st)
    slot_w = jnp.zeros((n_slots,), jnp.float32).at[dest].set(sw)
    block_e = jnp.minimum(jnp.searchsorted(pad_ends, jnp.arange(n_blocks, dtype=jnp.int32) * EXPERT_BLOCK,
                                           side='right'), N_EXPERTS - 1).astype(jnp.int32)
    xpad = jnp.concatenate([xf, jnp.zeros((1, D), xf.dtype)], axis=0)

    def expert_block(args):
        toks, e, wts = args
        out = swiglu(xpad[toks], w1[e], w3[e], w2[e])
        return out * wts[:, None].astype(out.dtype)

    y = lax.map(expert_block, (slot_tok.reshape(n_blocks, EXPERT_BLOCK), block_e,
                               slot_w.reshape(n_blocks, EXPERT_BLOCK)))
    routed = jax.ops.segment_sum(y.reshape(n_slots, D), slot_tok, num_segments=T + 1)[:T]
    shared = swiglu(xf, ws1, ws3, ws2)
    return (routed + shared).reshape(B, S, D)

def first_inputs(seed: int = 0) -> dict:
    key = jax.random.key(seed)
    ks = iter(jax.random.split(key, 40))
    L = DEPTH

    def nrm(shape, s):
        return jax.random.normal(next(ks), shape, jnp.float32) * s

    def gain(shape):
        return 1.0 + nrm(shape, 0.02)

    D = D_MODEL
    x = nrm((BATCH, SEQ, D), 1.0)
    c = nrm((BATCH, D), 1.0)
    positions = (jnp.arange(SEQ, dtype=jnp.int32)[None, :]
                 + jax.random.randint(next(ks), (BATCH, 1), 0, MAX_POS_OFFSET, dtype=jnp.int32))
    return {
        "x": x, "c": c, "positions": positions,
        "w_mod": nrm((L, D, 6 * D), 0.3 * D ** -0.5),
        "b_mod": nrm((L, 6 * D), 0.02),
        "norm_mix_g": gain((L, D)),
        "norm_ffn_g": gain((L, D)),
        "w_in": nrm((L, D, IN_COLS), D ** -0.5),
        "qn_g": gain((L, DA_HEAD_DIM)),
        "kn_g": gain((L, DA_HEAD_DIM)),
        "lam_q1": nrm((L, DA_HEAD_DIM), 0.1),
        "lam_k1": nrm((L, DA_HEAD_DIM), 0.1),
        "lam_q2": nrm((L, DA_HEAD_DIM), 0.1),
        "lam_k2": nrm((L, DA_HEAD_DIM), 0.1),
        "subln_g": gain((L, 2 * DA_HEAD_DIM)),
        "w_proj_a": nrm((L, DA_WIDTH, D), DA_WIDTH ** -0.5),
        "w_dw": nrm((L, CONV_WIDTH, CONV_CH), CONV_WIDTH ** -0.5),
        "b_dw": nrm((L, CONV_CH), 0.02),
        "conv_ln_g": gain((L, CONV_CH)),
        "conv_ln_b": nrm((L, CONV_CH), 0.02),
        "w_proj_b": nrm((L, CONV_CH, D), CONV_CH ** -0.5),
        "b_proj_b": nrm((L, D), 0.02),
        "w_proj_c": nrm((L, SB_WIDTH, D), SB_WIDTH ** -0.5),
        "w_out": nrm((L, D, D), D ** -0.5),
        "w_router": nrm((L, D, N_EXPERTS), D ** -0.5),
        "b_router": nrm((L, N_EXPERTS), 0.01),
        "w1": nrm((L, N_EXPERTS, D, EXPERT_FF), D ** -0.5),
        "w3": nrm((L, N_EXPERTS, D, EXPERT_FF), D ** -0.5),
        "w2": nrm((L, N_EXPERTS, EXPERT_FF, D), EXPERT_FF ** -0.5),
        "ws1": nrm((L, D, SHARED_FF), D ** -0.5),
        "ws3": nrm((L, D, SHARED_FF), D ** -0.5),
        "ws2": nrm((L, SHARED_FF, D), SHARED_FF ** -0.5),
    }

def first_block(x, c, positions, w_mod, b_mod, norm_mix_g, norm_ffn_g, w_in, qn_g, kn_g,
              lam_q1, lam_k1, lam_q2, lam_k2, subln_g, w_proj_a, w_dw, b_dw, conv_ln_g, conv_ln_b,
              w_proj_b, b_proj_b, w_proj_c, w_out, w_router, b_router, w1, w3, w2, ws1, ws3, ws2):
    cos, sin = rope_tables(positions, DA_HEAD_DIM)
    c_act = jax.nn.silu(c)
    for l in range(DEPTH):
        lambda_init = 0.8 - 0.6 * math.exp(-0.3 * l)
        mod = c_act @ w_mod[l] + b_mod[l]
        sh_m, sc_m, g_m, sh_f, sc_f, g_f = [m[:, None, :] for m in jnp.split(mod, 6, axis=-1)]
        h = rms_norm(x, norm_mix_g[l]) * (1.0 + sc_m) + sh_m
        x = x + g_m * mixer(h, cos, sin, lambda_init, w_in[l], qn_g[l], kn_g[l], lam_q1[l], lam_k1[l],
                            lam_q2[l], lam_k2[l], subln_g[l], w_proj_a[l], w_dw[l], b_dw[l],
                            conv_ln_g[l], conv_ln_b[l], w_proj_b[l], b_proj_b[l], w_proj_c[l], w_out[l])
        h = rms_norm(x, norm_ffn_g[l]) * (1.0 + sc_f) + sh_f
        x = x + g_f * moe_ffn(h, w_router[l], b_router[l], w1[l], w3[l], w2[l], ws1[l], ws3[l], ws2[l])
    return x


ROPE_THETA_2 = 500000.0
NEG = -1e30

GROUP_WIDTH = D_MODEL // 4
D_MIX = 4 * GROUP_WIDTH

MLA_HEADS = 4
MLA_NOPE = 64
MLA_ROPE = 32
MLA_QK = MLA_NOPE + MLA_ROPE
MLA_V = GROUP_WIDTH // MLA_HEADS
MLA_Q_RANK = 256
MLA_KV_RANK = 128

CONV_WIDTH_2 = 3

SG_CHUNK = 128
SG_GROUPS = 4
SG_GDIM = GROUP_WIDTH // SG_GROUPS

MOBA_HEADS = 4
MOBA_HD = GROUP_WIDTH // MOBA_HEADS
MOBA_ROT = MOBA_HD // 4
MOBA_BLOCK = 256
MOBA_TOPK = 3

SPLIT_SIZES = (
    MLA_Q_RANK, MLA_KV_RANK, MLA_ROPE, GROUP_WIDTH,
    GROUP_WIDTH, GROUP_WIDTH, GROUP_WIDTH, GROUP_WIDTH,
    GROUP_WIDTH, GROUP_WIDTH, GROUP_WIDTH,
    GROUP_WIDTH, GROUP_WIDTH, GROUP_WIDTH, GROUP_WIDTH,
)
D_IN = 3488


def rmsnorm(x, g):
    xf = x.astype(jnp.float32)
    y = xf * lax.rsqrt(jnp.mean(xf * xf, axis=-1, keepdims=True) + EPS)
    return (y * g).astype(x.dtype)

def layernorm(x, g, b):
    xf = x.astype(jnp.float32)
    mu = jnp.mean(xf, axis=-1, keepdims=True)
    var = jnp.mean(jnp.square(xf - mu), axis=-1, keepdims=True)
    y = (xf - mu) * lax.rsqrt(var + EPS)
    return (y * g + b).astype(x.dtype)

def rope(x, pos):
    rd = x.shape[-1]
    half = rd // 2
    inv = jnp.power(ROPE_THETA_2, -jnp.arange(half, dtype=jnp.float32) * 2.0 / rd)
    ang = pos.astype(jnp.float32)[..., None] * inv
    cos = jnp.cos(ang)[:, :, None, :]
    sin = jnp.sin(ang)[:, :, None, :]
    xf = x.astype(jnp.float32)
    x1, x2 = xf[..., :half], xf[..., half:]
    return jnp.concatenate([x1 * cos - x2 * sin, x2 * cos + x1 * sin], axis=-1).astype(x.dtype)

def causal_attention_blocks(q, k, v, scale):
    B, S, H, D = q.shape
    nq = S // Q_BLOCK
    qb = q.reshape(B, nq, Q_BLOCK, H, D).swapaxes(0, 1)
    kpos = jnp.arange(S)

    def one(args):
        qblk, i = args
        s = jnp.einsum('bqhd,bkhd->bhqk', qblk, k, preferred_element_type=jnp.float32) * scale
        qpos = i * Q_BLOCK + jnp.arange(Q_BLOCK)
        s = jnp.where(kpos[None, :] <= qpos[:, None], s, NEG)
        p = jax.nn.softmax(s, axis=-1)
        return jnp.einsum('bhqk,bkhd->bqhd', p.astype(v.dtype), v)

    out = lax.map(one, (qb, jnp.arange(nq)))
    return out.swapaxes(0, 1).reshape(B, S, H, v.shape[-1])

def moba_attention(q, k, v, scale):
    B, S, H, D = q.shape
    nb = -(-S // MOBA_BLOCK)
    Sp = nb * MOBA_BLOCK
    kk = min(MOBA_TOPK, nb)
    pad = ((0, 0), (0, Sp - S), (0, 0), (0, 0))
    kb = jnp.pad(k, pad).reshape(B, nb, MOBA_BLOCK, H, D).transpose(0, 3, 1, 2, 4)
    vb = jnp.pad(v, pad).reshape(B, nb, MOBA_BLOCK, H, D).transpose(0, 3, 1, 2, 4)
    kmean = jnp.mean(kb.astype(jnp.float32), axis=3)
    gate = jnp.einsum('bshd,bhnd->bhsn', q.astype(jnp.float32), kmean)
    qblk = jnp.arange(S) // MOBA_BLOCK
    past = jnp.arange(nb)[None, :] < qblk[:, None]
    gate = jnp.where(past, gate, NEG)
    _, idx = lax.top_k(gate, kk)
    valid = jnp.arange(kk)[None, :] < qblk[:, None]

    nq = S // Q_BLOCK
    qc = q.reshape(B, nq, Q_BLOCK, H, D).transpose(1, 0, 3, 2, 4)
    idxc = idx.reshape(B, H, nq, Q_BLOCK, kk).transpose(2, 0, 1, 3, 4)
    validc = valid.reshape(nq, Q_BLOCK, kk)
    bi = jnp.arange(B)[:, None, None, None]
    hi = jnp.arange(H)[None, :, None, None]
    n_sel = kk * MOBA_BLOCK

    def one(args):
        qx, ix, vx, i = args
        kg = kb[bi, hi, ix]
        vg = vb[bi, hi, ix]
        s_sel = jnp.einsum('bhqd,bhqrkd->bhqrk', qx, kg, preferred_element_type=jnp.float32) * scale
        s_sel = jnp.where(vx[None, None, :, :, None], s_sel, NEG).reshape(B, H, Q_BLOCK, n_sel)
        qpos = i * Q_BLOCK + jnp.arange(Q_BLOCK)
        own = (i * Q_BLOCK) // MOBA_BLOCK
        ko = lax.dynamic_index_in_dim(kb, own, axis=2, keepdims=False)
        vo = lax.dynamic_index_in_dim(vb, own, axis=2, keepdims=False)
        s_own = jnp.einsum('bhqd,bhkd->bhqk', qx, ko, preferred_element_type=jnp.float32) * scale
        kpos = own * MOBA_BLOCK + jnp.arange(MOBA_BLOCK)
        s_own = jnp.where(kpos[None, :] <= qpos[:, None], s_own, NEG)
        p = jax.nn.softmax(jnp.concatenate([s_sel, s_own], axis=-1), axis=-1).astype(v.dtype)
        p_sel = p[..., :n_sel].reshape(B, H, Q_BLOCK, kk, MOBA_BLOCK)
        p_own = p[..., n_sel:]
        return (jnp.einsum('bhqrk,bhqrkd->bhqd', p_sel, vg)
                + jnp.einsum('bhqk,bhkd->bhqd', p_own, vo))

    out = lax.map(one, (qc, idxc, validc, jnp.arange(nq)))
    return out.transpose(1, 0, 3, 2, 4).reshape(B, S, H, D)

def short_conv(z, w):
    C = z.shape[-1]
    return lax.conv_general_dilated(
        z, w[:, None, :].astype(z.dtype), window_strides=(1,), padding=[(CONV_WIDTH_2 - 1, 0)],
        dimension_numbers=('NWC', 'WIO', 'NWC'), feature_group_count=C)

def spatial_gate(u, v, ln_g, ln_b, w_s, b_s):
    B, S, C = v.shape
    nc = S // SG_CHUNK
    vn = layernorm(v, ln_g, ln_b).reshape(B, nc, SG_CHUNK, SG_GROUPS, SG_GDIM)
    mask = jnp.tril(jnp.ones((SG_CHUNK, SG_CHUNK), dtype=bool))
    ws = jnp.where(mask[None], w_s, jnp.zeros_like(w_s))
    mixed = jnp.einsum('gts,bcsgd->bctgd', ws, vn) + b_s.T[None, None, :, :, None]
    return u * mixed.reshape(B, S, C)

def hybrid_layer(x, positions, norm_g, w_in, mla_q_norm_g, mla_w_uq, mla_kv_norm_g, mla_w_ukv,
                 mla_q_g, mla_k_nope_g, mla_k_rope_g, conv_w, sg_ln_g, sg_ln_b, sg_w, sg_b,
                 moba_q_g, moba_k_g, w_out):
    B, S, _ = x.shape
    h = rmsnorm(x, norm_g)
    p = h @ w_in
    offs = np.cumsum(np.array(SPLIT_SIZES))[:-1].tolist()
    (cq, ckv, kr, g_a, c_h, c_b, c_c, g_b, sg_u, sg_v, g_c, mq, mk, mv, g_d) = jnp.split(p, offs, axis=-1)

    q = (rmsnorm(cq, mla_q_norm_g) @ mla_w_uq).reshape(B, S, MLA_HEADS, MLA_QK)
    kv = (rmsnorm(ckv, mla_kv_norm_g) @ mla_w_ukv).reshape(B, S, MLA_HEADS, MLA_NOPE + MLA_V)
    k_nope, v_a = kv[..., :MLA_NOPE], kv[..., MLA_NOPE:]
    q = rmsnorm(q, mla_q_g)
    q = jnp.concatenate([q[..., :MLA_NOPE], rope(q[..., MLA_NOPE:], positions)], axis=-1)
    k_nope = rmsnorm(k_nope, mla_k_nope_g)
    k_rope = rope(rmsnorm(kr, mla_k_rope_g)[:, :, None, :], positions)
    k = jnp.concatenate([k_nope, jnp.broadcast_to(k_rope, (B, S, MLA_HEADS, MLA_ROPE))], axis=-1)
    o_a = causal_attention_blocks(q, k, v_a, MLA_QK ** -0.5).reshape(B, S, GROUP_WIDTH)

    o_b = c_b * short_conv(c_c * c_h, conv_w)

    o_c = spatial_gate(sg_u, sg_v, sg_ln_g, sg_ln_b, sg_w, sg_b)

    qd = rmsnorm(mq.reshape(B, S, MOBA_HEADS, MOBA_HD), moba_q_g)
    kd = rmsnorm(mk.reshape(B, S, MOBA_HEADS, MOBA_HD), moba_k_g)
    vd = mv.reshape(B, S, MOBA_HEADS, MOBA_HD)
    qd = jnp.concatenate([rope(qd[..., :MOBA_ROT], positions), qd[..., MOBA_ROT:]], axis=-1)
    kd = jnp.concatenate([rope(kd[..., :MOBA_ROT], positions), kd[..., MOBA_ROT:]], axis=-1)
    o_d = moba_attention(qd, kd, vd, MOBA_HD ** -0.5).reshape(B, S, GROUP_WIDTH)

    y = jnp.concatenate([o_a * jax.nn.silu(g_a), o_b * jax.nn.silu(g_b),
                         o_c * jax.nn.silu(g_c), o_d * jax.nn.silu(g_d)], axis=-1)
    return y @ w_out

def second_inputs(seed: int = 0) -> dict:
    key = jax.random.key(seed)
    ks = jax.random.split(key, 24)
    L, D, GW = DEPTH, D_MODEL, GROUP_WIDTH
    f32 = jnp.float32

    def nrm(k, shape, scale):
        return jax.random.normal(k, shape, f32) * scale

    def gain(k, shape):
        return 1.0 + 0.05 * jax.random.normal(k, shape, f32)

    x = jax.random.normal(ks[0], (BATCH, SEQ, D), f32)
    offset = jax.random.randint(ks[1], (BATCH, 1), 0, 4096, dtype=jnp.int32)
    positions = (offset + jnp.arange(SEQ, dtype=jnp.int32)[None, :]).astype(jnp.int32)
    return {
        "x": x,
        "positions": positions,
        "norm_g": gain(ks[2], (L, D)),
        "w_in": nrm(ks[3], (L, D, D_IN), D ** -0.5),
        "mla_q_norm_g": gain(ks[4], (L, MLA_Q_RANK)),
        "mla_w_uq": nrm(ks[5], (L, MLA_Q_RANK, MLA_HEADS * MLA_QK), MLA_Q_RANK ** -0.5),
        "mla_kv_norm_g": gain(ks[6], (L, MLA_KV_RANK)),
        "mla_w_ukv": nrm(ks[7], (L, MLA_KV_RANK, MLA_HEADS * (MLA_NOPE + MLA_V)), MLA_KV_RANK ** -0.5),
        "mla_q_g": gain(ks[8], (L, MLA_QK)),
        "mla_k_nope_g": gain(ks[9], (L, MLA_NOPE)),
        "mla_k_rope_g": gain(ks[10], (L, MLA_ROPE)),
        "conv_w": nrm(ks[11], (L, CONV_WIDTH_2, GW), CONV_WIDTH_2 ** -0.5),
        "sg_ln_g": gain(ks[12], (L, GW)),
        "sg_ln_b": nrm(ks[13], (L, GW), 0.02),
        "sg_w": nrm(ks[14], (L, SG_GROUPS, SG_CHUNK, SG_CHUNK), SG_CHUNK ** -0.5),
        "sg_b": 1.0 + nrm(ks[15], (L, SG_GROUPS, SG_CHUNK), 0.1),
        "moba_q_g": gain(ks[16], (L, MOBA_HD)),
        "moba_k_g": gain(ks[17], (L, MOBA_HD)),
        "w_out": nrm(ks[18], (L, D_MIX, D), D_MIX ** -0.5),
    }

def second_block(x, positions, norm_g, w_in, mla_q_norm_g, mla_w_uq, mla_kv_norm_g, mla_w_ukv,
              mla_q_g, mla_k_nope_g, mla_k_rope_g, conv_w, sg_ln_g, sg_ln_b, sg_w, sg_b,
              moba_q_g, moba_k_g, w_out):
    for l in range(DEPTH):
        x = x + hybrid_layer(x, positions, norm_g[l], w_in[l], mla_q_norm_g[l], mla_w_uq[l],
                             mla_kv_norm_g[l], mla_w_ukv[l], mla_q_g[l], mla_k_nope_g[l],
                             mla_k_rope_g[l], conv_w[l], sg_ln_g[l], sg_ln_b[l], sg_w[l], sg_b[l],
                             moba_q_g[l], moba_k_g[l], w_out[l])
    return x


def setup_inputs(seed=0):
    out = dict(first_inputs(seed))
    for name, value in second_inputs(seed + 1).items():
        if name != "x":
            out[name + "_2"] = value
    return out


def reference(
    x, c, positions, w_mod, b_mod, norm_mix_g, norm_ffn_g, w_in, qn_g, kn_g, lam_q1, lam_k1,
    lam_q2, lam_k2, subln_g, w_proj_a, w_dw, b_dw, conv_ln_g, conv_ln_b, w_proj_b, b_proj_b,
    w_proj_c, w_out, w_router, b_router, w1, w3, w2, ws1, ws3, ws2, positions_2, norm_g_2,
    w_in_2, mla_q_norm_g_2, mla_w_uq_2, mla_kv_norm_g_2, mla_w_ukv_2, mla_q_g_2, mla_k_nope_g_2,
    mla_k_rope_g_2, conv_w_2, sg_ln_g_2, sg_ln_b_2, sg_w_2, sg_b_2, moba_q_g_2, moba_k_g_2,
    w_out_2,
):
    x = first_block(
        x, c, positions, w_mod, b_mod, norm_mix_g, norm_ffn_g, w_in, qn_g, kn_g, lam_q1, lam_k1,
        lam_q2, lam_k2, subln_g, w_proj_a, w_dw, b_dw, conv_ln_g, conv_ln_b, w_proj_b, b_proj_b,
        w_proj_c, w_out, w_router, b_router, w1, w3, w2, ws1, ws3, ws2,
    )
    return second_block(
        x, positions_2, norm_g_2, w_in_2, mla_q_norm_g_2, mla_w_uq_2, mla_kv_norm_g_2,
        mla_w_ukv_2, mla_q_g_2, mla_k_nope_g_2, mla_k_rope_g_2, conv_w_2, sg_ln_g_2, sg_ln_b_2,
        sg_w_2, sg_b_2, moba_q_g_2, moba_k_g_2, w_out_2,
    )


_drawn_inputs = setup_inputs


def setup_inputs(seed=0):
    import zlib

    import numpy as np

    out = dict(_drawn_inputs(seed))
    spreads = {}
    factors = {'norm_mix_g': 3.433,
     'qn_g': 4.321,
     'kn_g': 6.071,
     'lam_q1': 3.756,
     'lam_k1': 5.643,
     'subln_g': 3.95,
     'b_dw': 4.658,
     'conv_ln_g': 5.285,
     'conv_ln_b': 8.0,
     'b_proj_b': 4.709,
     'mla_q_norm_g_2': 8.0,
     'mla_kv_norm_g_2': 8.0,
     'mla_q_g_2': 8.0,
     'mla_k_nope_g_2': 8.0,
     'mla_k_rope_g_2': 8.0,
     'sg_ln_g_2': 3.977,
     'sg_ln_b_2': 8.0,
     'moba_q_g_2': 8.0,
     'moba_k_g_2': 8.0}
    for name, (base, spread) in spreads.items():
        noise = np.random.default_rng([zlib.crc32(name.encode()), seed]).standard_normal(out[name].shape)
        drawn = base * np.exp(spread * noise) if base else spread * noise
        out[name] = __import__('jax').numpy.asarray(drawn.astype(out[name].dtype))
    for name, factor in factors.items():
        out[name] = (out[name] * factor).astype(out[name].dtype)
    return out
```

```python
from contextlib import ExitStack
import math

import numpy as np
import concourse.bass as bass
from concourse import mybir

F32 = mybir.dt.float32
I32 = mybir.dt.int32
ALU = mybir.AluOpType
ACT = mybir.ActivationFunctionType
AX = mybir.AxisListType

P = 128
T = 2
SEQ = T * P
D = 1024
KT = D // P
DEPTH = 2
EPS = 1e-6
NEG = -1e30
CHUNK = 512
RING = 4
BANKS = 8

DA_HEADS, DA_HD = 4, 64
SB_HEADS, SB_HD = 8, 64
CONV_CH, TAPS = 512, 31
CT = CONV_CH // P
N_EXPERTS, N_GROUPS, TOPK_GROUPS, TOP_K, FF = 64, 8, 4, 8, 256
PER_GROUP = N_EXPERTS // N_GROUPS
ROUTED_SCALE = 2.5
SHARED = N_EXPERTS
UNROLL = 4
MOE_STEPS = 2 * (N_EXPERTS + 1)
MOD_CHUNKS = 6 * D // CHUNK

COLS_1 = {"qa": 0, "ka": 512, "va": 1024, "ug": 2048, "ua": 1536, "qc": 2560, "kc": 3072, "vc": 3584, "gt": 4096}
MOD_COL_PARTS = [0, 1, 3, 4]
MOD_ROW_PARTS = [2, 5]

MLA_H, MLA_NOPE, MLA_ROPE, MLA_QK = 4, 64, 32, 96
MOBA_H, MOBA_HD, MOBA_ROT = 4, 64, 16
SG_G, GW = 4, 256
D_IN_2 = 3488
NAT = {"cq": 0, "ckv": 256, "kr": 384, "ga": 416, "su": 672, "sv": 928, "gc": 1184, "mq": 1440, "mk": 1696,
       "mv": 1952, "gd": 2208}
NAT_COLS = 2464
CHUNKS_2 = [("t0", 672, 512, None), ("t1", 1184, 512, None), ("n0", 0, 512, 0), ("n1", 512, 160, 512),
            ("n2", 1696, 512, 672), ("n3", 2208, 512, 1184), ("n4", 2720, 512, 1696), ("n5", 3232, 256, 2208)]
ROPES = [(0, 32, 0), (32, 16, 1), (48, 8, 1)]
N_FREQ = 56


class Signal:

    def __init__(self, sem, per_layer=1, credit=0):
        self.sem, self.n, self.credit = sem, per_layer, credit

    def at(self, layer, k=1):
        return layer * self.n + (self.credit + k)


class Use:

    def __init__(self, tile, full, free, k_full, k_free):
        self.tile, self._full, self._free, self.k_full, self.k_free = tile, full, free, k_full, k_free
        self.full, self.free = full.sem, free.sem

    def free_at(self, layer):
        return self._free.at(layer, self.k_free)

    def consumed_at(self, layer):
        return self._free.at(layer, self.k_free + 1)

    def full_at(self, layer):
        return self._full.at(layer, self.k_full + 1)

    def full_before(self, layer):
        return self._full.at(layer, self.k_full + 1 - self._full.n)


class Chunk:

    def __init__(self, tile, filled, cum):
        self.tile, self._filled, self.cum, self.filled = tile, filled, cum, filled.sem

    def filled_at(self, layer):
        return self._filled.at(layer, self.cum)


def bank_plan(names, psum, sem, tag):
    fulls, frees = [0] * BANKS, [0] * BANKS
    places = []
    for i, name in enumerate(names):
        b = i % BANKS
        key = name if isinstance(name, str) else name[0]
        places.append((name, b, fulls[b], frees[b]))
        if not key.startswith("-"):
            frees[b] += 1
            if not key.startswith("="):
                fulls[b] += 1
    full = [Signal(sem(f"bank{b}_full_{tag}"), fulls[b], fulls[b]) for b in range(BANKS)]
    free = [Signal(sem(f"bank{b}_free_{tag}"), frees[b], 1) for b in range(BANKS)]
    uses = {name: Use(psum[b], full[b], free[b], kf, ke) for name, b, kf, ke in places}
    return uses, full, free


def broadcast(ap, axis, n):
    a = ap.unsqueeze(axis)
    shape = list(a.shape)
    shape[axis] = n
    return a.to_broadcast(shape)


def constants(nc, A, K):
    two_pi = 2 * math.pi
    c1 = 6.28125
    c2 = float(np.float32(round((two_pi - c1) * 2 ** 21) / 2 ** 21))
    c3 = two_pi - c1 - c2
    magic = 1.5 * 2 ** 23
    pi_in = 3.1415925
    with ExitStack() as ctx:
        def sb(name, shape, dt=F32):
            return ctx.enter_context(nc.sbuf_tensor(name, shape, dt))

        def sem(name):
            return ctx.enter_context(nc.semaphore(name))

        pos_i = sb("pos_i", [P, 2, T], I32)
        pos_f = sb("pos_f", [P, 2, T])
        inv = sb("inv", [P, N_FREQ])
        ang = sb("ang", [P, T, N_FREQ])
        turns = sb("turns", [P, T, N_FREQ])
        red = sb("red", [P, T, N_FREQ])
        wrap = sb("wrap", [P, T, N_FREQ])
        c_col = sb("c_col", [P, KT])
        c_sig = sb("c_sig", [P, KT])
        loaded, inv_ready, ang_ready, c_loaded, c_sig_ready, x_loaded = [
            sem(n) for n in ("loaded", "inv_ready", "ang_ready", "c_loaded", "c_sig_ready", "x_loaded")]
        block = ctx.enter_context(nc.Block())

        @block.sync
        def _(sp):
            for w, name in enumerate(("positions", "positions_2")):
                with nc.allow_non_contiguous_dma(reason="256 positions, one per partition"):
                    sp.dma_start(pos_i[:, w, :], A[name].rearrange("o (t p) -> p (o t)", p=P)).then_inc(loaded, 16)
            sp.dma_start(c_col[:], A["c"].rearrange("o (p k) -> p (o k)", k=KT)).then_inc(c_loaded, 16)
            for t in range(T):
                sp.dma_start(K.x[:, t, :], A["x"][0, t * P:(t + 1) * P, :]).then_inc(x_loaded, 16)
            sp.wait_ge(x_loaded, 16 * T)

        @block.gpsimd
        def _(pool):
            for (first, count, _), theta, dim in zip(ROPES, (10000.0, 500000.0, 500000.0), (64, 32, 16)):
                for i in range(count):
                    value = float(np.float32(theta) ** np.float32(-2.0 * i / dim))
                    last = nc.gpsimd.memset(inv[:, first + i:first + i + 1], value)
            last.then_inc(inv_ready, 1)
            nc.gpsimd.memset(K.eps[:], EPS)
            nc.gpsimd.memset(K.ones[:], 1.0)
            nc.gpsimd.memset(K.mean_conv[:], 1.0 / CONV_CH)
            for m in (K.ident, K.causal_neg, K.strict_neg):
                nc.gpsimd.memset(m[:], 0.0)
            for layer in range(DEPTH):
                li = 0.8 - 0.6 * math.exp(-0.3 * layer)
                nc.gpsimd.memset(K.lam_init[:, layer:layer + 1], li)
                nc.gpsimd.memset(K.lam_rest[:, layer:layer + 1], 1.0 - li)
            nc.gpsimd.memset(K.lower8[:], 1.0)
            pool.drain()
            square = [[-1, P]]
            nc.gpsimd.affine_select(out=K.ident[:], in_=K.ident[:], compare_op=ALU.not_equal, fill=1.0, base=0,
                                    pattern=square, channel_multiplier=1)
            nc.gpsimd.affine_select(out=K.causal_neg[:], in_=K.causal_neg[:], compare_op=ALU.is_ge, fill=NEG, base=0,
                                    pattern=square, channel_multiplier=1)
            nc.gpsimd.affine_select(out=K.strict_neg[:], in_=K.strict_neg[:], compare_op=ALU.is_gt, fill=NEG, base=0,
                                    pattern=[[1, P]], channel_multiplier=-1)
            nc.gpsimd.affine_select(out=K.strict_01[:], in_=K.ones[:], compare_op=ALU.is_gt, fill=0.0, base=0,
                                    pattern=[[1, P]], channel_multiplier=-1)
            nc.gpsimd.affine_select(out=K.tail[:], in_=K.ones[:], compare_op=ALU.is_ge, fill=0.0, base=0,
                                    pattern=square, channel_multiplier=1)
            nc.gpsimd.affine_select(out=K.head[:], in_=K.ones[:], compare_op=ALU.is_ge, fill=0.0, base=0,
                                    pattern=[[1, P]], channel_multiplier=-1)
            nc.gpsimd.affine_select(out=K.lower8[:], in_=K.lower8[:], compare_op=ALU.is_gt, fill=0.0, base=0,
                                    pattern=[[1, N_GROUPS], [-1, N_GROUPS]], channel_multiplier=0)
            pool.drain()

        @block.vector
        def _(dve):
            dve.wait_ge(loaded, 32)
            nc.vector.tensor_copy(pos_f[:], pos_i[:])
            dve.drain()
            dve.wait_ge(inv_ready, 1)
            for first, count, which in ROPES:
                for t in range(T):
                    nc.vector.tensor_scalar(ang[:, t, first:first + count], inv[:, first:first + count],
                                            pos_f[:, which, t:t + 1], None, ALU.mult)
            dve.drain()
            nc.vector.tensor_scalar(turns[:], ang[:], 1.0 / two_pi, magic, ALU.mult, ALU.add)
            dve.drain()
            nc.vector.tensor_scalar(turns[:], turns[:], magic, None, ALU.subtract)
            dve.drain()
            nc.vector.scalar_tensor_tensor(red[:], turns[:], -c1, ang[:], ALU.mult, ALU.add)
            dve.drain()
            nc.vector.scalar_tensor_tensor(ang[:], turns[:], -c2, red[:], ALU.mult, ALU.add)
            dve.drain()
            nc.vector.scalar_tensor_tensor(red[:], turns[:], -c3, ang[:], ALU.mult, ALU.add)
            dve.drain()
            nc.vector.tensor_scalar(ang[:], red[:], math.pi / 2, None, ALU.add)
            dve.drain()
            nc.vector.tensor_scalar(wrap[:], ang[:], math.pi, -two_pi, ALU.is_gt, ALU.mult)
            dve.drain()
            nc.vector.tensor_tensor(ang[:], ang[:], wrap[:], ALU.add)
            nc.vector.tensor_scalar(red[:], red[:], pi_in, -pi_in, ALU.min, ALU.max)
            dve.drain()
            nc.vector.tensor_scalar(ang[:], ang[:], pi_in, -pi_in, ALU.min, ALU.max)
            dve.drain().then_inc(ang_ready, 1)
            dve.wait_ge(c_sig_ready, 1)
            nc.vector.tensor_tensor(K.c_act[:], c_col[:], c_sig[:], ALU.mult)
            dve.drain()

        @block.scalar
        def _(act):
            act.wait_ge(c_loaded, 16)
            nc.scalar.activation(c_sig[:], c_col[:], ACT.Sigmoid).then_inc(c_sig_ready, 1)
            act.wait_ge(ang_ready, 1)
            nc.scalar.activation(K.sin[:], red[:], ACT.Sin)
            nc.scalar.activation(K.cos[:], ang[:], ACT.Sin)
            act.drain()


GROUPS_1 = (
    [("mod", c) for c in range(MOD_CHUNKS)] + ["vec"] + [("xT", 0, g) for g in range(4)]
    + [(n, i) for n in ("ug", "ua") for i in range(2)]
    + [(n, t) for n in ("qa", "ka") for t in range(T)]
    + [(n, i) for n in ("qc", "kc") for i in range(2)]
    + [(n, t) for n in ("va", "vc") for t in range(T)]
    + [("z0", par, i) for par in range(2) for i in range(2)] + [("z1", par) for par in range(2)]
    + [("suf", r, par) for r in range(3) for par in range(2)]
    + [("oc", i) for i in range(2)]
    + [("qkT", w, i) for w in range(2) for i in range(2)]
    + [("s1", m, i) for m in range(2) for i in range(2)] + [("s0", m) for m in range(2)]
    + ["cmean", "cvar"]
    + [("aT1", i) for i in range(2)] + ["aT0"] + [("oa", t) for t in range(T)] + [("oaT", i) for i in range(2)]
    + [(n, i, h, t) for i in range(3) for h in range(2) for t in range(T) for n in ("gt", "y")]
    + [("mT", g) for g in range(4)] + [("wo", h, t) for h in range(2) for t in range(T)]
    + [("xT", 1, g) for g in range(4)] + ["rt"]
    + [("=moe_y", t, h) for t in range(T) for h in range(2)] + [("-moe_h", t) for t in range(T)] + ["-moe_t"]
)
GROUPS_1 += ["-pad"] * (-len(GROUPS_1) % BANKS)

CHUNKS_1 = (
    [(("mod", c), ("mod", c)) for c in range(MOD_CHUNKS)]
    + [(n, (n, 1)) for n in ("ug", "ua", "qa", "ka", "qc", "kc", "va", "vc")]
    + [x for i in range(3) for x in (((("p", i)), ("y", i, 1, 1)), (("gt", i, 0), ("gt", i, 0, 1)),
                                     (("gt", i, 1), ("gt", i, 1, 1)))]
    + [(("wo", h), ("wo", h, 1)) for h in range(2)] + [("shared", None)]
)
assert len(CHUNKS_1) % RING == 0 and N_EXPERTS % UNROLL == 0 and UNROLL == RING


def first_block(nc, A, K):
    ds = bass.ds
    with ExitStack() as ctx:
        def sb(name, shape, dt=F32):
            return ctx.enter_context(nc.sbuf_tensor(name, shape, dt))

        def sem(name):
            return ctx.enter_context(nc.semaphore(name))

        def signal(name, per_layer=1, credit=0):
            return Signal(sem(name), per_layer, credit)

        norm_g = sb("norm_g", [P, 2, KT])
        mod_b = sb("mod_b", [P, 4, KT])
        gain_qk = sb("gain_qk", [P, 2, DA_HD])
        lam4 = sb("lam4", [P, 4, DA_HD])
        subln = sb("subln", [P, 2 * DA_HD])
        dw_rows = sb("dw_rows", [TAPS * CT, P])
        ch_rows = sb("ch_rows", [3 * CT, P])
        proj_b_bias = sb("proj_b_bias", [P, D])
        w_rt = sb("w_rt", [P, KT, N_EXPERTS])
        rt_bias = sb("rt_bias", [P, N_EXPERTS])
        gate = sb("gate", [P, 2, D])
        col4 = sb("col4", [P, 4, 2, KT])
        mod_col = sb("mod_col", [P, 4, KT])
        vec_t = sb("vec_t", [P, TAPS * CT + 3 * CT])
        std = sb("std", [P, T])
        sq_sum = sb("sq_sum", [P, T])
        hpad = sb("hpad", [P, CT, TAPS - 1 + SEQ])
        conv = sb("conv", [P, CT, SEQ])
        conv_t = sb("conv_t", [P, CT, SEQ])
        conv_std = sb("conv_std", [P, SEQ])
        qk = sb("qk", [P, T, 2 * 512])
        slots2 = sb("slots2", [P, 2, 2, D])
        work = slots2[:].rearrange("p s f n -> p (s f) n")
        va, vc = (work[:, i].rearrange("p (t n) -> p t n", t=T) for i in range(2))
        qc_t, kc_t = (work[:, i].rearrange("p (c n) -> p c n", c=CT) for i in (2, 3))
        qa_t = sb("qa_t", [P, DA_HEADS, SEQ])
        ka_t = sb("ka_t", [P, DA_HEADS, SEQ])
        z = sb("z", [P, SB_HEADS, SEQ + P])
        sp_ = sb("sp_", [P, SB_HEADS, SEQ + P])
        qk_std = sb("qk_std", [P, T * 16])
        row16 = sb("row16", [P, 3, 16])
        lam_p = sb("lam_p", [P, 2, DA_HD])
        lam_s = sb("lam_s", [P, 2])
        lam_e = sb("lam_e", [P, 2])
        lam = sb("lam", [P, 1])
        gain_o = sb("gain_o", [P, 2 * DA_HD])
        oa_std = sb("oa_std", [P, T * DA_HEADS])
        sig_g = sb("sig_g", [P, 2, CHUNK])
        y_tmp = sb("y_tmp", [P, CHUNK])
        pick = y_tmp[:].rearrange("p (q k) -> p q k", k=KT)
        score = sb("score", [P, T, N_EXPERTS])
        biased = sb("biased", [P, T, N_EXPERTS])
        top = sb("top", [P, T, N_GROUPS, 8])
        g_score = sb("g_score", [P, T, N_GROUPS])
        g_cmp = sb("g_cmp", [P, T, N_GROUPS, N_GROUPS])
        g_eq = sb("g_eq", [P, T, N_GROUPS, N_GROUPS])
        g_rank = sb("g_rank", [P, T, N_GROUPS])
        g_neg = sb("g_neg", [P, T, N_GROUPS])
        top8 = sb("top8", [P, T, 8])
        rest = sb("rest", [P, T, N_EXPERTS])
        w_sum = sb("w_sum", [P, T])
        route = sb("route", [P, T, N_EXPERTS + 1])
        sig_h = sb("sig_h", [P, T, FF])
        act_h = sb("act_h", [P, T, FF])
        act_t = sb("act_t", [P, T, 2, P])

        z_flat = z[:].rearrange("p h n -> p (h n)")
        e1 = z_flat[:, 0:8 * SEQ].rearrange("p (h n) -> p h n", h=8)
        e0 = z_flat[:, 8 * SEQ:8 * SEQ + 8 * P].rearrange("p (h n) -> p h n", h=8)
        a_t = sp_[:].rearrange("p h n -> p (h n)")[:, 0:DA_HEADS * 3 * P].rearrange("p (h b n) -> p h b n", h=DA_HEADS, b=3)
        oa = qa_t[:].rearrange("p h n -> p (h n)").rearrange("p (t n) -> p t n", t=T)
        oa_t = ka_t
        yc_t = kc_t
        yb_t = conv
        merged = qk
        m_t = K.h_t
        qk_rot = K.xn[:].rearrange("p t (h n) -> p t h n", n=DA_HD)
        qk_heads = qk[:].rearrange("p t (h n) -> p t h n", n=DA_HD)
        oa_heads = oa.rearrange("p t (h n) -> p (t h) n", n=2 * DA_HD)

        B, full, free = bank_plan(GROUPS_1, K.psum, sem, "1")
        filled = [Signal(sem(f"slot{s}_filled")) for s in range(RING)]
        filled2 = [Signal(sem(f"w2_slot{s}_filled")) for s in range(2)]
        C, loads, arrived = {}, [], [0] * RING
        for i, (name, reader) in enumerate(CHUNKS_1):
            s = i % RING
            arrived[s] += 32 if name in ("shared", "qa") else 16
            C[name] = Chunk(K.slots[s], filled[s], arrived[s])
            loads.append((name, s, CHUNKS_1[i - RING][1] if i >= RING else None, reader))
        turns = N_EXPERTS // UNROLL
        for s in range(RING):
            filled[s].n = arrived[s] + 32 * turns
        filled2[0].n = 16 * (N_EXPERTS // 2)
        filled2[1].n = 16 * (N_EXPERTS // 2 + 1)

        N_PARAMS = 2 + len(MOD_COL_PARTS) + len(MOD_ROW_PARTS) + 2 + 4 + 1 + 1 + 3 + 1 + 1 + 1
        params = signal("params_loaded", 16 * N_PARAMS)
        x_mid, x_out = signal("x_after_mixer"), signal("x_after_layer", 1, 1)
        std_ready = [signal(f"x_std_ready{i}") for i in range(2)]
        xn_ready = [signal(f"xn_ready{i}") for i in range(2)]
        ht_ready = [signal(f"ht_ready{i}") for i in range(2)]
        vec_ready = signal("vec_t_ready")
        ug_ready = signal("ug_sigmoid_ready", 2)
        qk_ready, qkc_ready, v_ready = signal("qk_ready"), signal("qkc_t_ready"), signal("v_ready")
        qk_sq_ready, qk_std_ready, qk_rot_ready = signal("qk_sq_ready"), signal("qk_std_ready"), signal("qk_rot_ready")
        log_ready, sp_ready, d_ready, ac_ready = (signal("softplus_log_ready"), signal("softplus_ready"),
                                                  signal("stick_log_ready"), signal("stick_ready"))
        yct_ready, qkt_ready = signal("yc_t_ready"), signal("qk_t_ready")
        lam_s_ready, lam_e_ready = signal("lam_sums_ready"), signal("lam_exp_ready")
        max_ready, exp_ready, a_ready, at_ready = (signal("row_max_ready"), signal("exp_ready"), signal("a_ready"),
                                                   signal("a_t_ready"))
        oa_sq_ready, oa_std_ready, oa_ready, oat_ready = (signal("oa_sq_ready"), signal("oa_std_ready"),
                                                          signal("oa_ready"), signal("oa_t_ready"))
        conv_ready, conv_sq_ready, conv_std_ready = signal("conv_ready"), signal("conv_sq_ready"), signal("conv_std_ready")
        conv_ln_ready, conv_sig_ready, ybt_ready = signal("conv_ln_ready"), signal("conv_sig_ready"), signal("yb_t_ready")
        sig_ready, y_used = signal("gate_sig_ready", 12), signal("gate_sig_used", 12)
        merged_ready, mt_ready = signal("merged_ready"), signal("merged_t_ready")
        score_ready, route_ready = signal("score_ready"), signal("route_ready")
        h_done = signal("expert_h_done", MOE_STEPS, MOE_STEPS)
        sig_h_ready = signal("expert_sigmoid_ready", MOE_STEPS)
        act_ready = signal("expert_act_ready", MOE_STEPS)
        tr_done = signal("expert_act_turned", MOE_STEPS)
        act_t_ready = signal("expert_act_t_ready", MOE_STEPS)
        w2_done = signal("expert_w2_done", MOE_STEPS, MOE_STEPS)
        done = signal("engines_done")

        y_bank = [[B["=moe_y", t, h].tile for h in range(2)] for t in range(T)]
        h_bank = [B["-moe_h", t].tile for t in range(T)]
        t_bank = B["-moe_t"].tile
        order = list(GROUPS_1)
        moe_before = [B[order[order.index(n) - BANKS]] for n in [("-moe_h", t) for t in range(T)] + ["-moe_t"]]

        block = ctx.enter_context(nc.Block())

        @block.sync
        def _(sp):
            for b in range(BANKS):
                sp.sem_inc(free[b].sem, 1)
                sp.sem_inc(full[b].sem, full[b].credit)
            sp.sem_inc(h_done.sem, MOE_STEPS)
            sp.sem_inc(w2_done.sem, MOE_STEPS)
            sp.sem_inc(x_out.sem, 1)

            def expert(l, e, s):
                for i, name in enumerate(("w1", "w3")):
                    sp.dma_start(K.slots[s][:, 4 * i:4 * i + 4, :].rearrange("p k n -> p (k n)"),
                                 A[name][ds(l, 1), ds(e, 1)].rearrange("a b (p k) n -> p (a b k n)", k=KT))\
                        .then_inc(filled[s].sem, 16)

            def expert2(l, e, s):
                sp.dma_start(slots2[:, s].rearrange("p f n -> p (f n)"),
                             A["w2"][ds(l, 1), ds(e, 1)].rearrange("a b (p f) n -> p (a b f n)", f=2))\
                    .then_inc(filled2[s].sem, 16)

            with sp.Fori(0, DEPTH) as l:
                for name, s, before, reader in loads:
                    if before is None:
                        sp.wait_ge(h_done.sem, h_done.at(l, MOE_STEPS - 2 * (RING - s) + 2) - MOE_STEPS)
                    else:
                        sp.wait_ge(B[before].full, B[before].full_at(l))
                    slot = K.slots[s]
                    key = name[0] if isinstance(name, tuple) else name
                    if key == "mod":
                        src = A["w_mod"][ds(l, 1), :, name[1] * CHUNK:(name[1] + 1) * CHUNK].rearrange(
                            "a (p k) n -> p (a k) n", k=KT)
                    elif key in ("gt", "ug", "ua", "qa", "ka", "qc", "kc", "va", "vc"):
                        col = COLS_1[key] + (name[1] * D + name[2] * CHUNK if key == "gt" else 0)
                        src = A["w_in"][ds(l, 1), :, col:col + CHUNK].rearrange("a (p k) n -> p (a k) n", k=KT)
                    elif key == "p":
                        slot = slot.rearrange("p k n -> p (k n)").rearrange("p (k n) -> p k n", n=D)
                        src = A[("w_proj_a", "w_proj_b", "w_proj_c")[name[1]]][ds(l, 1)].rearrange(
                            "a (k p) n -> p (a k) n", p=P)
                    elif key == "wo":
                        src = A["w_out"][ds(l, 1), :, name[1] * CHUNK:(name[1] + 1) * CHUNK].rearrange(
                            "a (k p) n -> p (a k) n", p=P)
                    if key == "shared":
                        for i, w in enumerate(("ws1", "ws3")):
                            sp.dma_start(slot[:, 4 * i:4 * i + 4, :].rearrange("p k n -> p (k n)"),
                                         A[w][ds(l, 1)].rearrange("a (p k) n -> p (a k n)", k=KT))\
                                .then_inc(filled[s].sem, 16)
                    elif key == "qa":
                        for half in (slice(P // 2, P), slice(0, P // 2)):
                            sp.dma_start(slot[half], src[half]).then_inc(filled[s].sem, 16)
                    else:
                        sp.dma_start(slot, src).then_inc(filled[s].sem, 16)
                sp.wait_ge(B["y", 2, 1, 1].full, B["y", 2, 1, 1].full_at(l))
                sp.wait_ge(w2_done.sem, w2_done.at(l, MOE_STEPS) - MOE_STEPS)
                sp.dma_start(slots2[:, 1].rearrange("p f n -> p (f n)"),
                             A["ws2"][ds(l, 1)].rearrange("a (p f) n -> p (a f n)", f=2)).then_inc(filled2[1].sem, 16)
                for e in range(UNROLL):
                    before = loads[len(loads) - RING + e][3]
                    if before is None:
                        sp.wait_ge(h_done.sem, h_done.at(l, 2))
                    else:
                        sp.wait_ge(B[before].full, B[before].full_at(l))
                    expert(l, e, e)
                    sp.wait_ge(w2_done.sem, w2_done.at(l, 2 * e) if e else w2_done.at(l, MOE_STEPS - 2) - MOE_STEPS)
                    expert2(l, e, e % 2)
                with sp.Fori(1, turns) as it:
                    for j in range(UNROLL):
                        sp.wait_ge(h_done.sem, h_done.at(l, 2 * (j - UNROLL + 2)) + it * (2 * UNROLL))
                        expert(l, it * UNROLL + j, j)
                        sp.wait_ge(w2_done.sem, w2_done.at(l, 2 * j) + it * (2 * UNROLL))
                        expert2(l, it * UNROLL + j, j % 2)

        @block.gpsimd
        def _(pool):
            with pool.Fori(0, DEPTH) as l:
                pool.wait_ge(x_out.sem, x_out.at(l, 0))
                one = ds(l, 1)

                def load(dst, src):
                    pool.dma_start(dst, src).then_inc(params.sem, 16)

                for i, name in enumerate(("norm_mix_g", "norm_ffn_g")):
                    load(norm_g[:, i, :], A[name][one].rearrange("a (p k) -> p (a k)", k=KT))
                for i, part in enumerate(MOD_COL_PARTS):
                    load(mod_b[:, i, :], A["b_mod"][one, part * D:(part + 1) * D].rearrange("a (p k) -> p (a k)", k=KT))
                for i, part in enumerate(MOD_ROW_PARTS):
                    load(gate[:, i, :], A["b_mod"][one, part * D:(part + 1) * D].to_broadcast([P, D]))
                for i, name in enumerate(("qn_g", "kn_g")):
                    load(gain_qk[:, i, :], A[name][one].to_broadcast([P, DA_HD]))
                for i, name in enumerate(("lam_q1", "lam_k1", "lam_q2", "lam_k2")):
                    load(lam4[:, i, :], A[name][one].to_broadcast([P, DA_HD]))
                load(subln[:], A["subln_g"][one].to_broadcast([P, 2 * DA_HD]))
                load(dw_rows[:], A["w_dw"][one].rearrange("a k (c p) -> (a k c) p", p=P))
                for i, name in enumerate(("b_dw", "conv_ln_g", "conv_ln_b")):
                    load(ch_rows[i * CT:(i + 1) * CT, :], A[name][one].rearrange("a (c p) -> (a c) p", p=P))
                load(proj_b_bias[:], A["b_proj_b"][one].to_broadcast([P, D]))
                load(w_rt[:], A["w_router"][one].rearrange("a (p k) n -> p (a k) n", k=KT))
                load(rt_bias[:], A["b_router"][one].to_broadcast([P, N_EXPERTS]))

        @block.tensor
        def _(pe):
            def begin(name, l):
                pe.wait_ge(B[name].free, B[name].free_at(l))
                return B[name].tile

            def chunk(name, l):
                pe.wait_ge(C[name].filled, C[name].filled_at(l))
                return C[name].tile

            def rows(name, l, w, t, stationary, cols=CHUNK):
                bank = begin(name, l)
                for k in range(KT):
                    mm = nc.tensor.matmul(bank[:, 0:cols], stationary[:, k, t * P:(t + 1) * P], w[:, k, 0:cols],
                                          start=(k == 0), stop=(k == KT - 1))
                mm.then_inc(B[name].full, 1)

            def columns(name, l, w, i):
                bank = begin(name, l)
                for j in range(2):
                    c = 2 * i + j
                    for k in range(KT):
                        mm = nc.tensor.matmul(bank[:, j * SEQ:(j + 1) * SEQ], w[:, k, c * P:(c + 1) * P], K.h_t[:, k, :],
                                              start=(k == 0), stop=(k == KT - 1))
                mm.then_inc(B[name].full, 1)

            def norm_turn(i, l):
                pe.wait_ge(xn_ready[i].sem, xn_ready[i].at(l))
                for g in range(4):
                    bank = begin(("xT", i, g), l)
                    for j in range(2):
                        for t in range(T):
                            mm = nc.tensor.transpose(bank[:, j * SEQ + t * P:j * SEQ + (t + 1) * P],
                                                     K.xn[:, t, 2 * g + j::KT], K.ident[:])
                    mm.then_inc(B["xT", i, g].full, 1)

            with pe.Fori(0, DEPTH) as l:
                for c in range(MOD_CHUNKS):
                    w = chunk(("mod", c), l)
                    bank = begin(("mod", c), l)
                    for k in range(KT):
                        mm = nc.tensor.matmul(bank[:], K.c_act[:, k:k + 1].to_broadcast([P, P]), w[:, k, :],
                                              start=(k == 0), stop=(k == KT - 1))
                    mm.then_inc(B["mod", c].full, 1)
                pe.wait_ge(params.sem, params.at(l, params.n))
                bank = begin("vec", l)
                nc.tensor.transpose(bank[:, 0:TAPS * CT], dw_rows[:], K.ident[0:TAPS * CT, 0:TAPS * CT])
                nc.tensor.transpose(bank[:, TAPS * CT:(TAPS + 3) * CT], ch_rows[:], K.ident[0:3 * CT, 0:3 * CT])\
                    .then_inc(B["vec"].full, 1)
                norm_turn(0, l)
                pe.wait_ge(ht_ready[0].sem, ht_ready[0].at(l))
                for name in ("ug", "ua"):
                    w = chunk(name, l)
                    for i in range(2):
                        columns((name, i), l, w, i)
                for name in ("qa", "ka"):
                    w = chunk(name, l)
                    for t in range(T):
                        rows((name, t), l, w, t, K.h_t)
                for name in ("qc", "kc"):
                    w = chunk(name, l)
                    for i in range(2):
                        columns((name, i), l, w, i)
                for name in ("va", "vc"):
                    w = chunk(name, l)
                    for t in range(T):
                        rows((name, t), l, w, t, K.h_t)

                pe.wait_ge(qkc_ready.sem, qkc_ready.at(l))
                for par in range(2):
                    part = slice(64 * par, 64 * par + 64)
                    for i in range(2):
                        bank = begin(("z0", par, i), l)
                        for j in range(2):
                            c = 2 * i + j
                            mm = nc.tensor.matmul(bank[:, j * SEQ:(j + 1) * SEQ], kc_t[part, c, 0:P], qc_t[part, c, :],
                                                  start=True, stop=True)
                        mm.then_inc(B["z0", par, i].full, 1)
                for par in range(2):
                    part = slice(64 * par, 64 * par + 64)
                    bank = begin(("z1", par), l)
                    for c in range(CT):
                        mm = nc.tensor.matmul(bank[:, c * P:(c + 1) * P], kc_t[part, c, P:SEQ], qc_t[part, c, P:SEQ],
                                              start=True, stop=True)
                    mm.then_inc(B["z1", par].full, 1)
                pe.wait_ge(sp_ready.sem, sp_ready.at(l))
                for r, parts in enumerate(([(K.tail, 0)], [(K.tail, P), (K.ones, 2 * P)], [(K.tail, 2 * P)])):
                    for par in range(2):
                        bank = begin(("suf", r, par), l)
                        for n, (m, c) in enumerate(parts):
                            mm = nc.tensor.matmul(bank[:], m[:], sp_[:, 4 * par:4 * par + 4, c:c + P],
                                                  start=(n == 0), stop=(n == len(parts) - 1))
                        mm.then_inc(B["suf", r, par].full, 1)
                pe.wait_ge(v_ready.sem, v_ready.at(l))
                pe.wait_ge(ac_ready.sem, ac_ready.at(l))
                for i in range(2):
                    bank = begin(("oc", i), l)
                    for j in range(2):
                        for par in range(2):
                            c = 2 * i + j
                            col = (2 * c + par) * SB_HD
                            out = bank[64 * par:64 * par + 64, j * SEQ:(j + 1) * SEQ]
                            nc.tensor.matmul(out, vc[:, 0, col:col + SB_HD], z[:, 4 * par + c, 0:SEQ],
                                             start=True, stop=False, skip_group_check=True)
                            mm = nc.tensor.matmul(out[:, P:SEQ], vc[:, 1, col:col + SB_HD], z[:, 4 * par + c, SEQ:SEQ + P],
                                                  start=False, stop=True, skip_group_check=True)
                    mm.then_inc(B["oc", i].full, 1)

                pe.wait_ge(qk_rot_ready.sem, qk_rot_ready.at(l))
                for w in range(2):
                    for i in range(2):
                        bank = begin(("qkT", w, i), l)
                        for j in range(2):
                            for t in range(T):
                                col = w * 512 + (2 * i + j) * P
                                mm = nc.tensor.transpose(bank[:, j * SEQ + t * P:j * SEQ + (t + 1) * P],
                                                         K.xn[:, t, col:col + P], K.ident[:])
                        mm.then_inc(B["qkT", w, i].full, 1)
                pe.wait_ge(qkt_ready.sem, qkt_ready.at(l))
                for m in range(2):
                    part = slice(64 * m, 64 * m + 64)
                    for i in range(2):
                        bank = begin(("s1", m, i), l)
                        for j in range(2):
                            mm = nc.tensor.matmul(bank[:, j * SEQ:(j + 1) * SEQ], qa_t[part, 2 * i + j, P:SEQ],
                                                  ka_t[part, 2 * i + j, :], start=True, stop=True)
                        mm.then_inc(B["s1", m, i].full, 1)
                for m in range(2):
                    part = slice(64 * m, 64 * m + 64)
                    bank = begin(("s0", m), l)
                    for h in range(DA_HEADS):
                        mm = nc.tensor.matmul(bank[:, h * P:(h + 1) * P], qa_t[part, h, 0:P], ka_t[part, h, 0:P],
                                              start=True, stop=True)
                    mm.then_inc(B["s0", m].full, 1)
                pe.wait_ge(conv_ready.sem, conv_ready.at(l))
                bank = begin("cmean", l)
                for c in range(CT):
                    mm = nc.tensor.matmul(bank[:, 0:SEQ], K.mean_conv[:], conv[:, c, :], start=(c == 0), stop=(c == CT - 1))
                mm.then_inc(B["cmean"].full, 1)
                pe.wait_ge(conv_sq_ready.sem, conv_sq_ready.at(l))
                bank = begin("cvar", l)
                for c in range(CT):
                    mm = nc.tensor.matmul(bank[:, 0:SEQ], K.mean_conv[:], conv_t[:, c, :], start=(c == 0), stop=(c == CT - 1))
                mm.then_inc(B["cvar"].full, 1)
                pe.wait_ge(a_ready.sem, a_ready.at(l))
                for i in range(2):
                    bank = begin(("aT1", i), l)
                    for j in range(2):
                        for b in range(2):
                            mm = nc.tensor.transpose(bank[:, (2 * j + b) * P:(2 * j + b + 1) * P],
                                                     e1[:, 2 * i + j, b * P:(b + 1) * P], K.ident[:])
                    mm.then_inc(B["aT1", i].full, 1)
                bank = begin("aT0", l)
                for h in range(DA_HEADS):
                    mm = nc.tensor.transpose(bank[:, h * P:(h + 1) * P], e0[:, h, :], K.ident[:])
                mm.then_inc(B["aT0"].full, 1)
                pe.wait_ge(at_ready.sem, at_ready.at(l))
                for t in range(T):
                    bank = begin(("oa", t), l)
                    for h in range(DA_HEADS):
                        col = slice(h * P, (h + 1) * P)
                        if t == 0:
                            mm = nc.tensor.matmul(bank[:, col], a_t[:, h, 0, :], va[:, 0, col], start=True, stop=True)
                        else:
                            nc.tensor.matmul(bank[:, col], a_t[:, h, 1, :], va[:, 0, col], start=True, stop=False)
                            mm = nc.tensor.matmul(bank[:, col], a_t[:, h, 2, :], va[:, 1, col], start=False, stop=True)
                    mm.then_inc(B["oa", t].full, 1)
                pe.wait_ge(oa_ready.sem, oa_ready.at(l))
                for i in range(2):
                    bank = begin(("oaT", i), l)
                    for j in range(2):
                        for t in range(T):
                            mm = nc.tensor.transpose(bank[:, j * SEQ + t * P:j * SEQ + (t + 1) * P],
                                                     oa[:, t, (2 * i + j) * P:(2 * i + j + 1) * P], K.ident[:])
                    mm.then_inc(B["oaT", i].full, 1)

                for i, (feat, ready) in enumerate(((oa_t, oat_ready), (yb_t, ybt_ready), (yc_t, yct_ready))):
                    pe.wait_ge(ready.sem, ready.at(l))
                    w = chunk(("p", i), l).rearrange("p k n -> p (k n)").rearrange("p (k n) -> p k n", n=D)
                    for h in range(2):
                        wg = chunk(("gt", i, h), l)
                        for t in range(T):
                            rows(("gt", i, h, t), l, wg, t, K.h_t)
                            bank = begin(("y", i, h, t), l)
                            for k in range(4):
                                mm = nc.tensor.matmul(bank[:], feat[:, k, t * P:(t + 1) * P],
                                                      w[:, k, h * CHUNK:(h + 1) * CHUNK], start=(k == 0), stop=(k == 3))
                            mm.then_inc(B["y", i, h, t].full, 1)
                pe.wait_ge(merged_ready.sem, merged_ready.at(l))
                for g in range(4):
                    bank = begin(("mT", g), l)
                    for j in range(2):
                        for t in range(T):
                            k = 2 * g + j
                            mm = nc.tensor.transpose(bank[:, j * SEQ + t * P:j * SEQ + (t + 1) * P],
                                                     merged[:, t, k * P:(k + 1) * P], K.ident[:])
                    mm.then_inc(B["mT", g].full, 1)
                pe.wait_ge(mt_ready.sem, mt_ready.at(l))
                for h in range(2):
                    w = chunk(("wo", h), l)
                    for t in range(T):
                        rows(("wo", h, t), l, w, t, m_t)

                norm_turn(1, l)
                pe.wait_ge(ht_ready[1].sem, ht_ready[1].at(l))
                bank = begin("rt", l)
                for t in range(T):
                    for k in range(KT):
                        mm = nc.tensor.matmul(bank[:, t * N_EXPERTS:(t + 1) * N_EXPERTS], K.h_t[:, k, t * P:(t + 1) * P],
                                              w_rt[:, k, :], start=(k == 0), stop=(k == KT - 1))
                mm.then_inc(B["rt"].full, 1)

                def expert_h(t, w, k0, k1):
                    for k in range(k0, k1):
                        mm = nc.tensor.matmul(h_bank[t][:], K.h_t[:, k, t * P:(t + 1) * P], w[:, :, k, :],
                                              start=(k == 0), stop=(k == KT - 1), skip_group_check=True)
                    if k1 == KT:
                        mm.then_inc(h_done.sem, 1)

                def expert_turn(t, n):
                    pe.wait_ge(act_ready.sem, act_ready.at(l, 1) + n)
                    for f in range(2):
                        mm = nc.tensor.transpose(t_bank[:, (2 * t + f) * P:(2 * t + f + 1) * P], act_h[:, t, f::2],
                                                 K.ident[:])
                    mm.then_inc(tr_done.sem, 1)

                def expert_w2(t, w, n, start):
                    pe.wait_ge(act_t_ready.sem, act_t_ready.at(l, 1) + n)
                    for f in range(2):
                        for h in range(2):
                            mm = nc.tensor.matmul(y_bank[t][h][:], act_t[:, t, f, :], w[:, f, h * CHUNK:(h + 1) * CHUNK],
                                                  start=(start and f == 0), stop=(f == 1), skip_group_check=True)
                    mm.then_inc(w2_done.sem, 1)

                def w13(s):
                    return K.slots[s].rearrange("p (i k) n -> p i (k n)", i=2).rearrange("p i (k n) -> p i k n", n=FF)

                for b in list(B["=moe_y", t, h] for t in range(T) for h in range(2)):
                    pe.wait_ge(b.free, b.free_at(l))
                for b in moe_before:
                    pe.wait_ge(b.free, b.consumed_at(l))
                pe.wait_ge(C["shared"].filled, C["shared"].filled_at(l))
                s = len(CHUNKS_1) % RING - 1
                expert_h(0, w13(s), 0, KT)
                expert_h(1, w13(s), 0, KT // 2)
                expert_turn(0, 0)
                expert_h(1, w13(s), KT // 2, KT)
                pe.wait_ge(filled2[1].sem, filled2[1].at(l, 16))
                expert_w2(0, slots2[:, 1], 0, True)
                for h in range(2):
                    nc.tensor.matmul(y_bank[1][h][:], K.strict_01[:, 0:1].to_broadcast([P, P]), K.h_t[:, 0:2, :],
                                     start=True, stop=True, skip_group_check=True)
                with pe.Fori(0, turns) as it:
                    for j in range(UNROLL):
                        n = it * (2 * UNROLL) + 2 * (j + 1)
                        w, w2, w2_before = w13(j), slots2[:, j % 2], slots2[:, (j + 1) % 2]
                        pe.wait_ge(filled[j].sem, filled[j].at(l, arrived[j] + 32) + it * 32)
                        expert_h(0, w, 0, KT // 2)
                        expert_turn(1, n - 1)
                        expert_h(0, w, KT // 2, KT)
                        expert_w2(1, w2_before, n - 1, False)
                        expert_h(1, w, 0, KT // 2)
                        expert_turn(0, n)
                        expert_h(1, w, KT // 2, KT)
                        pe.wait_ge(filled2[j % 2].sem,
                                   filled2[j % 2].at(l, 16 * (j // 2 + 1 + j % 2)) + it * (16 * (UNROLL // 2)))
                        expert_w2(0, w2, n, False)
                expert_turn(1, MOE_STEPS - 1)
                expert_w2(1, slots2[:, 1], MOE_STEPS - 1, False)

        @block.scalar
        def _(act):
            def full_of(name, l):
                act.wait_ge(B[name].full, B[name].full_at(l))
                return B[name].tile

            def row_norm(i, l):
                if i == 0:
                    act.wait_ge(x_out.sem, x_out.at(l, 0))
                else:
                    act.wait_ge(x_mid.sem, x_mid.at(l))
                for t in range(T):
                    nc.scalar.activation(K.xn[:, t, :], K.x[:, t, :], ACT.Square, accum_out=sq_sum[:, t:t + 1])
                act.drain()
                nc.scalar.activation(std[:], sq_sum[:], ACT.Sqrt, scale=1.0 / D, bias=K.eps[:]).then_inc(std_ready[i].sem, 1)

            def copy_out(name, l, dst, src, last=None, scale=1.0):
                nc.scalar.activation(dst, src, ACT.Copy, scale=scale).then_inc(B[name].free, 1)

            with act.Fori(0, DEPTH) as l:
                row_norm(0, l)
                bank = full_of("vec", l)
                copy_out("vec", l, vec_t[:], bank[:, 0:(TAPS + 3) * CT])
                act.drain().then_inc(vec_ready.sem, 1)
                for i in range(2):
                    bank = full_of(("ug", i), l)
                    nc.scalar.activation(conv_t[:, 2 * i:2 * i + 2, :], bank[:].rearrange("p (c n) -> p c n", c=2),
                                         ACT.Sigmoid).then_inc(B["ug", i].free, 1)
                act.drain().then_inc(ug_ready.sem, 2)
                for w, name in enumerate(("qa", "ka")):
                    for t in range(T):
                        bank = full_of((name, t), l)
                        copy_out((name, t), l, qk[:, t, w * 512:(w + 1) * 512], bank[:])
                act.drain().then_inc(qk_ready.sem, 1)
                for name, dst, scale in (("qc", qc_t, SB_HD ** -0.5), ("kc", kc_t, 1.0)):
                    for i in range(2):
                        bank = full_of((name, i), l)
                        copy_out((name, i), l, dst[:, 2 * i:2 * i + 2, :], bank[:].rearrange("p (c n) -> p c n", c=2),
                                 scale=scale)
                act.drain().then_inc(qkc_ready.sem, 1)
                for name, dst in (("va", va), ("vc", vc)):
                    for t in range(T):
                        bank = full_of((name, t), l)
                        copy_out((name, t), l, dst[:, t, :], bank[:])
                act.drain().then_inc(v_ready.sem, 1)
                act.wait_ge(qk_sq_ready.sem, qk_sq_ready.at(l))
                nc.scalar.activation(qk_std[:], qk_std[:], ACT.Sqrt, scale=1.0 / DA_HD, bias=K.eps[:])\
                    .then_inc(qk_std_ready.sem, 1)
                act.wait_ge(qk_rot_ready.sem, qk_rot_ready.at(l))
                for name, h0, nh, c0, n in ([(("z0", par, i), 4 * par + 2 * i, 2, 0, SEQ) for par in range(2) for i in range(2)]
                                            + [(("z1", par), 4 * par, 4, SEQ, P) for par in range(2)]):
                    src = full_of(name, l)[:].rearrange("p (h n) -> p h n", h=nh)
                    nc.scalar.activation(sp_[:, h0:h0 + nh, c0:c0 + n], src, ACT.Abs)
                    copy_out(name, l, z[:, h0:h0 + nh, c0:c0 + n], src)
                act.drain()
                nc.scalar.activation(sp_[:], sp_[:], ACT.Exp, scale=-1.0)
                act.drain()
                nc.scalar.activation(sp_[:], sp_[:], ACT.Ln, bias=1.0).then_inc(log_ready.sem, 1)
                act.wait_ge(d_ready.sem, d_ready.at(l))
                nc.scalar.activation(z[:], z[:], ACT.Exp).then_inc(ac_ready.sem, 1)
                for i in range(2):
                    bank = full_of(("oc", i), l)
                    copy_out(("oc", i), l, yc_t[:, 2 * i:2 * i + 2, :], bank[:].rearrange("p (c n) -> p c n", c=2))
                act.drain().then_inc(yct_ready.sem, 1)
                for w, dst in enumerate((qa_t, ka_t)):
                    for i in range(2):
                        bank = full_of(("qkT", w, i), l)
                        copy_out(("qkT", w, i), l, dst[:, 2 * i:2 * i + 2, :], bank[:].rearrange("p (c n) -> p c n", c=2))
                act.drain().then_inc(qkt_ready.sem, 1)
                act.wait_ge(lam_s_ready.sem, lam_s_ready.at(l))
                nc.scalar.activation(lam_e[:], lam_s[:], ACT.Exp).then_inc(lam_e_ready.sem, 1)
                act.wait_ge(max_ready.sem, max_ready.at(l))
                for r in range(16):
                    e = e1[:, r, :] if r < 8 else e0[:, r - 8, :]
                    nc.scalar.activation(e, e, ACT.Exp, bias=row16[:, 0, r:r + 1], scale=DA_HD ** -0.5,
                                         accum_out=row16[:, 1, r:r + 1])
                act.drain().then_inc(exp_ready.sem, 1)
                src = full_of("cvar", l)
                nc.scalar.activation(conv_std[:], src[:, 0:SEQ], ACT.Sqrt, bias=K.eps[:]).then_inc(B["cvar"].free, 1)
                act.drain().then_inc(conv_std_ready.sem, 1)
                for i in range(2):
                    bank = full_of(("aT1", i), l)
                    copy_out(("aT1", i), l, a_t[:, 2 * i:2 * i + 2, 1:3, :],
                             bank[:].rearrange("p (h b n) -> p h b n", h=2, b=2))
                bank = full_of("aT0", l)
                copy_out("aT0", l, a_t[:, :, 0, :], bank[:].rearrange("p (h n) -> p h n", h=DA_HEADS))
                act.drain().then_inc(at_ready.sem, 1)
                act.wait_ge(oa_sq_ready.sem, oa_sq_ready.at(l))
                nc.scalar.activation(oa_std[:], oa_std[:], ACT.Sqrt, scale=1.0 / (2 * DA_HD), bias=K.eps[:])\
                    .then_inc(oa_std_ready.sem, 1)
                act.wait_ge(conv_ln_ready.sem, conv_ln_ready.at(l))
                nc.scalar.activation(conv_t[:], conv[:], ACT.Sigmoid).then_inc(conv_sig_ready.sem, 1)
                for i in range(2):
                    bank = full_of(("oaT", i), l)
                    copy_out(("oaT", i), l, oa_t[:, 2 * i:2 * i + 2, :], bank[:].rearrange("p (c n) -> p c n", c=2))
                act.drain().then_inc(oat_ready.sem, 1)
                n = 0
                for i in range(3):
                    for h in range(2):
                        for t in range(T):
                            bank = full_of(("gt", i, h, t), l)
                            if n >= 2:
                                act.wait_ge(y_used.sem, y_used.at(l, n - 1))
                            nc.scalar.activation(sig_g[:, n % 2, :], bank[:], ACT.Sigmoid).then_inc(B["gt", i, h, t].free, 1)
                            act.drain().then_inc(sig_ready.sem, 1)
                            n += 1
                for g in range(4):
                    bank = full_of(("mT", g), l)
                    copy_out(("mT", g), l, m_t[:, 2 * g:2 * g + 2, :], bank[:].rearrange("p (c n) -> p c n", c=2))
                act.drain().then_inc(mt_ready.sem, 1)
                row_norm(1, l)
                bank = full_of("rt", l)
                nc.scalar.activation(score[:], bank[:, 0:T * N_EXPERTS].rearrange("p (t n) -> p t n", t=T), ACT.Sigmoid)\
                    .then_inc(B["rt"].free, 1)
                act.drain().then_inc(score_ready.sem, 1)

                def sigmoid_h(t, n):
                    act.wait_ge(h_done.sem, h_done.at(l, 1) + n)
                    nc.scalar.activation(sig_h[:, t, :], h_bank[t][:, 0:FF], ACT.Sigmoid).then_inc(sig_h_ready.sem, 1)

                def copy_turned(t, n):
                    act.wait_ge(tr_done.sem, tr_done.at(l, 1) + n)
                    nc.scalar.activation(act_t[:, t], t_bank[:, 2 * t * P:2 * (t + 1) * P].rearrange("p (f n) -> p f n", f=2),
                                         ACT.Copy).then_inc(act_t_ready.sem, 1)

                sigmoid_h(0, 0)
                copy_turned(0, 0)
                sigmoid_h(1, 1)
                with act.Fori(0, turns) as it:
                    for j in range(UNROLL):
                        n = it * (2 * UNROLL) + 2 * (j + 1)
                        copy_turned(1, n - 1)
                        sigmoid_h(0, n)
                        copy_turned(0, n)
                        sigmoid_h(1, n + 1)
                copy_turned(1, MOE_STEPS - 1)

        @block.vector
        def _(dve):
            v = nc.vector

            def full_of(name, l):
                dve.wait_ge(B[name].full, B[name].full_at(l))
                return B[name].tile

            def norm_x(i, l):
                dve.wait_ge(std_ready[i].sem, std_ready[i].at(l))
                v.reciprocal(std[:], std[:])
                dve.drain()
                for t in range(T):
                    v.tensor_scalar(K.xn[:, t, :], K.x[:, t, :], std[:, t:t + 1], None, ALU.mult)
                dve.drain().then_inc(xn_ready[i].sem, 1)

            def modulate(i, l):
                for g in range(4):
                    bank = full_of(("xT", i, g), l)
                    for j in range(2):
                        k = 2 * g + j
                        ins = v.tensor_scalar(K.h_t[:, k, :], bank[:, j * SEQ:(j + 1) * SEQ],
                                              mod_col[:, 2 * i + 1, k:k + 1], mod_col[:, 2 * i, k:k + 1], ALU.mult, ALU.add)
                    ins.then_inc(B["xT", i, g].free, 1)
                dve.drain().then_inc(ht_ready[i].sem, 1)

            v.memset(hpad[:, :, 0:TAPS - 1], 0.0)
            v.memset(route[:, :, SHARED:SHARED + 1], 1.0)
            with dve.Fori(0, DEPTH) as l:
                one = ds(l, 1)
                norm_x(0, l)
                dve.wait_ge(params.sem, params.at(l, params.n))
                v.tensor_tensor(lam_p[:], lam4[:, 0::2, :], lam4[:, 1::2, :], ALU.mult)
                dve.drain()
                v.tensor_reduce(lam_s[:], lam_p[:], AX.X, ALU.add).then_inc(lam_s_ready.sem, 1)
                v.tensor_scalar(gain_o[:], subln[:], K.lam_rest[:, one], None, ALU.mult)
                for c in range(MOD_CHUNKS):
                    part, half = divmod(c, 2)
                    bank = full_of(("mod", c), l)
                    if part in MOD_ROW_PARTS:
                        g = gate[:, MOD_ROW_PARTS.index(part), half * CHUNK:(half + 1) * CHUNK]
                        v.tensor_tensor(g, bank[:], g, ALU.add).then_inc(B["mod", c].free, 1)
                    else:
                        v.tensor_tensor(pick, bank[:].rearrange("p (q k) -> p q k", k=KT),
                                        broadcast(K.ident[:, 64 * half:64 * half + 64], 2, KT), ALU.mult)\
                            .then_inc(B["mod", c].free, 1)
                        dve.drain()
                        v.tensor_reduce(col4[:, MOD_COL_PARTS.index(part), half, :], pick.rearrange("p q k -> p k q"),
                                        AX.X, ALU.add)
                        dve.drain()
                v.tensor_tensor(mod_col[:], col4[:, :, 0, :], col4[:, :, 1, :], ALU.add)
                dve.drain()
                v.tensor_tensor(mod_col[:], mod_col[:], mod_b[:], ALU.add)
                dve.drain()
                for i in range(2):
                    v.scalar_tensor_tensor(mod_col[:, 2 * i + 1, :], mod_col[:, 2 * i + 1, :], 1.0, norm_g[:, i, :],
                                           ALU.add, ALU.mult)
                dve.drain()
                modulate(0, l)
                dve.wait_ge(ug_ready.sem, ug_ready.at(l, 2))
                for i in range(2):
                    bank = full_of(("ua", i), l)
                    v.tensor_tensor(hpad[:, 2 * i:2 * i + 2, TAPS - 1:], bank[:].rearrange("p (c n) -> p c n", c=2),
                                    conv_t[:, 2 * i:2 * i + 2, :], ALU.mult).then_inc(B["ua", i].free, 1)
                dve.drain()
                dve.wait_ge(vec_ready.sem, vec_ready.at(l))
                ch = TAPS * CT
                for k in range(TAPS):
                    for c in range(CT):
                        w = vec_t[:, k * CT + c:k * CT + c + 1]
                        if k == 0:
                            v.tensor_scalar(conv[:, c, :], hpad[:, c, 0:SEQ], w, vec_t[:, ch + c:ch + c + 1], ALU.mult, ALU.add)
                        else:
                            v.scalar_tensor_tensor(conv[:, c, :], hpad[:, c, k:k + SEQ], w, conv[:, c, :], ALU.mult, ALU.add)
                    dve.drain()
                dve.drain().then_inc(conv_ready.sem, 1)
                dve.wait_ge(qk_ready.sem, qk_ready.at(l))
                sq = z_flat[:, 0:T * 1024]
                qk_all = qk[:].rearrange("p t n -> p (t n)")
                v.tensor_tensor(sq, qk_all, qk_all, ALU.mult)
                dve.drain()
                v.tensor_reduce(qk_std[:], sq.rearrange("p (h n) -> p h n", n=DA_HD), AX.X, ALU.add)\
                    .then_inc(qk_sq_ready.sem, 1)
                dve.wait_ge(qk_std_ready.sem, qk_std_ready.at(l))
                v.reciprocal(qk_std[:], qk_std[:])
                dve.drain()
                heads = qk_all.rearrange("p (h n) -> p h n", n=DA_HD)
                v.tensor_tensor(heads, heads, broadcast(qk_std[:], 2, DA_HD), ALU.mult)
                dve.drain()
                for w in range(2):
                    part = qk_heads[:, :, 8 * w:8 * w + 8, :]
                    v.tensor_tensor(part, part, broadcast(broadcast(gain_qk[:, w, :], 1, 8), 1, T), ALU.mult)
                dve.drain()
                half = DA_HD // 2
                cos, sin = (broadcast(tab[:, :, 0:half], 2, 16) for tab in (K.cos, K.sin))
                s1 = z_flat[:, 0:1024].rearrange("p (t h n) -> p t h n", t=T, h=16)
                s2 = z_flat[:, 1024:2048].rearrange("p (t h n) -> p t h n", t=T, h=16)
                x1, x2 = qk_heads[:, :, :, 0:half], qk_heads[:, :, :, half:]
                v.tensor_tensor(s1, x1, cos, ALU.mult)
                v.tensor_tensor(s2, x2, sin, ALU.mult)
                dve.drain()
                v.tensor_tensor(qk_rot[:, :, :, 0:half], s1, s2, ALU.subtract)
                dve.drain()
                v.tensor_tensor(s1, x2, cos, ALU.mult)
                v.tensor_tensor(s2, x1, sin, ALU.mult)
                dve.drain()
                v.tensor_tensor(qk_rot[:, :, :, half:], s1, s2, ALU.add)
                dve.drain().then_inc(qk_rot_ready.sem, 1)
                dve.wait_ge(log_ready.sem, log_ready.at(l))
                v.scalar_tensor_tensor(sp_[:].rearrange("p h n -> p (h n)"), z_flat, 0.0,
                                       sp_[:].rearrange("p h n -> p (h n)"), ALU.max, ALU.add)
                dve.drain()
                diagonal = (0, 2 * P)
                for c in diagonal:
                    v.tensor_tensor(sp_[:, :, c:c + P], sp_[:, :, c:c + P], broadcast(K.strict_01[:], 1, SB_HEADS), ALU.mult)
                dve.drain().then_inc(sp_ready.sem, 1)
                for r in range(3):
                    for par in range(2):
                        bank = full_of(("suf", r, par), l)
                        zz = z[:, 4 * par:4 * par + 4, r * P:(r + 1) * P]
                        v.tensor_tensor(zz, zz, bank[:].rearrange("p (h n) -> p h n", h=4), ALU.subtract)\
                            .then_inc(B["suf", r, par].free, 1)
                dve.drain()
                for c in diagonal:
                    v.scalar_tensor_tensor(z[:, :, c:c + P], z[:, :, c:c + P], 0.0, broadcast(K.strict_neg[:], 1, SB_HEADS),
                                           ALU.min, ALU.add)
                v.tensor_scalar(z[:, :, P:2 * P], z[:, :, P:2 * P], 0.0, None, ALU.min)
                dve.drain().then_inc(d_ready.sem, 1)
                dve.wait_ge(yct_ready.sem, yct_ready.at(l))
                for m in range(2):
                    for i in range(2):
                        src = full_of(("s1", m, i), l)[:].rearrange("p (h n) -> p h n", h=2)
                        dst = e1[:, 4 * m + 2 * i:4 * m + 2 * i + 2, :]
                        v.tensor_copy(dst[:, :, 0:P], src[:, :, 0:P])
                        v.tensor_tensor(dst[:, :, P:SEQ], src[:, :, P:SEQ], broadcast(K.causal_neg[:], 1, 2), ALU.add)\
                            .then_inc(B["s1", m, i].free, 1)
                for m in range(2):
                    src = full_of(("s0", m), l)[:].rearrange("p (h n) -> p h n", h=4)
                    v.tensor_tensor(e0[:, 4 * m:4 * m + 4, :], src, broadcast(K.causal_neg[:], 1, 4), ALU.add)\
                        .then_inc(B["s0", m].free, 1)
                dve.drain()
                v.tensor_reduce(row16[:, 0, 0:8], e1, AX.X, ALU.max)
                v.tensor_reduce(row16[:, 0, 8:16], e0, AX.X, ALU.max)
                dve.drain()
                v.tensor_scalar(row16[:, 0, :], row16[:, 0, :], -DA_HD ** -0.5, None, ALU.mult)
                dve.drain().then_inc(max_ready.sem, 1)
                bank = full_of("cmean", l)
                v.tensor_tensor(conv[:], conv[:], broadcast(bank[:, 0:SEQ], 1, CT), ALU.subtract).then_inc(B["cmean"].free, 1)
                dve.drain()
                v.tensor_tensor(conv_t[:], conv[:], conv[:], ALU.mult)
                dve.drain().then_inc(conv_sq_ready.sem, 1)
                dve.wait_ge(lam_e_ready.sem, lam_e_ready.at(l))
                v.tensor_tensor(lam[:], lam_e[:, 0:1], lam_e[:, 1:2], ALU.subtract)
                dve.drain()
                v.tensor_scalar(lam[:], lam[:], K.lam_init[:, one], None, ALU.add)
                dve.wait_ge(exp_ready.sem, exp_ready.at(l))
                v.reciprocal(row16[:, 2, :], row16[:, 1, :])
                dve.drain()
                for c in (4, 12):
                    v.tensor_scalar(row16[:, 2, c:c + 4], row16[:, 2, c:c + 4], lam[:], None, ALU.mult)
                dve.drain()
                for e, c, n in ((e1, 0, SEQ), (e0, 8, P)):
                    v.tensor_tensor(e, e, broadcast(row16[:, 2, c:c + 8], 2, n), ALU.mult)
                dve.drain()
                for e in (e1, e0):
                    v.tensor_tensor(e[:, 0:4, :], e[:, 0:4, :], e[:, 4:8, :], ALU.subtract)
                dve.drain().then_inc(a_ready.sem, 1)
                dve.wait_ge(conv_std_ready.sem, conv_std_ready.at(l))
                v.reciprocal(conv_std[:], conv_std[:])
                dve.drain()
                v.tensor_tensor(conv[:], conv[:], broadcast(conv_std[:], 1, CT), ALU.mult)
                dve.drain()
                for c in range(CT):
                    v.tensor_scalar(conv[:, c, :], conv[:, c, :], vec_t[:, ch + CT + c:ch + CT + c + 1],
                                    vec_t[:, ch + 2 * CT + c:ch + 2 * CT + c + 1], ALU.mult, ALU.add)
                dve.drain().then_inc(conv_ln_ready.sem, 1)
                for t in range(T):
                    bank = full_of(("oa", t), l)
                    v.tensor_copy(oa[:, t, :], bank[:]).then_inc(B["oa", t].free, 1)
                dve.drain()
                sq = z_flat[:, 0:T * 512].rearrange("p (h n) -> p h n", n=2 * DA_HD)
                v.tensor_tensor(sq, oa_heads, oa_heads, ALU.mult)
                dve.drain()
                v.tensor_reduce(oa_std[:], sq, AX.X, ALU.add).then_inc(oa_sq_ready.sem, 1)
                dve.wait_ge(oa_std_ready.sem, oa_std_ready.at(l))
                v.reciprocal(oa_std[:], oa_std[:])
                dve.drain()
                v.tensor_tensor(oa_heads, oa_heads, broadcast(oa_std[:], 2, 2 * DA_HD), ALU.mult)
                dve.drain()
                v.tensor_tensor(oa_heads, oa_heads, broadcast(gain_o[:], 1, T * DA_HEADS), ALU.mult)
                dve.drain().then_inc(oa_ready.sem, 1)
                dve.wait_ge(conv_sig_ready.sem, conv_sig_ready.at(l))
                v.tensor_tensor(yb_t[:], conv[:], conv_t[:], ALU.mult)
                dve.drain().then_inc(ybt_ready.sem, 1)
                n = 0
                for i in range(3):
                    for h in range(2):
                        for t in range(T):
                            col = slice(h * CHUNK, (h + 1) * CHUNK)
                            dve.wait_ge(sig_ready.sem, sig_ready.at(l, n + 1))
                            bank = full_of(("y", i, h, t), l)
                            sig = sig_g[:, n % 2, :]
                            if i == 0:
                                v.tensor_tensor(merged[:, t, col], bank[:], sig, ALU.mult).then_inc(B["y", i, h, t].free, 1)
                                dve.drain().then_inc(y_used.sem, 1)
                            else:
                                if i == 1:
                                    v.tensor_tensor(y_tmp[:], bank[:], proj_b_bias[:, col], ALU.add)\
                                        .then_inc(B["y", i, h, t].free, 1)
                                    dve.drain()
                                    v.tensor_tensor(y_tmp[:], y_tmp[:], sig, ALU.mult)
                                else:
                                    v.tensor_tensor(y_tmp[:], bank[:], sig, ALU.mult).then_inc(B["y", i, h, t].free, 1)
                                dve.drain().then_inc(y_used.sem, 1)
                                v.tensor_tensor(merged[:, t, col], merged[:, t, col], y_tmp[:], ALU.add)
                                dve.drain()
                            n += 1
                dve.drain().then_inc(merged_ready.sem, 1)
                for h in range(2):
                    for t in range(T):
                        col = slice(h * CHUNK, (h + 1) * CHUNK)
                        bank = full_of(("wo", h, t), l)
                        v.tensor_tensor(y_tmp[:], bank[:], gate[:, 0, col], ALU.mult).then_inc(B["wo", h, t].free, 1)
                        dve.drain()
                        v.tensor_tensor(K.x[:, t, col], K.x[:, t, col], y_tmp[:], ALU.add)
                        dve.drain()
                dve.drain().then_inc(x_mid.sem, 1)

                norm_x(1, l)
                modulate(1, l)
                dve.wait_ge(score_ready.sem, score_ready.at(l))
                v.tensor_tensor(biased[:], score[:], broadcast(rt_bias[:], 1, T), ALU.add)
                dve.drain()
                for t in range(T):
                    for g in range(N_GROUPS):
                        v.max(out=top[:, t, g, :], in_=biased[:, t, g * PER_GROUP:(g + 1) * PER_GROUP])
                dve.drain()
                v.tensor_tensor(g_score[:], top[:, :, :, 0], top[:, :, :, 1], ALU.add)
                dve.drain()
                for t in range(T):
                    other, own = broadcast(g_score[:, t, :], 1, N_GROUPS), broadcast(g_score[:, t, :], 2, N_GROUPS)
                    v.tensor_tensor(g_cmp[:, t], other, own, ALU.is_gt)
                    v.tensor_tensor(g_eq[:, t], other, own, ALU.is_equal)
                dve.drain()
                for t in range(T):
                    v.tensor_tensor(g_eq[:, t], g_eq[:, t], K.lower8[:], ALU.mult)
                dve.drain()
                v.tensor_tensor(g_cmp[:], g_cmp[:], g_eq[:], ALU.add)
                dve.drain()
                v.tensor_reduce(g_rank[:], g_cmp[:], AX.X, ALU.add)
                dve.drain()
                v.tensor_scalar(g_rank[:], g_rank[:], TOPK_GROUPS - 0.5, None, ALU.is_lt)
                dve.drain()
                v.tensor_scalar(g_neg[:], g_rank[:], -NEG, NEG, ALU.mult, ALU.add)
                by_group = biased[:].rearrange("p t (g e) -> p t g e", g=N_GROUPS)
                v.tensor_tensor(by_group, by_group, broadcast(g_rank[:], 3, PER_GROUP), ALU.mult)
                dve.drain()
                v.tensor_tensor(by_group, by_group, broadcast(g_neg[:], 3, PER_GROUP), ALU.add)
                dve.drain()
                for t in range(T):
                    v.max(out=top8[:, t, :], in_=biased[:, t, :])
                dve.drain()
                for t in range(T):
                    v.match_replace(out=rest[:, t, :], in_to_replace=top8[:, t, :], in_values=biased[:, t, :],
                                    imm_value=3.0 * NEG)
                dve.drain()
                v.tensor_tensor(rest[:], rest[:], biased[:], ALU.not_equal)
                dve.drain()
                v.tensor_tensor(rest[:], rest[:], score[:], ALU.mult)
                dve.drain()
                v.tensor_reduce(w_sum[:], rest[:], AX.X, ALU.add)
                dve.drain()
                v.tensor_scalar(w_sum[:], w_sum[:], 1e-20, None, ALU.add)
                dve.drain()
                v.reciprocal(w_sum[:], w_sum[:])
                dve.drain()
                for t in range(T):
                    v.tensor_scalar(route[:, t, 0:N_EXPERTS], rest[:, t, :], w_sum[:, t:t + 1], ROUTED_SCALE,
                                    ALU.mult, ALU.mult)
                dve.drain()

                def expert_act(t, e, n):
                    dve.wait_ge(sig_h_ready.sem, sig_h_ready.at(l, 1) + n)
                    v.tensor_tensor(act_h[:, t, :], h_bank[t][:, 0:FF], sig_h[:, t, :], ALU.mult)
                    dve.drain()
                    v.scalar_tensor_tensor(act_h[:, t, :], h_bank[t][:, FF:2 * FF], route[:, t, e], act_h[:, t, :],
                                           ALU.mult, ALU.mult).then_inc(act_ready.sem, 1)

                for t in range(T):
                    expert_act(t, slice(SHARED, SHARED + 1), t)
                with dve.Fori(0, turns) as it:
                    for j in range(UNROLL):
                        for t in range(T):
                            expert_act(t, ds(it * UNROLL + j, 1), it * (2 * UNROLL) + (2 * (j + 1) + t))
                dve.wait_ge(w2_done.sem, w2_done.at(l, MOE_STEPS))
                for t in range(T):
                    for h in range(2):
                        col = slice(h * CHUNK, (h + 1) * CHUNK)
                        v.tensor_tensor(y_tmp[:], y_bank[t][h][:], gate[:, 1, col], ALU.mult)\
                            .then_inc(B["=moe_y", t, h].free, 1)
                        dve.drain()
                        v.tensor_tensor(K.x[:, t, col], K.x[:, t, col], y_tmp[:], ALU.add)
                        dve.drain()
                dve.drain().then_inc(x_out.sem, 1)


HEADS_2 = MLA_H + MOBA_H
GROUPS_2 = (
    ["vec", "wsT"] + [("xT", g) for g in range(4)]
    + ["c_h", "c_b", "c_c", "g_b"]
    + [(n, t) for n in ("n0", "n1", "n2", "n3", "n4", "n5") for t in range(T)]
    + ["cqT", "ckT"] + [("q", t) for t in range(T)] + [("kv", t) for t in range(T)]
    + [("bT", w) for w in range(2)]
    + [("mT", w, i) for w in range(2) for i in range(2)]
    + [("mix", t) for t in range(T)]
    + [("sm1", i) for i in range(2)] + ["sm0"] + [("sb1", par) for par in range(2)] + [("sb0", par) for par in range(2)]
    + [("aT1", i) for i in range(4)] + [("aT0", i) for i in range(2)] + [("o", t) for t in range(T)]
    + [("yT", i) for i in range(3)] + [("wo", h, t) for h in range(2) for t in range(T)]
)
GROUPS_2 += ["-pad"] * (-len(GROUPS_2) % BANKS)
READERS_2 = {"t0": "c_b", "t1": "g_b"} | {n: (n, 1) for n in ("n0", "n1", "n2", "n3", "n4", "n5")}


def second_block(nc, A, K, out):
    ds = bass.ds
    with ExitStack() as ctx:
        def sb(name, shape, dt=F32):
            return ctx.enter_context(nc.sbuf_tensor(name, shape, dt))

        def sem(name):
            return ctx.enter_context(nc.semaphore(name))

        def signal(name, per_layer=1, credit=0):
            return Signal(sem(name), per_layer, credit)

        norm_g = sb("norm_g2", [P, KT])
        gain_cq = sb("gain_cq", [P, 256])
        gain_ckv = sb("gain_ckv", [P, 128])
        gain_q = sb("gain_q", [P, MLA_QK])
        gain_kn = sb("gain_kn", [P, MLA_NOPE])
        gain_kr = sb("gain_kr", [P, MLA_ROPE])
        sg_gain = sb("sg_gain", [P, GW])
        sg_bias = sb("sg_bias", [P, GW])
        gain_moba = sb("gain_moba", [P, 2, MOBA_HD])
        w_uq = sb("w_uq", [P, 2, MLA_H * MLA_QK])
        w_ukv = sb("w_ukv", [P, MLA_H * 2 * 64])
        sg_w = sb("sg_w", [P, SG_G, P])
        cw_rows = sb("cw_rows", [6, P])
        sb_rows = sb("sb_rows", [SG_G, P])
        vec_t = sb("vec_t2", [P, 6 + SG_G])
        ws_t = sb("ws_t", [P, SG_G, P])
        std = sb("std2", [P, T])
        sq_sum = sb("sq_sum2", [P, T])
        nat = sb("nat", [P, T, NAT_COLS])
        cbr = sb("cbr", [P, 4, 2, SEQ])
        sig_b = sb("sig_b", [P, 2, SEQ])
        zpad = sb("zpad", [P, 2, 2 + SEQ])
        cv = sb("cv", [P, 2, SEQ])
        sig = sb("sig_acd", [P, 3, T, GW])
        scr = sb("scr", [P, T, 512])
        stat = sb("stat", [P, T, 12])
        mean_v = sb("mean_v", [P, T])
        stat2 = sb("stat2", [P, T, 8])
        kr = sb("kr", [P, T, MLA_ROPE])
        c_t = sb("c_t", [P, 3, SEQ])
        q_nat = sb("q_nat", [P, T, MLA_H, MLA_QK])
        kv_nat = sb("kv_nat", [P, T, MLA_H, 2 * 64])
        k_nat = sb("k_nat", [P, T, MLA_H, MLA_QK])
        rope1 = sb("rope1", [P, T, 8, 16])
        rope2 = sb("rope2", [P, T, 8, 16])
        rope3 = sb("rope3", [P, T, 8, 16])
        mqk_t = sb("mqk_t", [MLA_QK, 2, MLA_H, SEQ])
        bqk_t = sb("bqk_t", [P, 2, 2, SEQ])
        e1 = sb("e1_2", [P, HEADS_2, SEQ])
        e0 = sb("e0_2", [P, HEADS_2, P])
        row16 = sb("row16_2", [P, 3, 2 * HEADS_2])
        a_t = sb("a_t2", [P, HEADS_2, 3, P])
        y_nat = K.h_t[:].rearrange("p k n -> p (k n)")[:, 0:T * 3 * GW].rearrange("p (t i n) -> p t i n", t=T, i=3)
        y_t = K.xn[:].rearrange("p t n -> p (t n)").rearrange("p (k n) -> p k n", n=SEQ)

        def seg(name, n):
            return nat[:, :, NAT[name]:NAT[name] + n]

        B, full, free = bank_plan(GROUPS_2, K.psum, sem, "2")
        filled = [Signal(sem(f"slot{s}_filled2")) for s in range(RING)]
        names = [c[0] for c in CHUNKS_2] + [("wo", 0), ("wo", 1)]
        names += [None] * (-len(names) % RING)
        readers = [READERS_2.get(n) if n in READERS_2 else ((n[0], n[1], 1) if n else None) for n in names]
        C, loads, arrived = {}, [], [0] * RING
        for i, name in enumerate(names):
            s = i % RING
            if name is None:
                continue
            arrived[s] += 32 if name == "n0" else 16
            C[name] = Chunk(K.slots[s], filled[s], arrived[s])
            earlier = [(j, readers[j]) for j in range(s, i, RING) if readers[j]]
            last = [readers[j] for j in range(s, len(names), RING) if readers[j]][-1]
            loads.append((name, s, earlier[-1][1] if earlier else None, last))
        for s in range(RING):
            filled[s].n = arrived[s]

        N_PARAMS = 15
        params = signal("params_loaded2", 16 * N_PARAMS)
        x_out = signal("x_after_layer2", 1, 1)
        std_ready, xn_ready, ht_ready = signal("x_std_ready_2"), signal("xn_ready_2"), signal("ht_ready_2")
        vec_ready, wst_ready = signal("vec_t_ready2"), signal("ws_t_ready")
        cbr_ready, nat_ready, sig_acd_ready = signal("cbr_ready"), signal("nat_ready"), signal("sig_acd_ready")
        stat_ready, stat_std_ready = signal("stat_ready"), signal("stat_std_ready")
        c_ready, ct_ready, qkv_ready = signal("c_normed_ready"), signal("c_t_ready"), signal("q_kv_ready")
        stat2_ready, stat2_std_ready = signal("stat2_ready"), signal("stat2_std_ready")
        moba_ready, mla_ready, vn_ready = signal("moba_qk_ready"), signal("mla_qk_ready"), signal("vn_ready")
        bt_ready, mt_ready = signal("moba_t_ready"), signal("mla_t_ready")
        max_ready, exp_ready, a_ready, at_ready = (signal("row_max_ready2"), signal("exp_ready2"), signal("a_ready2"),
                                                   signal("a_t_ready2"))
        yb_ready, y_ready, yt_ready = signal("yb_ready"), signal("y_nat_ready"), signal("y_t_ready")
        stored = sem("stored")

        block = ctx.enter_context(nc.Block())

        @block.sync
        def _(sp):
            for b in range(BANKS):
                sp.sem_inc(free[b].sem, 1)
                sp.sem_inc(full[b].sem, full[b].credit)
            sp.sem_inc(x_out.sem, 1)
            with sp.Fori(0, DEPTH) as l:
                for name, s, before, last in loads:
                    if before is None:
                        sp.wait_ge(B[last].full, B[last].full_before(l))
                    else:
                        sp.wait_ge(B[before].full, B[before].full_at(l))
                    if name in READERS_2:
                        _, col, n, _ = next(c for c in CHUNKS_2 if c[0] == name)
                        src = A["w_in_2"][ds(l, 1), :, col:col + n].rearrange("a (p k) n -> p (a k) n", k=KT)
                    else:
                        n = CHUNK
                        src = A["w_out_2"][ds(l, 1), :, name[1] * n:(name[1] + 1) * n].rearrange("a (k p) n -> p (a k) n", p=P)
                    for half in (slice(P // 2, P), slice(0, P // 2)) if name == "n0" else (slice(0, P),):
                        sp.dma_start(K.slots[s][half, :, 0:n], src[half]).then_inc(filled[s].sem, 16)
            sp.wait_ge(x_out.sem, x_out.credit + DEPTH)
            for t in range(T):
                sp.dma_start(out[0, t * P:(t + 1) * P, :], K.x[:, t, :]).then_inc(stored, 16)
            sp.wait_ge(stored, 16 * T)

        @block.gpsimd
        def _(pool):
            with pool.Fori(0, DEPTH) as l:
                pool.wait_ge(x_out.sem, x_out.at(l, 0))
                one = ds(l, 1)

                def load(dst, src):
                    pool.dma_start(dst, src).then_inc(params.sem, 16)

                load(norm_g[:], A["norm_g_2"][one].rearrange("a (p k) -> p (a k)", k=KT))
                load(cw_rows[:], A["conv_w_2"][one].rearrange("a k (c p) -> (a k c) p", p=P))
                load(sb_rows[:], A["sg_b_2"][one].rearrange("a g p -> (a g) p"))
                load(sg_w[:], A["sg_w_2"][one].rearrange("a g t s -> t (a g) s"))
                for dst, name in ((gain_cq, "mla_q_norm_g_2"), (gain_ckv, "mla_kv_norm_g_2"), (gain_q, "mla_q_g_2"),
                                  (gain_kn, "mla_k_nope_g_2"), (gain_kr, "mla_k_rope_g_2"), (sg_gain, "sg_ln_g_2"),
                                  (sg_bias, "sg_ln_b_2")):
                    load(dst[:], A[name][one].to_broadcast(list(dst.shape)))
                for w, name in enumerate(("moba_q_g_2", "moba_k_g_2")):
                    load(gain_moba[:, w, :], A[name][one].to_broadcast([P, MOBA_HD]))
                load(w_uq[:], A["mla_w_uq_2"][one].rearrange("a (k p) n -> p (a k) n", p=P))
                load(w_ukv[:], A["mla_w_ukv_2"][one].rearrange("a p n -> p (a n)"))

        @block.tensor
        def _(pe):
            def begin(name, l):
                pe.wait_ge(B[name].free, B[name].free_at(l))
                return B[name].tile

            def chunk(name, l):
                pe.wait_ge(C[name].filled, C[name].filled_at(l))
                return C[name].tile

            def rows(name, l, w, t, stationary, cols=CHUNK):
                bank = begin(name, l)
                for k in range(KT):
                    mm = nc.tensor.matmul(bank[:, 0:cols], stationary[:, k, t * P:(t + 1) * P], w[:, k, 0:cols],
                                          start=(k == 0), stop=(k == KT - 1))
                mm.then_inc(B[name].full, 1)

            def turn(name, l, pieces, size=P):
                bank = begin(name, l)
                for col, src in pieces:
                    mm = nc.tensor.transpose(bank[0:size, col:col + P], src, K.ident[:])
                mm.then_inc(B[name].full, 1)

            with pe.Fori(0, DEPTH) as l:
                pe.wait_ge(params.sem, params.at(l, params.n))
                bank = begin("vec", l)
                turn("wsT", l, [(g * P, sg_w[:, g, :]) for g in range(SG_G)])
                nc.tensor.transpose(bank[:, 0:6], cw_rows[:], K.ident[0:6, 0:6])
                nc.tensor.transpose(bank[:, 6:6 + SG_G], sb_rows[:], K.ident[0:SG_G, 0:SG_G]).then_inc(B["vec"].full, 1)
                pe.wait_ge(xn_ready.sem, xn_ready.at(l))
                for g in range(4):
                    turn(("xT", g), l, [(j * SEQ + t * P, K.xn[:, t, 2 * g + j::KT]) for j in range(2) for t in range(T)])
                pe.wait_ge(ht_ready.sem, ht_ready.at(l))
                for name, pair in (("t0", ("c_h", "c_b")), ("t1", ("c_c", "g_b"))):
                    w = chunk(name, l)
                    for i, group in enumerate(pair):
                        bank = begin(group, l)
                        for j in range(2):
                            c = 2 * i + j
                            for k in range(KT):
                                mm = nc.tensor.matmul(bank[:, j * SEQ:(j + 1) * SEQ], w[:, k, c * P:(c + 1) * P],
                                                      K.h_t[:, k, :], start=(k == 0), stop=(k == KT - 1))
                        mm.then_inc(B[group].full, 1)
                for name, _, n, place in CHUNKS_2:
                    if place is not None:
                        w = chunk(name, l)
                        for t in range(T):
                            rows((name, t), l, w, t, K.h_t, n)
                pe.wait_ge(c_ready.sem, c_ready.at(l))
                turn("cqT", l, [(k * SEQ + t * P, nat[:, t, k * P:(k + 1) * P]) for k in range(2) for t in range(T)])
                turn("ckT", l, [(t * P, nat[:, t, NAT["ckv"]:NAT["ckv"] + P]) for t in range(T)])
                pe.wait_ge(ct_ready.sem, ct_ready.at(l))
                for t in range(T):
                    bank = begin(("q", t), l)
                    for k in range(2):
                        mm = nc.tensor.matmul(bank[:, 0:MLA_H * MLA_QK], c_t[:, k, t * P:(t + 1) * P], w_uq[:, k, :],
                                              start=(k == 0), stop=(k == 1))
                    mm.then_inc(B["q", t].full, 1)
                for t in range(T):
                    bank = begin(("kv", t), l)
                    nc.tensor.matmul(bank[:], c_t[:, 2, t * P:(t + 1) * P], w_ukv[:], start=True, stop=True)\
                        .then_inc(B["kv", t].full, 1)
                pe.wait_ge(moba_ready.sem, moba_ready.at(l))
                for w, name in enumerate(("mq", "mk")):
                    turn(("bT", w), l, [(i * SEQ + t * P, nat[:, t, NAT[name] + i * P:NAT[name] + (i + 1) * P])
                                        for i in range(2) for t in range(T)])
                pe.wait_ge(mla_ready.sem, mla_ready.at(l))
                for w, src in enumerate((q_nat, k_nat)):
                    for i in range(2):
                        turn(("mT", w, i), l, [(j * SEQ + t * P, src[:, t, 2 * i + j, :]) for j in range(2) for t in range(T)],
                             MLA_QK)
                pe.wait_ge(wst_ready.sem, wst_ready.at(l))
                pe.wait_ge(vn_ready.sem, vn_ready.at(l))
                for t in range(T):
                    bank = begin(("mix", t), l)
                    for g in range(SG_G):
                        mm = nc.tensor.matmul(bank[:, g * 64:(g + 1) * 64], ws_t[:, g, :], seg("sv", GW)[:, t, g * 64:(g + 1) * 64],
                                              start=True, stop=True)
                    mm.then_inc(B["mix", t].full, 1)
                pe.wait_ge(mt_ready.sem, mt_ready.at(l))
                for i in range(2):
                    bank = begin(("sm1", i), l)
                    for j in range(2):
                        mm = nc.tensor.matmul(bank[:, j * SEQ:(j + 1) * SEQ], mqk_t[:, 0, 2 * i + j, P:SEQ],
                                              mqk_t[:, 1, 2 * i + j, :], start=True, stop=True)
                    mm.then_inc(B["sm1", i].full, 1)
                bank = begin("sm0", l)
                for h in range(MLA_H):
                    mm = nc.tensor.matmul(bank[:, h * P:(h + 1) * P], mqk_t[:, 0, h, 0:P], mqk_t[:, 1, h, 0:P],
                                          start=True, stop=True)
                mm.then_inc(B["sm0"].full, 1)
                pe.wait_ge(bt_ready.sem, bt_ready.at(l))
                for n, q0, keys in (("sb1", P, SEQ), ("sb0", 0, P)):
                    for par in range(2):
                        part = slice(64 * par, 64 * par + 64)
                        bank = begin((n, par), l)
                        for i in range(2):
                            mm = nc.tensor.matmul(bank[:, i * keys:(i + 1) * keys], bqk_t[part, 0, i, q0:q0 + P],
                                                  bqk_t[part, 1, i, 0:keys], start=True, stop=True)
                        mm.then_inc(B[n, par].full, 1)
                pe.wait_ge(a_ready.sem, a_ready.at(l))
                for i in range(4):
                    turn(("aT1", i), l, [((2 * j + b) * P, e1[:, 2 * i + j, b * P:(b + 1) * P])
                                         for j in range(2) for b in range(2)])
                for i in range(2):
                    turn(("aT0", i), l, [(j * P, e0[:, 4 * i + j, :]) for j in range(4)])
                pe.wait_ge(at_ready.sem, at_ready.at(l))
                for t in range(T):
                    bank = begin(("o", t), l)
                    for r in range(HEADS_2):
                        if r < MLA_H:
                            col, values = r * 64, lambda b, r=r: kv_nat[:, b, r, 64:128]
                        else:
                            head = 2 * ((r - MLA_H) % 2) + (r - MLA_H) // 2
                            col, values = (MLA_H + head) * 64, lambda b, head=head: seg("mv", GW)[:, b, head * 64:(head + 1) * 64]
                        o = bank[:, col:col + 64]
                        if t == 0:
                            mm = nc.tensor.matmul(o, a_t[:, r, 0, :], values(0), start=True, stop=True)
                        else:
                            nc.tensor.matmul(o, a_t[:, r, 1, :], values(0), start=True, stop=False)
                            mm = nc.tensor.matmul(o, a_t[:, r, 2, :], values(1), start=False, stop=True)
                    mm.then_inc(B["o", t].full, 1)
                pe.wait_ge(y_ready.sem, y_ready.at(l))
                for i in range(3):
                    turn(("yT", i), l, [(j * SEQ + t * P, y_nat[:, t, i, j * P:(j + 1) * P]) for j in range(2) for t in range(T)])
                pe.wait_ge(yb_ready.sem, yb_ready.at(l))
                pe.wait_ge(yt_ready.sem, yt_ready.at(l))
                for h in range(2):
                    w = chunk(("wo", h), l)
                    for t in range(T):
                        rows(("wo", h, t), l, w, t, y_t)

        @block.scalar
        def _(act):
            def full_of(name, l):
                act.wait_ge(B[name].full, B[name].full_at(l))
                return B[name].tile

            def copy_out(name, l, dst, src):
                nc.scalar.activation(dst, src, ACT.Copy).then_inc(B[name].free, 1)

            def pairs(bank):
                return bank[:].rearrange("p (c n) -> p c n", c=2)

            with act.Fori(0, DEPTH) as l:
                act.wait_ge(x_out.sem, x_out.at(l, 0))
                for t in range(T):
                    nc.scalar.activation(K.xn[:, t, :], K.x[:, t, :], ACT.Square, accum_out=sq_sum[:, t:t + 1])
                act.drain()
                nc.scalar.activation(std[:], sq_sum[:], ACT.Sqrt, scale=1.0 / D, bias=K.eps[:]).then_inc(std_ready.sem, 1)
                bank = full_of("vec", l)
                copy_out("vec", l, vec_t[:], bank[:, 0:6 + SG_G])
                act.drain().then_inc(vec_ready.sem, 1)
                for i, name in enumerate(("c_h", "c_b", "c_c", "g_b")):
                    bank = full_of(name, l)
                    if name == "g_b":
                        nc.scalar.activation(sig_b[:], pairs(bank), ACT.Sigmoid)
                    copy_out(name, l, cbr[:, i], pairs(bank))
                act.drain().then_inc(cbr_ready.sem, 1)
                for name, _, n, place in CHUNKS_2:
                    if place is not None:
                        for t in range(T):
                            bank = full_of((name, t), l)
                            copy_out((name, t), l, nat[:, t, place:place + n], bank[:, 0:n])
                act.drain().then_inc(nat_ready.sem, 1)
                for i, name in enumerate(("ga", "gc", "gd")):
                    nc.scalar.activation(sig[:, i], seg(name, GW), ACT.Sigmoid)
                act.drain().then_inc(sig_acd_ready.sem, 1)
                act.wait_ge(stat_ready.sem, stat_ready.at(l))
                nc.scalar.activation(stat[:], stat[:], ACT.Sqrt, bias=K.eps[:]).then_inc(stat_std_ready.sem, 1)
                bank = full_of("cqT", l)
                copy_out("cqT", l, c_t[:, 0:2, :], pairs(bank))
                bank = full_of("ckT", l)
                copy_out("ckT", l, c_t[:, 2, :], bank[:, 0:SEQ])
                act.drain().then_inc(ct_ready.sem, 1)
                for t in range(T):
                    bank = full_of(("q", t), l)
                    copy_out(("q", t), l, q_nat[:, t].rearrange("p h n -> p (h n)"), bank[:, 0:MLA_H * MLA_QK])
                for t in range(T):
                    bank = full_of(("kv", t), l)
                    copy_out(("kv", t), l, kv_nat[:, t].rearrange("p h n -> p (h n)"), bank[:])
                act.drain().then_inc(qkv_ready.sem, 1)
                act.wait_ge(stat2_ready.sem, stat2_ready.at(l))
                nc.scalar.activation(stat2[:], stat2[:], ACT.Sqrt, bias=K.eps[:]).then_inc(stat2_std_ready.sem, 1)
                for w in range(2):
                    bank = full_of(("bT", w), l)
                    copy_out(("bT", w), l, bqk_t[:, w], pairs(bank))
                act.drain().then_inc(bt_ready.sem, 1)
                for w in range(2):
                    for i in range(2):
                        bank = full_of(("mT", w, i), l)
                        copy_out(("mT", w, i), l, mqk_t[:, w, 2 * i:2 * i + 2, :],
                                 bank[0:MLA_QK, :].rearrange("p (c n) -> p c n", c=2))
                act.drain().then_inc(mt_ready.sem, 1)
                act.wait_ge(max_ready.sem, max_ready.at(l))
                for r in range(2 * HEADS_2):
                    e = e1[:, r, :] if r < HEADS_2 else e0[:, r - HEADS_2, :]
                    scale = (MLA_QK if r % HEADS_2 < MLA_H else MOBA_HD) ** -0.5
                    nc.scalar.activation(e, e, ACT.Exp, bias=row16[:, 0, r:r + 1], scale=scale,
                                         accum_out=row16[:, 1, r:r + 1])
                act.drain().then_inc(exp_ready.sem, 1)
                for i in range(4):
                    bank = full_of(("aT1", i), l)
                    copy_out(("aT1", i), l, a_t[:, 2 * i:2 * i + 2, 1:3, :],
                             bank[:].rearrange("p (h b n) -> p h b n", h=2, b=2))
                for i in range(2):
                    bank = full_of(("aT0", i), l)
                    copy_out(("aT0", i), l, a_t[:, 4 * i:4 * i + 4, 0, :], bank[:].rearrange("p (h n) -> p h n", h=4))
                act.drain().then_inc(at_ready.sem, 1)
                for i, k in enumerate((0, 4, 6)):
                    bank = full_of(("yT", i), l)
                    copy_out(("yT", i), l, y_t[:, k:k + 2, :], pairs(bank))
                act.drain().then_inc(yt_ready.sem, 1)

        @block.vector
        def _(dve):
            v = nc.vector

            def full_of(name, l):
                dve.wait_ge(B[name].full, B[name].full_at(l))
                return B[name].tile

            def square_sums(dst, src, scratch, n):
                v.tensor_tensor(scratch, src, src, ALU.mult)
                dve.drain()
                v.tensor_reduce(dst, scratch, AX.X, ALU.add)
                dve.drain()
                v.tensor_scalar(dst, dst, 1.0 / n, None, ALU.mult)
                dve.drain()

            def rotate(x1, x2, o1, o2, freqs, heads, half):
                cos, sin = K.cos[:, :, freqs:freqs + half], K.sin[:, :, freqs:freqs + half]
                if heads:
                    cos, sin = broadcast(cos, 2, heads), broadcast(sin, 2, heads)
                    r1, r2, r3 = (r[:, :, 0:heads, 0:half] for r in (rope1, rope2, rope3))
                else:
                    r1, r2, r3 = (r[:, :, 0, 0:half] for r in (rope1, rope2, rope3))
                v.tensor_tensor(r1, x1, cos, ALU.mult)
                v.tensor_tensor(r2, x2, sin, ALU.mult)
                v.tensor_tensor(r3, x1, sin, ALU.mult)
                dve.drain()
                v.tensor_tensor(r1, r1, r2, ALU.subtract)
                dve.drain()
                v.tensor_tensor(r2, x2, cos, ALU.mult)
                dve.drain()
                v.tensor_copy(o1, r1)
                v.tensor_tensor(o2, r2, r3, ALU.add)
                dve.drain()

            v.memset(zpad[:, :, 0:2], 0.0)
            with dve.Fori(0, DEPTH) as l:
                dve.wait_ge(std_ready.sem, std_ready.at(l))
                v.reciprocal(std[:], std[:])
                dve.drain()
                for t in range(T):
                    v.tensor_scalar(K.xn[:, t, :], K.x[:, t, :], std[:, t:t + 1], None, ALU.mult)
                dve.drain().then_inc(xn_ready.sem, 1)
                dve.wait_ge(params.sem, params.at(l, params.n))
                bank = full_of("wsT", l)
                v.tensor_tensor(ws_t[:], bank[:].rearrange("p (g n) -> p g n", g=SG_G), broadcast(K.head[:], 1, SG_G), ALU.mult)\
                    .then_inc(B["wsT"].free, 1)
                dve.drain().then_inc(wst_ready.sem, 1)
                for g in range(4):
                    bank = full_of(("xT", g), l)
                    for j in range(2):
                        k = 2 * g + j
                        ins = v.tensor_scalar(K.h_t[:, k, :], bank[:, j * SEQ:(j + 1) * SEQ], norm_g[:, k:k + 1], None, ALU.mult)
                    ins.then_inc(B["xT", g].free, 1)
                dve.drain().then_inc(ht_ready.sem, 1)
                dve.wait_ge(vec_ready.sem, vec_ready.at(l))
                dve.wait_ge(cbr_ready.sem, cbr_ready.at(l))
                v.tensor_tensor(zpad[:, :, 2:], cbr[:, 2], cbr[:, 0], ALU.mult)
                dve.drain()
                for k in range(3):
                    for c in range(2):
                        w = vec_t[:, 2 * k + c:2 * k + c + 1]
                        if k == 0:
                            v.tensor_scalar(cv[:, c, :], zpad[:, c, 0:SEQ], w, None, ALU.mult)
                        else:
                            v.scalar_tensor_tensor(cv[:, c, :], zpad[:, c, k:k + SEQ], w, cv[:, c, :], ALU.mult, ALU.add)
                    dve.drain()
                v.tensor_tensor(cv[:], cv[:], cbr[:, 1], ALU.mult)
                v.tensor_tensor(sig_b[:], sig_b[:], cbr[:, 3], ALU.mult)
                dve.drain()
                v.tensor_tensor(y_t[:, 2:4, :], cv[:], sig_b[:], ALU.mult)
                dve.drain().then_inc(yb_ready.sem, 1)
                dve.wait_ge(nat_ready.sem, nat_ready.at(l))
                v.tensor_reduce(mean_v[:], seg("sv", GW), AX.X, ALU.add)
                dve.drain()
                v.tensor_scalar(mean_v[:], mean_v[:], 1.0 / GW, None, ALU.mult)
                dve.drain()
                for t in range(T):
                    v.tensor_scalar(seg("sv", GW)[:, t, :], seg("sv", GW)[:, t, :], mean_v[:, t:t + 1], None, ALU.subtract)
                dve.drain()
                square_sums(stat[:, :, 11], seg("sv", GW), scr[:, :, 0:GW], GW)
                square_sums(stat[:, :, 0], seg("cq", 256), scr[:, :, 0:256], 256)
                square_sums(stat[:, :, 1], seg("ckv", 128), scr[:, :, 0:128], 128)
                square_sums(stat[:, :, 2], seg("kr", MLA_ROPE), scr[:, :, 0:MLA_ROPE], MLA_ROPE)
                moba = nat[:, :, NAT["mq"]:NAT["mq"] + 512].rearrange("p t (h n) -> p t h n", n=MOBA_HD)
                square_sums(stat[:, :, 3:11], moba, scr[:].rearrange("p t (h n) -> p t h n", n=MOBA_HD), MOBA_HD)
                dve.drain().then_inc(stat_ready.sem, 1)
                dve.wait_ge(stat_std_ready.sem, stat_std_ready.at(l))
                v.reciprocal(stat[:], stat[:])
                dve.drain()
                for i, (name, n, gain) in enumerate((("cq", 256, gain_cq), ("ckv", 128, gain_ckv), ("kr", MLA_ROPE, gain_kr))):
                    for t in range(T):
                        v.scalar_tensor_tensor(seg(name, n)[:, t, :], seg(name, n)[:, t, :], stat[:, t, i:i + 1], gain[:],
                                               ALU.mult, ALU.mult)
                dve.drain().then_inc(c_ready.sem, 1)
                v.tensor_tensor(moba, moba, broadcast(stat[:, :, 3:11], 3, MOBA_HD), ALU.mult)
                dve.drain()
                for w in range(2):
                    part = moba[:, :, 4 * w:4 * w + 4, :]
                    v.tensor_tensor(part, part, broadcast(broadcast(gain_moba[:, w, :], 1, 4), 1, T), ALU.mult)
                dve.drain()
                x1, x2 = moba[:, :, :, 0:8], moba[:, :, :, 8:16]
                rotate(x1, x2, x1, x2, ROPES[2][0], 8, 8)
                dve.drain().then_inc(moba_ready.sem, 1)
                for t in range(T):
                    v.scalar_tensor_tensor(seg("sv", GW)[:, t, :], seg("sv", GW)[:, t, :], stat[:, t, 11:12], sg_gain[:],
                                           ALU.mult, ALU.mult)
                dve.drain()
                v.tensor_tensor(seg("sv", GW), seg("sv", GW), broadcast(sg_bias[:], 1, T), ALU.add)
                dve.drain().then_inc(vn_ready.sem, 1)
                krs = seg("kr", MLA_ROPE)
                rotate(krs[:, :, 0:16], krs[:, :, 16:32], kr[:, :, 0:16], kr[:, :, 16:32], ROPES[1][0], None, 16)
                dve.wait_ge(qkv_ready.sem, qkv_ready.at(l))
                for t in range(T):
                    square_sums(stat2[:, t, 0:4], q_nat[:, t], scr[:, 0, 0:MLA_H * MLA_QK].rearrange("p (h n) -> p h n", h=MLA_H), MLA_QK)
                    square_sums(stat2[:, t, 4:8], kv_nat[:, t, :, 0:64], scr[:, 0, 0:MLA_H * 64].rearrange("p (h n) -> p h n", h=MLA_H), 64)
                dve.drain().then_inc(stat2_ready.sem, 1)
                dve.wait_ge(stat2_std_ready.sem, stat2_std_ready.at(l))
                v.reciprocal(stat2[:], stat2[:])
                dve.drain()
                for t in range(T):
                    v.tensor_tensor(q_nat[:, t], q_nat[:, t], broadcast(stat2[:, t, 0:4], 2, MLA_QK), ALU.mult)
                    v.tensor_tensor(k_nat[:, t, :, 0:64], kv_nat[:, t, :, 0:64], broadcast(stat2[:, t, 4:8], 2, 64), ALU.mult)
                    v.tensor_copy(k_nat[:, t, :, 64:], broadcast(kr[:, t, :], 1, MLA_H))
                dve.drain()
                for t in range(T):
                    v.tensor_tensor(q_nat[:, t], q_nat[:, t], broadcast(gain_q[:], 1, MLA_H), ALU.mult)
                    v.tensor_tensor(k_nat[:, t, :, 0:64], k_nat[:, t, :, 0:64], broadcast(gain_kn[:], 1, MLA_H), ALU.mult)
                dve.drain()
                q1, q2 = q_nat[:, :, :, 64:80], q_nat[:, :, :, 80:96]
                rotate(q1, q2, q1, q2, ROPES[1][0], MLA_H, 16)
                dve.drain().then_inc(mla_ready.sem, 1)
                dve.wait_ge(sig_acd_ready.sem, sig_acd_ready.at(l))
                for i, name in enumerate(("ga", "gc", "gd")):
                    v.tensor_tensor(sig[:, i], sig[:, i], seg(name, GW), ALU.mult)
                dve.drain()
                for t in range(T):
                    bank = full_of(("mix", t), l)
                    for g in range(SG_G):
                        col = slice(g * 64, (g + 1) * 64)
                        ins = v.scalar_tensor_tensor(y_nat[:, t, 1, col], bank[:, col], vec_t[:, 6 + g:7 + g],
                                                     seg("su", GW)[:, t, col], ALU.add, ALU.mult)
                    ins.then_inc(B["mix", t].free, 1)
                dve.drain()
                v.tensor_tensor(y_nat[:, :, 1], y_nat[:, :, 1], sig[:, 1], ALU.mult)
                for r0, groups in ((0, [("sm1", 0), ("sm1", 1)]), (MLA_H, [("sb1", 0), ("sb1", 1)])):
                    if r0:
                        src = full_of("sm0", l)[:].rearrange("p (h n) -> p h n", h=4)
                        v.tensor_tensor(e0[:, 0:4, :], src, broadcast(K.causal_neg[:], 1, 4), ALU.add).then_inc(B["sm0"].free, 1)
                    for i, name in enumerate(groups):
                        src = full_of(name, l)[:].rearrange("p (h n) -> p h n", h=2)
                        dst = e1[:, r0 + 2 * i:r0 + 2 * i + 2, :]
                        v.tensor_copy(dst[:, :, 0:P], src[:, :, 0:P])
                        v.tensor_tensor(dst[:, :, P:SEQ], src[:, :, P:SEQ], broadcast(K.causal_neg[:], 1, 2), ALU.add)\
                            .then_inc(B[name].free, 1)
                for par in range(2):
                    src = full_of(("sb0", par), l)[:, 0:2 * P].rearrange("p (h n) -> p h n", h=2)
                    v.tensor_tensor(e0[:, MLA_H + 2 * par:MLA_H + 2 * par + 2, :], src, broadcast(K.causal_neg[:], 1, 2), ALU.add)\
                        .then_inc(B["sb0", par].free, 1)
                dve.drain()
                v.tensor_reduce(row16[:, 0, 0:HEADS_2], e1[:], AX.X, ALU.max)
                v.tensor_reduce(row16[:, 0, HEADS_2:], e0[:], AX.X, ALU.max)
                dve.drain()
                for r0 in (0, HEADS_2):
                    v.tensor_scalar(row16[:, 0, r0:r0 + 4], row16[:, 0, r0:r0 + 4], -MLA_QK ** -0.5, None, ALU.mult)
                    v.tensor_scalar(row16[:, 0, r0 + 4:r0 + 8], row16[:, 0, r0 + 4:r0 + 8], -MOBA_HD ** -0.5, None, ALU.mult)
                dve.drain().then_inc(max_ready.sem, 1)
                dve.wait_ge(exp_ready.sem, exp_ready.at(l))
                v.reciprocal(row16[:, 2, :], row16[:, 1, :])
                dve.drain()
                for e, c, n in ((e1[:], 0, SEQ), (e0[:], HEADS_2, P)):
                    v.tensor_tensor(e, e, broadcast(row16[:, 2, c:c + HEADS_2], 2, n), ALU.mult)
                dve.drain().then_inc(a_ready.sem, 1)
                for t in range(T):
                    bank = full_of(("o", t), l)
                    v.tensor_tensor(y_nat[:, t, 0], bank[:, 0:GW], sig[:, 0, t], ALU.mult)
                    v.tensor_tensor(y_nat[:, t, 2], bank[:, GW:2 * GW], sig[:, 2, t], ALU.mult).then_inc(B["o", t].free, 1)
                dve.drain().then_inc(y_ready.sem, 1)
                for h in range(2):
                    for t in range(T):
                        col = slice(h * CHUNK, (h + 1) * CHUNK)
                        bank = full_of(("wo", h, t), l)
                        v.tensor_tensor(K.x[:, t, col], K.x[:, t, col], bank[:], ALU.add).then_inc(B["wo", h, t].free, 1)
                dve.drain().then_inc(x_out.sem, 1)


class Kept:
    pass


def build(nc, A, out):
    with ExitStack() as ctx:
        K = Kept()

        def keep(name, shape):
            return ctx.enter_context(nc.sbuf_tensor(name, shape, F32))

        K.x = keep("x_tokens", [P, T, D])
        K.xn = keep("xn", [P, T, D])
        K.h_t = keep("h_t", [P, KT, SEQ])
        ring = keep("weight_ring", [P, RING, KT, CHUNK])
        K.slots = [ring[:, s] for s in range(RING)]
        K.ident = keep("ident", [P, P])
        K.ones = keep("ones", [P, P])
        K.mean_conv = keep("mean_conv", [P, P])
        K.causal_neg = keep("causal_neg", [P, P])
        K.strict_neg = keep("strict_neg", [P, P])
        K.strict_01 = keep("strict_01", [P, P])
        K.tail = keep("tail", [P, P])
        K.head = keep("head", [P, P])
        K.lower8 = keep("lower8", [P, N_GROUPS, N_GROUPS])
        K.eps = keep("eps", [P, 1])
        K.lam_init = keep("lam_init", [P, DEPTH])
        K.lam_rest = keep("lam_rest", [P, DEPTH])
        K.sin = keep("sin", [P, T, N_FREQ])
        K.cos = keep("cos", [P, T, N_FREQ])
        K.c_act = keep("c_act", [P, KT])
        psum = ctx.enter_context(nc.psum_tensor("banks", [P, BANKS, 512], F32))
        K.psum = [psum[:, b] for b in range(BANKS)]
        constants(nc, A, K)
        first_block(nc, A, K)
        second_block(nc, A, K, out)


INPUTS = [
    "x", "c", "positions", "w_mod", "b_mod", "norm_mix_g", "norm_ffn_g", "w_in", "qn_g", "kn_g", "lam_q1", "lam_k1",
    "lam_q2", "lam_k2", "subln_g", "w_proj_a", "w_dw", "b_dw", "conv_ln_g", "conv_ln_b", "w_proj_b", "b_proj_b",
    "w_proj_c", "w_out", "w_router", "b_router", "w1", "w3", "w2", "ws1", "ws3", "ws2", "positions_2", "norm_g_2",
    "w_in_2", "mla_q_norm_g_2", "mla_w_uq_2", "mla_kv_norm_g_2", "mla_w_ukv_2", "mla_q_g_2", "mla_k_nope_g_2",
    "mla_k_rope_g_2", "conv_w_2", "sg_ln_g_2", "sg_ln_b_2", "sg_w_2", "sg_b_2", "moba_q_g_2", "moba_k_g_2", "w_out_2",
]


def kernel(**inputs):
    from concourse import bacc
    from concourse.bass_utils import run_bass_kernel_spmd

    nc = bacc.Bacc("TRN2", target_bir_lowering=False, num_devices=1)
    arrays, A = {}, {}
    for name in INPUTS:
        a = np.ascontiguousarray(inputs[name])
        arrays[f"in_{name}"] = a
        A[name] = nc.dram_tensor(f"in_{name}", a.shape, mybir.dt.from_np(a.dtype), kind="ExternalInput").ap()
    out = nc.dram_tensor("out", (1, SEQ, D), F32, kind="ExternalOutput").ap()
    build(nc, A, out)
    result = run_bass_kernel_spmd(nc, [arrays], core_ids=[0])
    return result.results[0]["out"]
```

```python
from contextlib import ExitStack
import math

import numpy as np
import concourse.bass as bass
from concourse import mybir

F32 = mybir.dt.float32
I32 = mybir.dt.int32
BF16 = mybir.dt.bfloat16
ALU = mybir.AluOpType
ACT = mybir.ActivationFunctionType
AX = mybir.AxisListType

P = 128
T = 2
SEQ = T * P
D = 1024
KT = D // P
DEPTH = 2
EPS = 1e-6
NEG = -1e30
CHUNK = 512
RING = 4
BANKS = 8

DA_HEADS, DA_HD = 4, 64
SB_HEADS, SB_HD = 8, 64
CONV_CH, TAPS = 512, 31
CT = CONV_CH // P
N_EXPERTS, N_GROUPS, TOPK_GROUPS, TOP_K, FF = 64, 8, 4, 8, 256
PER_GROUP = N_EXPERTS // N_GROUPS
ROUTED_SCALE = 2.5
UNROLL = 4
PAIRS = UNROLL // 2
SLOTS = 64
ROUNDS = SEQ // SLOTS - 1
EXTRA = SEQ * TOP_K // SLOTS
MAX_BLOCKS = N_EXPERTS + EXTRA
BLOCK_COLS = MAX_BLOCKS + 2 * UNROLL
PARTS = 3
MOD_CHUNKS = 6 * D // CHUNK

COLS_1 = {"qa": 0, "ka": 512, "va": 1024, "ug": 2048, "ua": 1536, "qc": 2560, "kc": 3072, "vc": 3584, "gt": 4096}
MOD_COL_PARTS = [0, 1, 3, 4]
MOD_ROW_PARTS = [2, 5]

MLA_H, MLA_NOPE, MLA_ROPE, MLA_QK = 4, 64, 32, 96
MOBA_H, MOBA_HD, MOBA_ROT = 4, 64, 16
SG_G, GW = 4, 256
D_IN_2 = 3488
NAT = {"cq": 0, "ckv": 256, "kr": 384, "ga": 416, "su": 672, "sv": 928, "gc": 1184, "mq": 1440, "mk": 1696,
       "mv": 1952, "gd": 2208}
NAT_COLS = 2464
CHUNKS_2 = [("t0", 672, 512, None), ("t1", 1184, 512, None), ("n0", 0, 512, 0), ("n1", 512, 160, 512),
            ("n2", 1696, 512, 672), ("n3", 2208, 512, 1184), ("n4", 2720, 512, 1696), ("n5", 3232, 256, 2208)]
ROPES = [(0, 32, 0), (32, 16, 1), (48, 8, 1)]
N_FREQ = 56


class Signal:

    def __init__(self, sem, per_layer=1, credit=0):
        self.sem, self.n, self.credit = sem, per_layer, credit

    def at(self, layer, k=1):
        return layer * self.n + (self.credit + k)


class Use:

    def __init__(self, tile, full, free, k_full, k_free):
        self.tile, self._full, self._free, self.k_full, self.k_free = tile, full, free, k_full, k_free
        self.full, self.free = full.sem, free.sem

    def free_at(self, layer):
        return self._free.at(layer, self.k_free)

    def consumed_at(self, layer):
        return self._free.at(layer, self.k_free + 1)

    def full_at(self, layer):
        return self._full.at(layer, self.k_full + 1)

    def full_before(self, layer):
        return self._full.at(layer, self.k_full + 1 - self._full.n)


class Chunk:

    def __init__(self, tile, filled, cum):
        self.tile, self._filled, self.cum, self.filled = tile, filled, cum, filled.sem

    def filled_at(self, layer):
        return self._filled.at(layer, self.cum)


def bank_plan(names, psum, sem, tag):
    fulls, frees = [0] * BANKS, [0] * BANKS
    places = []
    for i, name in enumerate(names):
        b = i % BANKS
        key = name if isinstance(name, str) else name[0]
        places.append((name, b, fulls[b], frees[b]))
        if not key.startswith("-"):
            frees[b] += 1
            if not key.startswith("="):
                fulls[b] += 1
    full = [Signal(sem(f"bank{b}_full_{tag}"), fulls[b], fulls[b]) for b in range(BANKS)]
    free = [Signal(sem(f"bank{b}_free_{tag}"), frees[b], 1) for b in range(BANKS)]
    uses = {name: Use(psum[b], full[b], free[b], kf, ke) for name, b, kf, ke in places}
    return uses, full, free


def broadcast(ap, axis, n):
    a = ap.unsqueeze(axis)
    shape = list(a.shape)
    shape[axis] = n
    return a.to_broadcast(shape)


def constants(nc, A, K):
    two_pi = 2 * math.pi
    c1 = 6.28125
    c2 = float(np.float32(round((two_pi - c1) * 2 ** 21) / 2 ** 21))
    c3 = two_pi - c1 - c2
    magic = 1.5 * 2 ** 23
    pi_in = 3.1415925
    with ExitStack() as ctx:
        def sb(name, shape, dt=F32):
            return ctx.enter_context(nc.sbuf_tensor(name, shape, dt))

        def sem(name):
            return ctx.enter_context(nc.semaphore(name))

        pos_i = sb("pos_i", [P, 2, T], I32)
        pos_f = sb("pos_f", [P, 2, T])
        inv = sb("inv", [P, N_FREQ])
        ang = sb("ang", [P, T, N_FREQ])
        turns = sb("turns", [P, T, N_FREQ])
        red = sb("red", [P, T, N_FREQ])
        wrap = sb("wrap", [P, T, N_FREQ])
        c_col = sb("c_col", [P, KT])
        c_sig = sb("c_sig", [P, KT])
        loaded, inv_ready, ang_ready, c_loaded, c_sig_ready, x_loaded = [
            sem(n) for n in ("loaded", "inv_ready", "ang_ready", "c_loaded", "c_sig_ready", "x_loaded")]
        ramp_i = sb("ramp_i", [P, SLOTS + 1], I32)
        part_i = sb("part_i", [P, 1], I32)
        block = ctx.enter_context(nc.Block())

        @block.sync
        def _(sp):
            for w, name in enumerate(("positions", "positions_2")):
                with nc.allow_non_contiguous_dma(reason="256 positions, one per partition"):
                    sp.dma_start(pos_i[:, w, :], A[name].rearrange("o (t p) -> p (o t)", p=P)).then_inc(loaded, 16)
            sp.dma_start(c_col[:], A["c"].rearrange("o (p k) -> p (o k)", k=KT)).then_inc(c_loaded, 16)
            for t in range(T):
                sp.dma_start(K.x[:, t, :], A["x"][0, t * P:(t + 1) * P, :]).then_inc(x_loaded, 16)
            sp.wait_ge(x_loaded, 16 * T)

        @block.gpsimd
        def _(pool):
            for (first, count, _), theta, dim in zip(ROPES, (10000.0, 500000.0, 500000.0), (64, 32, 16)):
                for i in range(count):
                    value = float(np.float32(theta) ** np.float32(-2.0 * i / dim))
                    last = nc.gpsimd.memset(inv[:, first + i:first + i + 1], value)
            last.then_inc(inv_ready, 1)
            nc.gpsimd.memset(K.eps[:], EPS)
            nc.gpsimd.memset(K.ones[:], 1.0)
            nc.gpsimd.memset(K.mean_conv[:], 1.0 / CONV_CH)
            for m in (K.ident, K.causal_neg, K.strict_neg):
                nc.gpsimd.memset(m[:], 0.0)
            for layer in range(DEPTH):
                li = 0.8 - 0.6 * math.exp(-0.3 * layer)
                nc.gpsimd.memset(K.lam_init[:, layer:layer + 1], li)
                nc.gpsimd.memset(K.lam_rest[:, layer:layer + 1], 1.0 - li)
            nc.gpsimd.memset(K.lower8[:], 1.0)
            nc.gpsimd.iota(K.table[:], pattern=[[1, BLOCK_COLS]], base=0, channel_multiplier=0)
            nc.gpsimd.memset(K.first_turn[:], 0)
            nc.gpsimd.memset(K.first_turn_f[:], 0.0)
            nc.gpsimd.iota(ramp_i[:], pattern=[[1, SLOTS + 1]], base=0, channel_multiplier=0)
            nc.gpsimd.iota(part_i[:], pattern=[[0, 1]], base=0, channel_multiplier=1)
            nc.gpsimd.memset(K.minus_slots[:], -float(SLOTS))
            for r in range(ROUNDS):
                nc.gpsimd.memset(K.full_rounds[:, r:r + 1], float((r + 1) * SLOTS))
            pool.drain()
            nc.gpsimd.tensor_copy(K.ramp[:], ramp_i[:])
            nc.gpsimd.tensor_copy(K.part[:], part_i[:])
            for g in range(2):
                nc.gpsimd.affine_select(out=K.strict_twice[:, g, :], in_=K.ones[:, 0:N_EXPERTS], compare_op=ALU.is_gt, fill=0.0,
                                        base=0, pattern=[[1, N_EXPERTS]], channel_multiplier=-1)
            square = [[-1, P]]
            nc.gpsimd.affine_select(out=K.ident[:], in_=K.ident[:], compare_op=ALU.not_equal, fill=1.0, base=0,
                                    pattern=square, channel_multiplier=1)
            nc.gpsimd.affine_select(out=K.causal_neg[:], in_=K.causal_neg[:], compare_op=ALU.is_ge, fill=NEG, base=0,
                                    pattern=square, channel_multiplier=1)
            nc.gpsimd.affine_select(out=K.strict_neg[:], in_=K.strict_neg[:], compare_op=ALU.is_gt, fill=NEG, base=0,
                                    pattern=[[1, P]], channel_multiplier=-1)
            nc.gpsimd.affine_select(out=K.strict_01[:], in_=K.ones[:], compare_op=ALU.is_gt, fill=0.0, base=0,
                                    pattern=[[1, P]], channel_multiplier=-1)
            nc.gpsimd.affine_select(out=K.tail[:], in_=K.ones[:], compare_op=ALU.is_ge, fill=0.0, base=0,
                                    pattern=square, channel_multiplier=1)
            nc.gpsimd.affine_select(out=K.head[:], in_=K.ones[:], compare_op=ALU.is_ge, fill=0.0, base=0,
                                    pattern=[[1, P]], channel_multiplier=-1)
            nc.gpsimd.affine_select(out=K.lower8[:], in_=K.lower8[:], compare_op=ALU.is_gt, fill=0.0, base=0,
                                    pattern=[[1, N_GROUPS], [-1, N_GROUPS]], channel_multiplier=0)
            pool.drain()

        @block.vector
        def _(dve):
            dve.wait_ge(loaded, 32)
            nc.vector.tensor_copy(pos_f[:], pos_i[:])
            dve.drain()
            dve.wait_ge(inv_ready, 1)
            for first, count, which in ROPES:
                for t in range(T):
                    nc.vector.tensor_scalar(ang[:, t, first:first + count], inv[:, first:first + count],
                                            pos_f[:, which, t:t + 1], None, ALU.mult)
            dve.drain()
            nc.vector.tensor_scalar(turns[:], ang[:], 1.0 / two_pi, magic, ALU.mult, ALU.add)
            dve.drain()
            nc.vector.tensor_scalar(turns[:], turns[:], magic, None, ALU.subtract)
            dve.drain()
            nc.vector.scalar_tensor_tensor(red[:], turns[:], -c1, ang[:], ALU.mult, ALU.add)
            dve.drain()
            nc.vector.scalar_tensor_tensor(ang[:], turns[:], -c2, red[:], ALU.mult, ALU.add)
            dve.drain()
            nc.vector.scalar_tensor_tensor(red[:], turns[:], -c3, ang[:], ALU.mult, ALU.add)
            dve.drain()
            nc.vector.tensor_scalar(ang[:], red[:], math.pi / 2, None, ALU.add)
            dve.drain()
            nc.vector.tensor_scalar(wrap[:], ang[:], math.pi, -two_pi, ALU.is_gt, ALU.mult)
            dve.drain()
            nc.vector.tensor_tensor(ang[:], ang[:], wrap[:], ALU.add)
            nc.vector.tensor_scalar(red[:], red[:], pi_in, -pi_in, ALU.min, ALU.max)
            dve.drain()
            nc.vector.tensor_scalar(ang[:], ang[:], pi_in, -pi_in, ALU.min, ALU.max)
            dve.drain().then_inc(ang_ready, 1)
            dve.wait_ge(c_sig_ready, 1)
            nc.vector.tensor_tensor(K.c_act[:], c_col[:], c_sig[:], ALU.mult)
            dve.drain()

        @block.scalar
        def _(act):
            act.wait_ge(c_loaded, 16)
            nc.scalar.activation(c_sig[:], c_col[:], ACT.Sigmoid).then_inc(c_sig_ready, 1)
            act.wait_ge(ang_ready, 1)
            nc.scalar.activation(K.sin[:], red[:], ACT.Sin)
            nc.scalar.activation(K.cos[:], ang[:], ACT.Sin)
            act.drain()


GROUPS_1 = (
    [("mod", c) for c in range(MOD_CHUNKS)] + ["vec"] + [("xT", 0, g) for g in range(4)]
    + [(n, i) for n in ("ug", "ua") for i in range(2)]
    + [(n, t) for n in ("qa", "ka") for t in range(T)]
    + [(n, i) for n in ("qc", "kc") for i in range(2)]
    + [(n, t) for n in ("va", "vc") for t in range(T)]
    + [("z0", par, i) for par in range(2) for i in range(2)] + [("z1", par) for par in range(2)]
    + [("suf", r, par) for r in range(3) for par in range(2)]
    + [("oc", i) for i in range(2)]
    + [("qkT", w, i) for w in range(2) for i in range(2)]
    + [("s1", m, i) for m in range(2) for i in range(2)] + [("s0", m) for m in range(2)]
    + ["cmean", "cvar"]
    + [("aT1", i) for i in range(2)] + ["aT0"] + [("oa", t) for t in range(T)] + [("oaT", i) for i in range(2)]
    + [(n, i, h, t) for i in range(3) for h in range(2) for t in range(T) for n in ("gt", "y")]
    + [("mT", g) for g in range(4)] + [("wo", h, t) for h in range(2) for t in range(T)]
    + [("xT", 1, g) for g in range(4)] + ["rt"]
    + [("=moe_y", t, h) for t in range(T) for h in range(2)] + ["-moe_h", "-moe_x"] + [("-moe_o", h) for h in range(2)]
)
GROUPS_1 += ["-pad"] * (-len(GROUPS_1) % BANKS)

CHUNKS_1 = (
    [(("mod", c), ("mod", c)) for c in range(MOD_CHUNKS)]
    + [(n, (n, 1)) for n in ("ug", "ua", "qa", "ka", "qc", "kc", "va", "vc")]
    + [x for i in range(3) for x in (((("p", i)), ("y", i, 1, 1)), (("gt", i, 0), ("gt", i, 0, 1)),
                                     (("gt", i, 1), ("gt", i, 1, 1)))]
    + [(("wo", h), ("wo", h, 1)) for h in range(2)] + [("shared", None)]
)
assert len(CHUNKS_1) % RING == 0 and N_EXPERTS % UNROLL == 0 and UNROLL == RING


def first_block(nc, A, K):
    ds = bass.ds
    with ExitStack() as ctx:
        def sb(name, shape, dt=F32):
            return ctx.enter_context(nc.sbuf_tensor(name, shape, dt))

        def sem(name):
            return ctx.enter_context(nc.semaphore(name))

        def signal(name, per_layer=1, credit=0):
            return Signal(sem(name), per_layer, credit)

        norm_g = sb("norm_g", [P, 2, KT])
        mod_b = sb("mod_b", [P, 4, KT])
        gain_qk = sb("gain_qk", [P, 2, DA_HD])
        lam4 = sb("lam4", [P, 4, DA_HD])
        subln = sb("subln", [P, 2 * DA_HD])
        dw_rows = sb("dw_rows", [TAPS * CT, P])
        ch_rows = sb("ch_rows", [3 * CT, P])
        proj_b_bias = sb("proj_b_bias", [P, D])
        w_rt = sb("w_rt", [P, KT, N_EXPERTS])
        rt_bias = sb("rt_bias", [P, N_EXPERTS])
        gate = sb("gate", [P, 2, D])
        col4 = sb("col4", [P, 4, 2, KT])
        mod_col = sb("mod_col", [P, 4, KT])
        vec_t = sb("vec_t", [P, TAPS * CT + 3 * CT])
        std = sb("std", [P, T])
        sq_sum = sb("sq_sum", [P, T])
        hpad = sb("hpad", [P, CT, TAPS - 1 + SEQ])
        conv = sb("conv", [P, CT, SEQ])
        conv_t = sb("conv_t", [P, CT, SEQ])
        conv_std = sb("conv_std", [P, SEQ])
        qk = sb("qk", [P, T, 2 * 512])
        slots2 = sb("slots2", [P, 2, 2, D])
        work = slots2[:].rearrange("p s f n -> p (s f) n")
        va, vc = (work[:, i].rearrange("p (t n) -> p t n", t=T) for i in range(2))
        qc_t, kc_t = (work[:, i].rearrange("p (c n) -> p c n", c=CT) for i in (2, 3))
        qa_t = sb("qa_t", [P, DA_HEADS, SEQ])
        ka_t = sb("ka_t", [P, DA_HEADS, SEQ])
        z = sb("z", [P, SB_HEADS, SEQ + P])
        sp_ = sb("sp_", [P, SB_HEADS, SEQ + P])
        qk_std = sb("qk_std", [P, T * 16])
        row16 = sb("row16", [P, 3, 16])
        lam_p = sb("lam_p", [P, 2, DA_HD])
        lam_s = sb("lam_s", [P, 2])
        lam_e = sb("lam_e", [P, 2])
        lam = sb("lam", [P, 1])
        gain_o = sb("gain_o", [P, 2 * DA_HD])
        oa_std = sb("oa_std", [P, T * DA_HEADS])
        sig_g = sb("sig_g", [P, 2, CHUNK])
        y_tmp = sb("y_tmp", [P, CHUNK])
        pick = y_tmp[:].rearrange("p (q k) -> p q k", k=KT)
        score = sb("score", [P, T, N_EXPERTS])
        biased = sb("biased", [P, T, N_EXPERTS])
        top = sb("top", [P, T, N_GROUPS, 8])
        g_score = sb("g_score", [P, T, N_GROUPS])
        g_cmp = sb("g_cmp", [P, T, N_GROUPS, N_GROUPS])
        g_eq = sb("g_eq", [P, T, N_GROUPS, N_GROUPS])
        g_rank = sb("g_rank", [P, T, N_GROUPS])
        g_neg = sb("g_neg", [P, T, N_GROUPS])
        top8 = sb("top8", [P, T, 8])
        rest = sb("rest", [P, T, N_EXPERTS])
        w_sum = sb("w_sum", [P, T])
        chosen = sb("chosen", [P, T, 2, N_EXPERTS])
        place_64 = sb("place_64", [P, T, 2, N_EXPERTS])
        place = sb("place", [P, T, 2, BLOCK_COLS])
        more = sb("more", [P, ROUNDS + 1])
        more_below = sb("more_below", [P, ROUNDS + 1])
        extra_at = sb("extra_at", [P, ROUNDS + 1])
        extra_hot = sb("extra_hot", [P, ROUNDS, EXTRA])
        extra_any = sb("extra_any", [P, EXTRA])
        extra_round = sb("extra_round", [P, EXTRA])
        turns_cmp = sb("turns_cmp", [P, EXTRA // UNROLL])
        turns_f = sb("turns_f", [P, 1])
        sig_h = sb("sig_h", [P, T, FF])
        act_h = sb("act_h", [P, T, FF])
        act_t = sb("act_t", [P, T, 2, P])

        z_flat = z[:].rearrange("p h n -> p (h n)")
        e1 = z_flat[:, 0:8 * SEQ].rearrange("p (h n) -> p h n", h=8)
        e0 = z_flat[:, 8 * SEQ:8 * SEQ + 8 * P].rearrange("p (h n) -> p h n", h=8)
        a_t = sp_[:].rearrange("p h n -> p (h n)")[:, 0:DA_HEADS * 3 * P].rearrange("p (h b n) -> p h b n", h=DA_HEADS, b=3)
        oa = qa_t[:].rearrange("p h n -> p (h n)").rearrange("p (t n) -> p t n", t=T)
        oa_t = ka_t
        yc_t = kc_t
        yb_t = conv
        merged = qk
        m_t = K.h_t
        qk_rot = K.xn[:].rearrange("p t (h n) -> p t h n", n=DA_HD)
        qk_heads = qk[:].rearrange("p t (h n) -> p t h n", n=DA_HD)
        cut, at = [], T * D
        for n in (2 * T * 2 * SLOTS, 2 * T * SLOTS // 2, FF // 2, FF // 2):
            cut.append(z_flat[:, at:at + n])
            at += n
        assert at <= SB_HEADS * (SEQ + P)
        spread = cut[0].rearrange("p (i t b s) -> p i t b s", i=2, t=T, b=2)
        pick_hot = cut[1].bitcast(BF16).rearrange("p (b t s) -> p b t s", b=2, t=T)
        sig_blk, act_blk = cut[2:4]
        x_blk = qa_t[:].rearrange("p h n -> p (h n)").rearrange("p (b k s) -> p b k s", b=2, k=KT)
        place_t = ka_t[:].rearrange("p h n -> p (h n)")[:, 0:T * P].rearrange("p (t n) -> p t n", t=T)
        turned = conv[:].rearrange("p c n -> p (c n)").rearrange("p (i b n) -> p i b n", i=2, b=2)
        o_blk = conv_t[:].rearrange("p c n -> p (c n)")
        w2_slots = [slots2[:, 0], slots2[:, 1], qk[:].rearrange("p t n -> p (t n)").rearrange("p (f n) -> p f n", f=2),
                    z_flat[:, 0:T * D].rearrange("p (f n) -> p f n", f=2)]
        xn_parts = sp_[:].rearrange("p h n -> p (h n)").bitcast(BF16).rearrange("p (t c k q) -> p t c k q", t=T, c=PARTS, k=KT)
        xn_rest = qk[:].rearrange("p t (k q) -> p t k q", k=KT)
        oa_heads = oa.rearrange("p t (h n) -> p (t h) n", n=2 * DA_HD)

        B, full, free = bank_plan(GROUPS_1, K.psum, sem, "1")
        filled = [Signal(sem(f"slot{s}_filled")) for s in range(RING)]
        C, loads, arrived = {}, [], [0] * RING
        for i, (name, reader) in enumerate(CHUNKS_1):
            s = i % RING
            arrived[s] += 32 if name in ("shared", "qa") else 16
            C[name] = Chunk(K.slots[s], filled[s], arrived[s])
            loads.append((name, s, CHUNKS_1[i - RING][1] if i >= RING else None, reader))
        for s in range(RING):
            filled[s].n = arrived[s]
        shared2_filled = Signal(sem("shared_w2_filled"), 16)
        w13_filled = [sem(f"slot{s}_w13_filled") for s in range(RING)]
        w2_filled = [sem(f"w2_slot{s}_filled") for s in range(RING)]

        N_PARAMS = 2 + len(MOD_COL_PARTS) + len(MOD_ROW_PARTS) + 2 + 4 + 1 + 1 + 3 + 1 + 1 + 1
        params = signal("params_loaded", 16 * N_PARAMS)
        x_mid, x_out = signal("x_after_mixer"), signal("x_after_layer", 1, 1)
        std_ready = [signal(f"x_std_ready{i}") for i in range(2)]
        xn_ready = [signal(f"xn_ready{i}") for i in range(2)]
        ht_ready = [signal(f"ht_ready{i}") for i in range(2)]
        vec_ready = signal("vec_t_ready")
        ug_ready = signal("ug_sigmoid_ready", 2)
        qk_ready, qkc_ready, v_ready = signal("qk_ready"), signal("qkc_t_ready"), signal("v_ready")
        qk_sq_ready, qk_std_ready, qk_rot_ready = signal("qk_sq_ready"), signal("qk_std_ready"), signal("qk_rot_ready")
        log_ready, sp_ready, d_ready, ac_ready = (signal("softplus_log_ready"), signal("softplus_ready"),
                                                  signal("stick_log_ready"), signal("stick_ready"))
        yct_ready, qkt_ready = signal("yc_t_ready"), signal("qk_t_ready")
        lam_s_ready, lam_e_ready = signal("lam_sums_ready"), signal("lam_exp_ready")
        max_ready, exp_ready, a_ready, at_ready = (signal("row_max_ready"), signal("exp_ready"), signal("a_ready"),
                                                   signal("a_t_ready"))
        oa_sq_ready, oa_std_ready, oa_ready, oat_ready = (signal("oa_sq_ready"), signal("oa_std_ready"),
                                                          signal("oa_ready"), signal("oa_t_ready"))
        conv_ready, conv_sq_ready, conv_std_ready = signal("conv_ready"), signal("conv_sq_ready"), signal("conv_std_ready")
        conv_ln_ready, conv_sig_ready, ybt_ready = signal("conv_ln_ready"), signal("conv_sig_ready"), signal("yb_t_ready")
        sig_ready, y_used = signal("gate_sig_ready", 12), signal("gate_sig_used", 12)
        merged_ready, mt_ready = signal("merged_ready"), signal("merged_t_ready")
        score_ready, chosen_ready = signal("score_ready"), signal("chosen_ready")
        sh_h_done, sh_sig_ready, sh_act_ready, sh_turned, sh_act_t_ready, sh_done = (
            signal(f"shared_{n}", T) for n in ("h_done", "sigmoid_ready", "act_ready", "act_turned", "act_t_ready", "w2_done"))
        count_done, more_ready, index_done = signal("count_done"), signal("more_ready"), signal("index_done")
        extra_ready, place_t_ready, list_done = signal("extra_ready"), signal("place_t_ready"), signal("list_done")
        table_ready, parts_ready = signal("table_ready"), signal("xn_parts_ready")
        hot_ready, gather_done, x_ready, h_done, sig_ready_blk, act_ready, turn_done, turned_ready = (
            sem(f"block_{n}") for n in ("hot_ready", "gather_done", "x_ready", "h_done", "sigmoid_ready", "act_ready",
                                        "turn_done", "turned_ready"))
        o_done, o_ready, added = (sem(f"pair_{n}") for n in ("o_done", "o_ready", "added"))
        wait_carrier = sem("wait_carrier")

        y_bank = [[B["=moe_y", t, h].tile for h in range(2)] for t in range(T)]
        h_bank, x_bank, o_bank, o_bank2 = (B[n].tile for n in ("-moe_h", "-moe_x", ("-moe_o", 0), ("-moe_o", 1)))
        o_banks = [o_bank, o_bank2]
        sh_bank = [h_bank, x_bank]
        sh_turn_bank = [o_bank2, x_bank]
        order = list(GROUPS_1)
        moe_before = [B[order[order.index(n) - BANKS]] for n in ("-moe_h", "-moe_x", ("-moe_o", 0), ("-moe_o", 1))]
        at_count, at_index, at_expert, at_place, at_weight = 128, 132, 136, 168, 256

        def block_count(eng, l):
            last_turn = eng.value_load(K.last_turn[0:1, ds(l, 1)], min_val=0, max_val=MAX_BLOCKS // UNROLL - 1)
            before = eng.value_load(K.first_turn[0:1, ds(l, 1)], min_val=0, max_val=DEPTH * MAX_BLOCKS // UNROLL)

            def nth(it, j):
                return (before + it) * UNROLL + (j + 1)

            def pairs(it, i):
                return (before + it) * PAIRS + (i + 1)

            return last_turn, nth, pairs

        block = ctx.enter_context(nc.Block())

        @block.sync
        def _(sp):
            for b in range(BANKS):
                sp.sem_inc(free[b].sem, 1)
                sp.sem_inc(full[b].sem, full[b].credit)
            sp.sem_inc(h_done, RING)
            sp.sem_inc(x_out.sem, 1)

            def expert13(l, e, s):
                for i, name in enumerate(("w1", "w3")):
                    sp.dma_start(K.slots[s][:, 4 * i:4 * i + 4, :].rearrange("p k n -> p (k n)"),
                                 A[name][ds(l, 1), ds(e, 1)].rearrange("a b (p k) n -> p (a b k n)", k=KT))\
                        .then_inc(w13_filled[s], 16)

            def expert2(l, e, s):
                sp.dma_start(w2_slots[s], A["w2"][ds(l, 1), ds(e, 1)].rearrange("a b (f p) n -> p (a b f) n", p=P))\
                    .then_inc(w2_filled[s], 16)

            with sp.Fori(0, DEPTH) as l:
                turns_before = sp.value_load(K.first_turn[0:1, ds(l, 1)], min_val=0, max_val=DEPTH * MAX_BLOCKS // UNROLL)
                for name, s, before, reader in loads:
                    if before is None:
                        sp.wait_ge(h_done, turns_before * UNROLL + (s + 1))
                    else:
                        sp.wait_ge(B[before].full, B[before].full_at(l))
                    slot = K.slots[s]
                    key = name[0] if isinstance(name, tuple) else name
                    if key == "mod":
                        src = A["w_mod"][ds(l, 1), :, name[1] * CHUNK:(name[1] + 1) * CHUNK].rearrange(
                            "a (p k) n -> p (a k) n", k=KT)
                    elif key in ("gt", "ug", "ua", "qa", "ka", "qc", "kc", "va", "vc"):
                        col = COLS_1[key] + (name[1] * D + name[2] * CHUNK if key == "gt" else 0)
                        src = A["w_in"][ds(l, 1), :, col:col + CHUNK].rearrange("a (p k) n -> p (a k) n", k=KT)
                    elif key == "p":
                        slot = slot.rearrange("p k n -> p (k n)").rearrange("p (k n) -> p k n", n=D)
                        src = A[("w_proj_a", "w_proj_b", "w_proj_c")[name[1]]][ds(l, 1)].rearrange(
                            "a (k p) n -> p (a k) n", p=P)
                    elif key == "wo":
                        src = A["w_out"][ds(l, 1), :, name[1] * CHUNK:(name[1] + 1) * CHUNK].rearrange(
                            "a (k p) n -> p (a k) n", p=P)
                    if key == "shared":
                        for i, w in enumerate(("ws1", "ws3")):
                            sp.dma_start(slot[:, 4 * i:4 * i + 4, :].rearrange("p k n -> p (k n)"),
                                         A[w][ds(l, 1)].rearrange("a (p k) n -> p (a k n)", k=KT))\
                                .then_inc(filled[s].sem, 16)
                    elif key == "qa":
                        for half in (slice(P // 2, P), slice(0, P // 2)):
                            sp.dma_start(slot[half], src[half]).then_inc(filled[s].sem, 16)
                    else:
                        sp.dma_start(slot, src).then_inc(filled[s].sem, 16)
                sp.wait_ge(B["y", 2, 1, 1].full, B["y", 2, 1, 1].full_at(l))
                sp.dma_start(slots2[:, 1].rearrange("p f n -> p (f n)"),
                             A["ws2"][ds(l, 1)].rearrange("a (p f) n -> p (a f n)", f=2)).then_inc(shared2_filled.sem, 16)
                for e in range(UNROLL):
                    before = loads[len(loads) - RING + e][3]
                    if before is None:
                        sp.wait_ge(sh_h_done.sem, sh_h_done.at(l, T))
                    else:
                        sp.wait_ge(B[before].full, B[before].full_at(l))
                    expert13(l, e, e)
                expert2(l, 0, 0)
                sp.wait_ge(sh_done.sem, sh_done.at(l, T))
                expert2(l, 1, 1)
                sp.wait_ge(parts_ready.sem, parts_ready.at(l))
                expert2(l, 2, 2)
                expert2(l, 3, 3)
                sp.wait_ge(table_ready.sem, table_ready.at(l))
                sp.sem_inc(wait_carrier, 1)
                last_turn, nth, pairs = block_count(sp, l)
                with sp.Fori(1, last_turn + 1) as it:
                    for j in range(UNROLL):
                        e = sp.value_load(K.table[0:1, ds(it * UNROLL + j, 1)], min_val=0, max_val=N_EXPERTS - 1)
                        sp.wait_ge(h_done, nth(it, j))
                        sp.sem_inc(wait_carrier, 1)
                        expert13(l, e, j)
                        sp.wait_ge(o_done, pairs(it, j // 2 - PAIRS))
                        sp.sem_inc(wait_carrier, 1)
                        expert2(l, e, j)

        @block.gpsimd
        def _(pool):
            with pool.Fori(0, DEPTH) as l:
                pool.wait_ge(x_out.sem, x_out.at(l, 0))
                one = ds(l, 1)

                def load(dst, src):
                    pool.dma_start(dst, src).then_inc(params.sem, 16)

                for i, name in enumerate(("norm_mix_g", "norm_ffn_g")):
                    load(norm_g[:, i, :], A[name][one].rearrange("a (p k) -> p (a k)", k=KT))
                for i, part in enumerate(MOD_COL_PARTS):
                    load(mod_b[:, i, :], A["b_mod"][one, part * D:(part + 1) * D].rearrange("a (p k) -> p (a k)", k=KT))
                for i, part in enumerate(MOD_ROW_PARTS):
                    load(gate[:, i, :], A["b_mod"][one, part * D:(part + 1) * D].to_broadcast([P, D]))
                for i, name in enumerate(("qn_g", "kn_g")):
                    load(gain_qk[:, i, :], A[name][one].to_broadcast([P, DA_HD]))
                for i, name in enumerate(("lam_q1", "lam_k1", "lam_q2", "lam_k2")):
                    load(lam4[:, i, :], A[name][one].to_broadcast([P, DA_HD]))
                load(subln[:], A["subln_g"][one].to_broadcast([P, 2 * DA_HD]))
                load(dw_rows[:], A["w_dw"][one].rearrange("a k (c p) -> (a k c) p", p=P))
                for i, name in enumerate(("b_dw", "conv_ln_g", "conv_ln_b")):
                    load(ch_rows[i * CT:(i + 1) * CT, :], A[name][one].rearrange("a (c p) -> (a c) p", p=P))
                load(proj_b_bias[:], A["b_proj_b"][one].to_broadcast([P, D]))
                load(w_rt[:], A["w_router"][one].rearrange("a (p k) n -> p (a k) n", k=KT))
                load(rt_bias[:], A["b_router"][one].to_broadcast([P, N_EXPERTS]))
                pool.wait_ge(xn_ready[1].sem, xn_ready[1].at(l))
                pool.sem_inc(wait_carrier, 1)
                by_k = K.xn[:].rearrange("p t (q k) -> p t k q", k=KT)
                for c in range(PARTS):
                    for t in range(T):
                        nc.gpsimd.tensor_copy(xn_parts[:, t, c], by_k[:, t] if c == 0 else xn_rest[:, t])
                    pool.drain()
                    if c < PARTS - 1:
                        for t in range(T):
                            nc.gpsimd.tensor_tensor(xn_rest[:, t], by_k[:, t] if c == 0 else xn_rest[:, t], xn_parts[:, t, c],
                                                    ALU.subtract)
                        pool.drain()
                pool.drain().then_inc(parts_ready.sem, 1)

        @block.tensor
        def _(pe):
            def begin(name, l):
                pe.wait_ge(B[name].free, B[name].free_at(l))
                return B[name].tile

            def chunk(name, l):
                pe.wait_ge(C[name].filled, C[name].filled_at(l))
                return C[name].tile

            def rows(name, l, w, t, stationary, cols=CHUNK):
                bank = begin(name, l)
                for k in range(KT):
                    mm = nc.tensor.matmul(bank[:, 0:cols], stationary[:, k, t * P:(t + 1) * P], w[:, k, 0:cols],
                                          start=(k == 0), stop=(k == KT - 1))
                mm.then_inc(B[name].full, 1)

            def columns(name, l, w, i):
                bank = begin(name, l)
                for j in range(2):
                    c = 2 * i + j
                    for k in range(KT):
                        mm = nc.tensor.matmul(bank[:, j * SEQ:(j + 1) * SEQ], w[:, k, c * P:(c + 1) * P], K.h_t[:, k, :],
                                              start=(k == 0), stop=(k == KT - 1))
                mm.then_inc(B[name].full, 1)

            def norm_turn(i, l):
                pe.wait_ge(xn_ready[i].sem, xn_ready[i].at(l))
                for g in range(4):
                    bank = begin(("xT", i, g), l)
                    for j in range(2):
                        for t in range(T):
                            mm = nc.tensor.transpose(bank[:, j * SEQ + t * P:j * SEQ + (t + 1) * P],
                                                     K.xn[:, t, 2 * g + j::KT], K.ident[:])
                    mm.then_inc(B["xT", i, g].full, 1)

            with pe.Fori(0, DEPTH) as l:
                for c in range(MOD_CHUNKS):
                    w = chunk(("mod", c), l)
                    bank = begin(("mod", c), l)
                    for k in range(KT):
                        mm = nc.tensor.matmul(bank[:], K.c_act[:, k:k + 1].to_broadcast([P, P]), w[:, k, :],
                                              start=(k == 0), stop=(k == KT - 1))
                    mm.then_inc(B["mod", c].full, 1)
                pe.wait_ge(params.sem, params.at(l, params.n))
                bank = begin("vec", l)
                nc.tensor.transpose(bank[:, 0:TAPS * CT], dw_rows[:], K.ident[0:TAPS * CT, 0:TAPS * CT])
                nc.tensor.transpose(bank[:, TAPS * CT:(TAPS + 3) * CT], ch_rows[:], K.ident[0:3 * CT, 0:3 * CT])\
                    .then_inc(B["vec"].full, 1)
                norm_turn(0, l)
                pe.wait_ge(ht_ready[0].sem, ht_ready[0].at(l))
                for name in ("ug", "ua"):
                    w = chunk(name, l)
                    for i in range(2):
                        columns((name, i), l, w, i)
                for name in ("qa", "ka"):
                    w = chunk(name, l)
                    for t in range(T):
                        rows((name, t), l, w, t, K.h_t)
                for name in ("qc", "kc"):
                    w = chunk(name, l)
                    for i in range(2):
                        columns((name, i), l, w, i)
                for name in ("va", "vc"):
                    w = chunk(name, l)
                    for t in range(T):
                        rows((name, t), l, w, t, K.h_t)

                pe.wait_ge(qkc_ready.sem, qkc_ready.at(l))
                for par in range(2):
                    part = slice(64 * par, 64 * par + 64)
                    for i in range(2):
                        bank = begin(("z0", par, i), l)
                        for j in range(2):
                            c = 2 * i + j
                            mm = nc.tensor.matmul(bank[:, j * SEQ:(j + 1) * SEQ], kc_t[part, c, 0:P], qc_t[part, c, :],
                                                  start=True, stop=True)
                        mm.then_inc(B["z0", par, i].full, 1)
                for par in range(2):
                    part = slice(64 * par, 64 * par + 64)
                    bank = begin(("z1", par), l)
                    for c in range(CT):
                        mm = nc.tensor.matmul(bank[:, c * P:(c + 1) * P], kc_t[part, c, P:SEQ], qc_t[part, c, P:SEQ],
                                              start=True, stop=True)
                    mm.then_inc(B["z1", par].full, 1)
                pe.wait_ge(sp_ready.sem, sp_ready.at(l))
                for r, parts in enumerate(([(K.tail, 0)], [(K.tail, P), (K.ones, 2 * P)], [(K.tail, 2 * P)])):
                    for par in range(2):
                        bank = begin(("suf", r, par), l)
                        for n, (m, c) in enumerate(parts):
                            mm = nc.tensor.matmul(bank[:], m[:], sp_[:, 4 * par:4 * par + 4, c:c + P],
                                                  start=(n == 0), stop=(n == len(parts) - 1))
                        mm.then_inc(B["suf", r, par].full, 1)
                pe.wait_ge(v_ready.sem, v_ready.at(l))
                pe.wait_ge(ac_ready.sem, ac_ready.at(l))
                for i in range(2):
                    bank = begin(("oc", i), l)
                    for j in range(2):
                        for par in range(2):
                            c = 2 * i + j
                            col = (2 * c + par) * SB_HD
                            out = bank[64 * par:64 * par + 64, j * SEQ:(j + 1) * SEQ]
                            nc.tensor.matmul(out, vc[:, 0, col:col + SB_HD], z[:, 4 * par + c, 0:SEQ],
                                             start=True, stop=False, skip_group_check=True)
                            mm = nc.tensor.matmul(out[:, P:SEQ], vc[:, 1, col:col + SB_HD], z[:, 4 * par + c, SEQ:SEQ + P],
                                                  start=False, stop=True, skip_group_check=True)
                    mm.then_inc(B["oc", i].full, 1)

                pe.wait_ge(qk_rot_ready.sem, qk_rot_ready.at(l))
                for w in range(2):
                    for i in range(2):
                        bank = begin(("qkT", w, i), l)
                        for j in range(2):
                            for t in range(T):
                                col = w * 512 + (2 * i + j) * P
                                mm = nc.tensor.transpose(bank[:, j * SEQ + t * P:j * SEQ + (t + 1) * P],
                                                         K.xn[:, t, col:col + P], K.ident[:])
                        mm.then_inc(B["qkT", w, i].full, 1)
                pe.wait_ge(qkt_ready.sem, qkt_ready.at(l))
                for m in range(2):
                    part = slice(64 * m, 64 * m + 64)
                    for i in range(2):
                        bank = begin(("s1", m, i), l)
                        for j in range(2):
                            mm = nc.tensor.matmul(bank[:, j * SEQ:(j + 1) * SEQ], qa_t[part, 2 * i + j, P:SEQ],
                                                  ka_t[part, 2 * i + j, :], start=True, stop=True)
                        mm.then_inc(B["s1", m, i].full, 1)
                for m in range(2):
                    part = slice(64 * m, 64 * m + 64)
                    bank = begin(("s0", m), l)
                    for h in range(DA_HEADS):
                        mm = nc.tensor.matmul(bank[:, h * P:(h + 1) * P], qa_t[part, h, 0:P], ka_t[part, h, 0:P],
                                              start=True, stop=True)
                    mm.then_inc(B["s0", m].full, 1)
                pe.wait_ge(conv_ready.sem, conv_ready.at(l))
                bank = begin("cmean", l)
                for c in range(CT):
                    mm = nc.tensor.matmul(bank[:, 0:SEQ], K.mean_conv[:], conv[:, c, :], start=(c == 0), stop=(c == CT - 1))
                mm.then_inc(B["cmean"].full, 1)
                pe.wait_ge(conv_sq_ready.sem, conv_sq_ready.at(l))
                bank = begin("cvar", l)
                for c in range(CT):
                    mm = nc.tensor.matmul(bank[:, 0:SEQ], K.mean_conv[:], conv_t[:, c, :], start=(c == 0), stop=(c == CT - 1))
                mm.then_inc(B["cvar"].full, 1)
                pe.wait_ge(a_ready.sem, a_ready.at(l))
                for i in range(2):
                    bank = begin(("aT1", i), l)
                    for j in range(2):
                        for b in range(2):
                            mm = nc.tensor.transpose(bank[:, (2 * j + b) * P:(2 * j + b + 1) * P],
                                                     e1[:, 2 * i + j, b * P:(b + 1) * P], K.ident[:])
                    mm.then_inc(B["aT1", i].full, 1)
                bank = begin("aT0", l)
                for h in range(DA_HEADS):
                    mm = nc.tensor.transpose(bank[:, h * P:(h + 1) * P], e0[:, h, :], K.ident[:])
                mm.then_inc(B["aT0"].full, 1)
                pe.wait_ge(at_ready.sem, at_ready.at(l))
                for t in range(T):
                    bank = begin(("oa", t), l)
                    for h in range(DA_HEADS):
                        col = slice(h * P, (h + 1) * P)
                        if t == 0:
                            mm = nc.tensor.matmul(bank[:, col], a_t[:, h, 0, :], va[:, 0, col], start=True, stop=True)
                        else:
                            nc.tensor.matmul(bank[:, col], a_t[:, h, 1, :], va[:, 0, col], start=True, stop=False)
                            mm = nc.tensor.matmul(bank[:, col], a_t[:, h, 2, :], va[:, 1, col], start=False, stop=True)
                    mm.then_inc(B["oa", t].full, 1)
                pe.wait_ge(oa_ready.sem, oa_ready.at(l))
                for i in range(2):
                    bank = begin(("oaT", i), l)
                    for j in range(2):
                        for t in range(T):
                            mm = nc.tensor.transpose(bank[:, j * SEQ + t * P:j * SEQ + (t + 1) * P],
                                                     oa[:, t, (2 * i + j) * P:(2 * i + j + 1) * P], K.ident[:])
                    mm.then_inc(B["oaT", i].full, 1)

                for i, (feat, ready) in enumerate(((oa_t, oat_ready), (yb_t, ybt_ready), (yc_t, yct_ready))):
                    pe.wait_ge(ready.sem, ready.at(l))
                    w = chunk(("p", i), l).rearrange("p k n -> p (k n)").rearrange("p (k n) -> p k n", n=D)
                    for h in range(2):
                        wg = chunk(("gt", i, h), l)
                        for t in range(T):
                            rows(("gt", i, h, t), l, wg, t, K.h_t)
                            bank = begin(("y", i, h, t), l)
                            for k in range(4):
                                mm = nc.tensor.matmul(bank[:], feat[:, k, t * P:(t + 1) * P],
                                                      w[:, k, h * CHUNK:(h + 1) * CHUNK], start=(k == 0), stop=(k == 3))
                            mm.then_inc(B["y", i, h, t].full, 1)
                pe.wait_ge(merged_ready.sem, merged_ready.at(l))
                for g in range(4):
                    bank = begin(("mT", g), l)
                    for j in range(2):
                        for t in range(T):
                            k = 2 * g + j
                            mm = nc.tensor.transpose(bank[:, j * SEQ + t * P:j * SEQ + (t + 1) * P],
                                                     merged[:, t, k * P:(k + 1) * P], K.ident[:])
                    mm.then_inc(B["mT", g].full, 1)
                pe.wait_ge(mt_ready.sem, mt_ready.at(l))
                for h in range(2):
                    w = chunk(("wo", h), l)
                    for t in range(T):
                        rows(("wo", h, t), l, w, t, m_t)

                norm_turn(1, l)
                pe.wait_ge(ht_ready[1].sem, ht_ready[1].at(l))
                bank = begin("rt", l)
                for t in range(T):
                    for k in range(KT):
                        mm = nc.tensor.matmul(bank[:, t * N_EXPERTS:(t + 1) * N_EXPERTS], K.h_t[:, k, t * P:(t + 1) * P],
                                              w_rt[:, k, :], start=(k == 0), stop=(k == KT - 1))
                mm.then_inc(B["rt"].full, 1)

                def shared_h(t, w):
                    for k in range(KT):
                        mm = nc.tensor.matmul(sh_bank[t][:], K.h_t[:, k, t * P:(t + 1) * P], w[:, :, k, :],
                                              start=(k == 0), stop=(k == KT - 1))
                    mm.then_inc(sh_h_done.sem, 1)

                def shared_turn(t):
                    pe.wait_ge(sh_act_ready.sem, sh_act_ready.at(l, t + 1))
                    for f in range(2):
                        mm = nc.tensor.transpose(sh_turn_bank[t][:, f * P:(f + 1) * P], act_h[:, t, f::2], K.ident[:])
                    mm.then_inc(sh_turned.sem, 1)

                def shared_w2(t, w):
                    pe.wait_ge(sh_act_t_ready.sem, sh_act_t_ready.at(l, t + 1))
                    for f in range(2):
                        for h in range(2):
                            mm = nc.tensor.matmul(y_bank[t][h][:], act_t[:, t, f, :], w[:, f, h * CHUNK:(h + 1) * CHUNK],
                                                  start=(f == 0), stop=(f == 1), skip_group_check=True)
                    mm.then_inc(sh_done.sem, 1)

                def w13(s):
                    return K.slots[s].rearrange("p (i k) n -> p i (k n)", i=2).rearrange("p i (k n) -> p i k n", n=FF)

                for b in list(B["=moe_y", t, h] for t in range(T) for h in range(2)):
                    pe.wait_ge(b.free, b.free_at(l))
                for b in moe_before:
                    pe.wait_ge(b.free, b.consumed_at(l))
                pe.wait_ge(C["shared"].filled, C["shared"].filled_at(l))
                for t in range(T):
                    shared_h(t, w13(len(CHUNKS_1) % RING - 1))
                pe.wait_ge(chosen_ready.sem, chosen_ready.at(l))
                nc.tensor.matmul(o_bank[:, 0:N_EXPERTS], K.strict_01[:], chosen[:, 0, 0, :], start=True, stop=True)
                nc.tensor.matmul(o_bank[:, N_EXPERTS:2 * N_EXPERTS], K.strict_01[:], chosen[:, 1, 0, :], start=True, stop=False)
                nc.tensor.matmul(o_bank[:, N_EXPERTS:2 * N_EXPERTS], K.ones[:], chosen[:, 0, 0, :], start=False, stop=True)
                for t in range(T):
                    mm = nc.tensor.matmul(o_bank[:, at_count:at_count + 4], chosen[:, t].rearrange("p g e -> p (g e)"), K.ones[:, 0:4],
                                          start=(t == 0), stop=(t == T - 1))
                mm.then_inc(count_done.sem, 1)
                for t in range(T):
                    shared_turn(t)
                pe.wait_ge(more_ready.sem, more_ready.at(l))
                e64 = slice(0, N_EXPERTS)
                index = o_bank[:, at_index:at_index + ROUNDS + 1]
                nc.tensor.matmul(index, K.strict_twice[e64].rearrange("p g e -> p (g e)"), more[e64, :], start=True, stop=False)
                nc.tensor.matmul(index, K.ones[e64, :], more_below[e64, :], start=False, stop=True)
                for t in range(T):
                    mm = nc.tensor.transpose(h_bank[:, t * P:(t + 1) * P], place_64[:, t].rearrange("p i e -> p (i e)"),
                                             K.ident[:])
                mm.then_inc(index_done.sem, 1)
                pe.wait_ge(shared2_filled.sem, shared2_filled.at(l, 16))
                shared_w2(0, slots2[:, 1])
                pe.wait_ge(extra_ready.sem, extra_ready.at(l))
                pe.wait_ge(place_t_ready.sem, place_t_ready.at(l))
                nc.tensor.matmul(o_bank[:, at_expert:at_expert + EXTRA], K.part[e64, 0:1].to_broadcast([N_EXPERTS, P]),
                                 extra_any[e64, :], start=True, stop=True)
                for t in range(T):
                    out = o_bank[:, at_place + t * EXTRA:at_place + (t + 1) * EXTRA]
                    nc.tensor.matmul(out, place_t[e64, t, :], extra_any[e64, :], start=True, stop=False)
                    nc.tensor.matmul(out, K.minus_slots[e64, :], extra_round[e64, :], start=False, stop=True)
                for t in range(T):
                    mm = nc.tensor.matmul(h_bank[:, at_weight + t * EXTRA:at_weight + (t + 1) * EXTRA],
                                          place_t[N_EXPERTS:P, t, :], extra_any[N_EXPERTS:P, :], start=True, stop=True)
                mm.then_inc(list_done.sem, 1)
                shared_w2(1, slots2[:, 1])

                pe.wait_ge(table_ready.sem, table_ready.at(l))
                pe.wait_ge(parts_ready.sem, parts_ready.at(l))
                last_turn, nth, pairs = block_count(pe, l)

                def gather(it, j):
                    pe.wait_ge(hot_ready, nth(it, j))
                    for k in range(KT):
                        for t in range(T):
                            for c in range(PARTS):
                                mm = nc.tensor.matmul(x_bank[:, k * SLOTS:(k + 1) * SLOTS], xn_parts[:, t, c, k, :],
                                                      pick_hot[:, j % 2, t, :], start=(t == 0 and c == 0),
                                                      stop=(t == T - 1 and c == PARTS - 1))
                    mm.then_inc(gather_done, 1)

                def block_h(it, j):
                    pe.wait_ge(x_ready, nth(it, j))
                    pe.wait_ge(w13_filled[j], nth(it, -1) * (32 // UNROLL) + 32)
                    for k in range(KT):
                        for g in range(2):
                            mm = nc.tensor.matmul(h_bank[g * SLOTS:(g + 1) * SLOTS, 0:FF], x_blk[:, j % 2, k, :],
                                                  w13(j)[:, :, k, g * (FF // 2):(g + 1) * (FF // 2)],
                                                  start=(k == 0), stop=(k == KT - 1), skip_group_check=True)
                    mm.then_inc(h_done, 1)

                def block_turn(it, j):
                    pe.wait_ge(act_ready, nth(it, j))
                    nc.tensor.transpose(h_bank[:, FF:FF + P], act_blk, K.ident[:])
                    nc.tensor.transpose(h_bank[:, FF + P:FF + 2 * P],
                                        spread[:, j // 2, j % 2].rearrange("p b s -> p (b s)"), K.ident[:]).then_inc(turn_done, 1)

                def pair_w2(it, i):
                    for b in range(2):
                        pe.wait_ge(w2_filled[2 * i + b], nth(it, -1) * (16 // UNROLL) + 16)
                    for f in range(2):
                        for h in range(2):
                            for b in range(2):
                                mm = nc.tensor.matmul(o_banks[h][b * SLOTS:(b + 1) * SLOTS, :],
                                                      turned[:, i, b, f * SLOTS:(f + 1) * SLOTS],
                                                      w2_slots[2 * i + b][:, f, h * CHUNK:(h + 1) * CHUNK],
                                                      start=(f == 0), stop=(f == 1), skip_group_check=True)
                    mm.then_inc(o_done, 1)

                def pair_add(it, i, t):
                    pe.wait_ge(o_ready, pairs(it, i))
                    for h in range(2):
                        mm = nc.tensor.matmul(y_bank[t][h][:], turned[:, i % PAIRS, t, P:2 * P], o_blk[:, h * CHUNK:(h + 1) * CHUNK],
                                              start=False, stop=True, skip_group_check=True)
                    if t == T - 1:
                        mm.then_inc(added, 1)

                def turn(it, first=False, last=False):
                    for i in range(PAIRS):
                        a, b = 2 * i, 2 * i + 1
                        block_h(it, a)
                        gather(it, b)
                        block_turn(it, a)
                        if not (first and i == 0):
                            pair_add(it, i - 1, 0)
                        pe.wait_ge(turned_ready, nth(it, a))
                        block_h(it, b)
                        if not (first and i == 0):
                            pair_add(it, i - 1, 1)
                        block_turn(it, b)
                        if not (last and i == PAIRS - 1):
                            gather(it, b + 1)
                        pe.wait_ge(turned_ready, nth(it, b))
                        pair_w2(it, i)

                gather(0, 0)
                turn(0, first=True)
                with pe.Fori(1, last_turn) as it:
                    turn(it)
                turn(last_turn, last=True)
                for t in range(T):
                    pair_add(last_turn, PAIRS - 1, t)

        @block.scalar
        def _(act):
            def full_of(name, l):
                act.wait_ge(B[name].full, B[name].full_at(l))
                return B[name].tile

            def row_norm(i, l):
                if i == 0:
                    act.wait_ge(x_out.sem, x_out.at(l, 0))
                else:
                    act.wait_ge(x_mid.sem, x_mid.at(l))
                for t in range(T):
                    nc.scalar.activation(K.xn[:, t, :], K.x[:, t, :], ACT.Square, accum_out=sq_sum[:, t:t + 1])
                act.drain()
                nc.scalar.activation(std[:], sq_sum[:], ACT.Sqrt, scale=1.0 / D, bias=K.eps[:]).then_inc(std_ready[i].sem, 1)

            def copy_out(name, l, dst, src, last=None, scale=1.0):
                nc.scalar.activation(dst, src, ACT.Copy, scale=scale).then_inc(B[name].free, 1)

            with act.Fori(0, DEPTH) as l:
                row_norm(0, l)
                bank = full_of("vec", l)
                copy_out("vec", l, vec_t[:], bank[:, 0:(TAPS + 3) * CT])
                act.drain().then_inc(vec_ready.sem, 1)
                for i in range(2):
                    bank = full_of(("ug", i), l)
                    nc.scalar.activation(conv_t[:, 2 * i:2 * i + 2, :], bank[:].rearrange("p (c n) -> p c n", c=2),
                                         ACT.Sigmoid).then_inc(B["ug", i].free, 1)
                act.drain().then_inc(ug_ready.sem, 2)
                for w, name in enumerate(("qa", "ka")):
                    for t in range(T):
                        bank = full_of((name, t), l)
                        copy_out((name, t), l, qk[:, t, w * 512:(w + 1) * 512], bank[:])
                act.drain().then_inc(qk_ready.sem, 1)
                for name, dst, scale in (("qc", qc_t, SB_HD ** -0.5), ("kc", kc_t, 1.0)):
                    for i in range(2):
                        bank = full_of((name, i), l)
                        copy_out((name, i), l, dst[:, 2 * i:2 * i + 2, :], bank[:].rearrange("p (c n) -> p c n", c=2),
                                 scale=scale)
                act.drain().then_inc(qkc_ready.sem, 1)
                for name, dst in (("va", va), ("vc", vc)):
                    for t in range(T):
                        bank = full_of((name, t), l)
                        copy_out((name, t), l, dst[:, t, :], bank[:])
                act.drain().then_inc(v_ready.sem, 1)
                act.wait_ge(qk_sq_ready.sem, qk_sq_ready.at(l))
                nc.scalar.activation(qk_std[:], qk_std[:], ACT.Sqrt, scale=1.0 / DA_HD, bias=K.eps[:])\
                    .then_inc(qk_std_ready.sem, 1)
                act.wait_ge(qk_rot_ready.sem, qk_rot_ready.at(l))
                for name, h0, nh, c0, n in ([(("z0", par, i), 4 * par + 2 * i, 2, 0, SEQ) for par in range(2) for i in range(2)]
                                            + [(("z1", par), 4 * par, 4, SEQ, P) for par in range(2)]):
                    src = full_of(name, l)[:].rearrange("p (h n) -> p h n", h=nh)
                    nc.scalar.activation(sp_[:, h0:h0 + nh, c0:c0 + n], src, ACT.Abs)
                    copy_out(name, l, z[:, h0:h0 + nh, c0:c0 + n], src)
                act.drain()
                nc.scalar.activation(sp_[:], sp_[:], ACT.Exp, scale=-1.0)
                act.drain()
                nc.scalar.activation(sp_[:], sp_[:], ACT.Ln, bias=1.0).then_inc(log_ready.sem, 1)
                act.wait_ge(d_ready.sem, d_ready.at(l))
                nc.scalar.activation(z[:], z[:], ACT.Exp).then_inc(ac_ready.sem, 1)
                for i in range(2):
                    bank = full_of(("oc", i), l)
                    copy_out(("oc", i), l, yc_t[:, 2 * i:2 * i + 2, :], bank[:].rearrange("p (c n) -> p c n", c=2))
                act.drain().then_inc(yct_ready.sem, 1)
                for w, dst in enumerate((qa_t, ka_t)):
                    for i in range(2):
                        bank = full_of(("qkT", w, i), l)
                        copy_out(("qkT", w, i), l, dst[:, 2 * i:2 * i + 2, :], bank[:].rearrange("p (c n) -> p c n", c=2))
                act.drain().then_inc(qkt_ready.sem, 1)
                act.wait_ge(lam_s_ready.sem, lam_s_ready.at(l))
                nc.scalar.activation(lam_e[:], lam_s[:], ACT.Exp).then_inc(lam_e_ready.sem, 1)
                act.wait_ge(max_ready.sem, max_ready.at(l))
                for r in range(16):
                    e = e1[:, r, :] if r < 8 else e0[:, r - 8, :]
                    nc.scalar.activation(e, e, ACT.Exp, bias=row16[:, 0, r:r + 1], scale=DA_HD ** -0.5,
                                         accum_out=row16[:, 1, r:r + 1])
                act.drain().then_inc(exp_ready.sem, 1)
                src = full_of("cvar", l)
                nc.scalar.activation(conv_std[:], src[:, 0:SEQ], ACT.Sqrt, bias=K.eps[:]).then_inc(B["cvar"].free, 1)
                act.drain().then_inc(conv_std_ready.sem, 1)
                for i in range(2):
                    bank = full_of(("aT1", i), l)
                    copy_out(("aT1", i), l, a_t[:, 2 * i:2 * i + 2, 1:3, :],
                             bank[:].rearrange("p (h b n) -> p h b n", h=2, b=2))
                bank = full_of("aT0", l)
                copy_out("aT0", l, a_t[:, :, 0, :], bank[:].rearrange("p (h n) -> p h n", h=DA_HEADS))
                act.drain().then_inc(at_ready.sem, 1)
                act.wait_ge(oa_sq_ready.sem, oa_sq_ready.at(l))
                nc.scalar.activation(oa_std[:], oa_std[:], ACT.Sqrt, scale=1.0 / (2 * DA_HD), bias=K.eps[:])\
                    .then_inc(oa_std_ready.sem, 1)
                act.wait_ge(conv_ln_ready.sem, conv_ln_ready.at(l))
                nc.scalar.activation(conv_t[:], conv[:], ACT.Sigmoid).then_inc(conv_sig_ready.sem, 1)
                for i in range(2):
                    bank = full_of(("oaT", i), l)
                    copy_out(("oaT", i), l, oa_t[:, 2 * i:2 * i + 2, :], bank[:].rearrange("p (c n) -> p c n", c=2))
                act.drain().then_inc(oat_ready.sem, 1)
                n = 0
                for i in range(3):
                    for h in range(2):
                        for t in range(T):
                            bank = full_of(("gt", i, h, t), l)
                            if n >= 2:
                                act.wait_ge(y_used.sem, y_used.at(l, n - 1))
                            nc.scalar.activation(sig_g[:, n % 2, :], bank[:], ACT.Sigmoid).then_inc(B["gt", i, h, t].free, 1)
                            act.drain().then_inc(sig_ready.sem, 1)
                            n += 1
                for g in range(4):
                    bank = full_of(("mT", g), l)
                    copy_out(("mT", g), l, m_t[:, 2 * g:2 * g + 2, :], bank[:].rearrange("p (c n) -> p c n", c=2))
                act.drain().then_inc(mt_ready.sem, 1)
                row_norm(1, l)
                bank = full_of("rt", l)
                nc.scalar.activation(score[:], bank[:, 0:T * N_EXPERTS].rearrange("p (t n) -> p t n", t=T), ACT.Sigmoid)\
                    .then_inc(B["rt"].free, 1)
                act.drain().then_inc(score_ready.sem, 1)

                for t in range(T):
                    act.wait_ge(sh_h_done.sem, sh_h_done.at(l, t + 1))
                    nc.scalar.activation(sig_h[:, t, :], sh_bank[t][:, 0:FF], ACT.Sigmoid).then_inc(sh_sig_ready.sem, 1)
                for t in range(T):
                    act.wait_ge(sh_turned.sem, sh_turned.at(l, t + 1))
                    nc.scalar.activation(act_t[:, t], sh_turn_bank[t][:, 0:2 * P].rearrange("p (f n) -> p f n", f=2), ACT.Copy)\
                        .then_inc(sh_act_t_ready.sem, 1)
                act.wait_ge(index_done.sem, index_done.at(l))
                nc.scalar.activation(place_t, h_bank[:, 0:T * P].rearrange("p (t n) -> p t n", t=T), ACT.Copy)\
                    .then_inc(place_t_ready.sem, 1)

                act.wait_ge(table_ready.sem, table_ready.at(l))
                last_turn, nth, pairs = block_count(act, l)

                def sigmoid(it, j):
                    act.wait_ge(h_done, nth(it, j) + RING)
                    nc.scalar.activation(sig_blk, h_bank[:, 0:FF // 2], ACT.Sigmoid).then_inc(sig_ready_blk, 1)

                def copy_turned(it, j):
                    act.wait_ge(turn_done, nth(it, j))
                    nc.scalar.activation(turned[:, j // 2, j % 2], h_bank[:, FF:FF + 2 * P], ACT.Copy).then_inc(turned_ready, 1)

                def turn(it):
                    for i in range(PAIRS):
                        for j in (2 * i, 2 * i + 1):
                            sigmoid(it, j)
                            copy_turned(it, j)
                        act.wait_ge(o_done, pairs(it, i))
                        for h in range(2):
                            cp = nc.scalar.activation(o_blk[:, h * CHUNK:(h + 1) * CHUNK], o_banks[h][:], ACT.Copy)
                        cp.then_inc(o_ready, 1)

                with act.Fori(0, last_turn + 1) as it:
                    turn(it)

        @block.vector
        def _(dve):
            v = nc.vector

            def full_of(name, l):
                dve.wait_ge(B[name].full, B[name].full_at(l))
                return B[name].tile

            def norm_x(i, l):
                dve.wait_ge(std_ready[i].sem, std_ready[i].at(l))
                v.reciprocal(std[:], std[:])
                dve.drain()
                for t in range(T):
                    v.tensor_scalar(K.xn[:, t, :], K.x[:, t, :], std[:, t:t + 1], None, ALU.mult)
                dve.drain().then_inc(xn_ready[i].sem, 1)

            def modulate(i, l):
                for g in range(4):
                    bank = full_of(("xT", i, g), l)
                    for j in range(2):
                        k = 2 * g + j
                        ins = v.tensor_scalar(K.h_t[:, k, :], bank[:, j * SEQ:(j + 1) * SEQ],
                                              mod_col[:, 2 * i + 1, k:k + 1], mod_col[:, 2 * i, k:k + 1], ALU.mult, ALU.add)
                    ins.then_inc(B["xT", i, g].free, 1)
                dve.drain().then_inc(ht_ready[i].sem, 1)

            v.memset(hpad[:, :, 0:TAPS - 1], 0.0)
            v.memset(more[:], 0.0)
            v.memset(more_below[:], 0.0)
            with dve.Fori(0, DEPTH) as l:
                one = ds(l, 1)
                norm_x(0, l)
                dve.wait_ge(params.sem, params.at(l, params.n))
                v.tensor_tensor(lam_p[:], lam4[:, 0::2, :], lam4[:, 1::2, :], ALU.mult)
                dve.drain()
                v.tensor_reduce(lam_s[:], lam_p[:], AX.X, ALU.add).then_inc(lam_s_ready.sem, 1)
                v.tensor_scalar(gain_o[:], subln[:], K.lam_rest[:, one], None, ALU.mult)
                for c in range(MOD_CHUNKS):
                    part, half = divmod(c, 2)
                    bank = full_of(("mod", c), l)
                    if part in MOD_ROW_PARTS:
                        g = gate[:, MOD_ROW_PARTS.index(part), half * CHUNK:(half + 1) * CHUNK]
                        v.tensor_tensor(g, bank[:], g, ALU.add).then_inc(B["mod", c].free, 1)
                    else:
                        v.tensor_tensor(pick, bank[:].rearrange("p (q k) -> p q k", k=KT),
                                        broadcast(K.ident[:, 64 * half:64 * half + 64], 2, KT), ALU.mult)\
                            .then_inc(B["mod", c].free, 1)
                        dve.drain()
                        v.tensor_reduce(col4[:, MOD_COL_PARTS.index(part), half, :], pick.rearrange("p q k -> p k q"),
                                        AX.X, ALU.add)
                        dve.drain()
                v.tensor_tensor(mod_col[:], col4[:, :, 0, :], col4[:, :, 1, :], ALU.add)
                dve.drain()
                v.tensor_tensor(mod_col[:], mod_col[:], mod_b[:], ALU.add)
                dve.drain()
                for i in range(2):
                    v.scalar_tensor_tensor(mod_col[:, 2 * i + 1, :], mod_col[:, 2 * i + 1, :], 1.0, norm_g[:, i, :],
                                           ALU.add, ALU.mult)
                dve.drain()
                modulate(0, l)
                dve.wait_ge(ug_ready.sem, ug_ready.at(l, 2))
                for i in range(2):
                    bank = full_of(("ua", i), l)
                    v.tensor_tensor(hpad[:, 2 * i:2 * i + 2, TAPS - 1:], bank[:].rearrange("p (c n) -> p c n", c=2),
                                    conv_t[:, 2 * i:2 * i + 2, :], ALU.mult).then_inc(B["ua", i].free, 1)
                dve.drain()
                dve.wait_ge(vec_ready.sem, vec_ready.at(l))
                ch = TAPS * CT
                for k in range(TAPS):
                    for c in range(CT):
                        w = vec_t[:, k * CT + c:k * CT + c + 1]
                        if k == 0:
                            v.tensor_scalar(conv[:, c, :], hpad[:, c, 0:SEQ], w, vec_t[:, ch + c:ch + c + 1], ALU.mult, ALU.add)
                        else:
                            v.scalar_tensor_tensor(conv[:, c, :], hpad[:, c, k:k + SEQ], w, conv[:, c, :], ALU.mult, ALU.add)
                    dve.drain()
                dve.drain().then_inc(conv_ready.sem, 1)
                dve.wait_ge(qk_ready.sem, qk_ready.at(l))
                sq = z_flat[:, 0:T * 1024]
                qk_all = qk[:].rearrange("p t n -> p (t n)")
                v.tensor_tensor(sq, qk_all, qk_all, ALU.mult)
                dve.drain()
                v.tensor_reduce(qk_std[:], sq.rearrange("p (h n) -> p h n", n=DA_HD), AX.X, ALU.add)\
                    .then_inc(qk_sq_ready.sem, 1)
                dve.wait_ge(qk_std_ready.sem, qk_std_ready.at(l))
                v.reciprocal(qk_std[:], qk_std[:])
                dve.drain()
                heads = qk_all.rearrange("p (h n) -> p h n", n=DA_HD)
                v.tensor_tensor(heads, heads, broadcast(qk_std[:], 2, DA_HD), ALU.mult)
                dve.drain()
                for w in range(2):
                    part = qk_heads[:, :, 8 * w:8 * w + 8, :]
                    v.tensor_tensor(part, part, broadcast(broadcast(gain_qk[:, w, :], 1, 8), 1, T), ALU.mult)
                dve.drain()
                half = DA_HD // 2
                cos, sin = (broadcast(tab[:, :, 0:half], 2, 16) for tab in (K.cos, K.sin))
                s1 = z_flat[:, 0:1024].rearrange("p (t h n) -> p t h n", t=T, h=16)
                s2 = z_flat[:, 1024:2048].rearrange("p (t h n) -> p t h n", t=T, h=16)
                x1, x2 = qk_heads[:, :, :, 0:half], qk_heads[:, :, :, half:]
                v.tensor_tensor(s1, x1, cos, ALU.mult)
                v.tensor_tensor(s2, x2, sin, ALU.mult)
                dve.drain()
                v.tensor_tensor(qk_rot[:, :, :, 0:half], s1, s2, ALU.subtract)
                dve.drain()
                v.tensor_tensor(s1, x2, cos, ALU.mult)
                v.tensor_tensor(s2, x1, sin, ALU.mult)
                dve.drain()
                v.tensor_tensor(qk_rot[:, :, :, half:], s1, s2, ALU.add)
                dve.drain().then_inc(qk_rot_ready.sem, 1)
                dve.wait_ge(log_ready.sem, log_ready.at(l))
                v.scalar_tensor_tensor(sp_[:].rearrange("p h n -> p (h n)"), z_flat, 0.0,
                                       sp_[:].rearrange("p h n -> p (h n)"), ALU.max, ALU.add)
                dve.drain()
                diagonal = (0, 2 * P)
                for c in diagonal:
                    v.tensor_tensor(sp_[:, :, c:c + P], sp_[:, :, c:c + P], broadcast(K.strict_01[:], 1, SB_HEADS), ALU.mult)
                dve.drain().then_inc(sp_ready.sem, 1)
                for r in range(3):
                    for par in range(2):
                        bank = full_of(("suf", r, par), l)
                        zz = z[:, 4 * par:4 * par + 4, r * P:(r + 1) * P]
                        v.tensor_tensor(zz, zz, bank[:].rearrange("p (h n) -> p h n", h=4), ALU.subtract)\
                            .then_inc(B["suf", r, par].free, 1)
                dve.drain()
                for c in diagonal:
                    v.scalar_tensor_tensor(z[:, :, c:c + P], z[:, :, c:c + P], 0.0, broadcast(K.strict_neg[:], 1, SB_HEADS),
                                           ALU.min, ALU.add)
                v.tensor_scalar(z[:, :, P:2 * P], z[:, :, P:2 * P], 0.0, None, ALU.min)
                dve.drain().then_inc(d_ready.sem, 1)
                dve.wait_ge(yct_ready.sem, yct_ready.at(l))
                for m in range(2):
                    for i in range(2):
                        src = full_of(("s1", m, i), l)[:].rearrange("p (h n) -> p h n", h=2)
                        dst = e1[:, 4 * m + 2 * i:4 * m + 2 * i + 2, :]
                        v.tensor_copy(dst[:, :, 0:P], src[:, :, 0:P])
                        v.tensor_tensor(dst[:, :, P:SEQ], src[:, :, P:SEQ], broadcast(K.causal_neg[:], 1, 2), ALU.add)\
                            .then_inc(B["s1", m, i].free, 1)
                for m in range(2):
                    src = full_of(("s0", m), l)[:].rearrange("p (h n) -> p h n", h=4)
                    v.tensor_tensor(e0[:, 4 * m:4 * m + 4, :], src, broadcast(K.causal_neg[:], 1, 4), ALU.add)\
                        .then_inc(B["s0", m].free, 1)
                dve.drain()
                v.tensor_reduce(row16[:, 0, 0:8], e1, AX.X, ALU.max)
                v.tensor_reduce(row16[:, 0, 8:16], e0, AX.X, ALU.max)
                dve.drain()
                v.tensor_scalar(row16[:, 0, :], row16[:, 0, :], -DA_HD ** -0.5, None, ALU.mult)
                dve.drain().then_inc(max_ready.sem, 1)
                bank = full_of("cmean", l)
                v.tensor_tensor(conv[:], conv[:], broadcast(bank[:, 0:SEQ], 1, CT), ALU.subtract).then_inc(B["cmean"].free, 1)
                dve.drain()
                v.tensor_tensor(conv_t[:], conv[:], conv[:], ALU.mult)
                dve.drain().then_inc(conv_sq_ready.sem, 1)
                dve.wait_ge(lam_e_ready.sem, lam_e_ready.at(l))
                v.tensor_tensor(lam[:], lam_e[:, 0:1], lam_e[:, 1:2], ALU.subtract)
                dve.drain()
                v.tensor_scalar(lam[:], lam[:], K.lam_init[:, one], None, ALU.add)
                dve.wait_ge(exp_ready.sem, exp_ready.at(l))
                v.reciprocal(row16[:, 2, :], row16[:, 1, :])
                dve.drain()
                for c in (4, 12):
                    v.tensor_scalar(row16[:, 2, c:c + 4], row16[:, 2, c:c + 4], lam[:], None, ALU.mult)
                dve.drain()
                for e, c, n in ((e1, 0, SEQ), (e0, 8, P)):
                    v.tensor_tensor(e, e, broadcast(row16[:, 2, c:c + 8], 2, n), ALU.mult)
                dve.drain()
                for e in (e1, e0):
                    v.tensor_tensor(e[:, 0:4, :], e[:, 0:4, :], e[:, 4:8, :], ALU.subtract)
                dve.drain().then_inc(a_ready.sem, 1)
                dve.wait_ge(conv_std_ready.sem, conv_std_ready.at(l))
                v.reciprocal(conv_std[:], conv_std[:])
                dve.drain()
                v.tensor_tensor(conv[:], conv[:], broadcast(conv_std[:], 1, CT), ALU.mult)
                dve.drain()
                for c in range(CT):
                    v.tensor_scalar(conv[:, c, :], conv[:, c, :], vec_t[:, ch + CT + c:ch + CT + c + 1],
                                    vec_t[:, ch + 2 * CT + c:ch + 2 * CT + c + 1], ALU.mult, ALU.add)
                dve.drain().then_inc(conv_ln_ready.sem, 1)
                for t in range(T):
                    bank = full_of(("oa", t), l)
                    v.tensor_copy(oa[:, t, :], bank[:]).then_inc(B["oa", t].free, 1)
                dve.drain()
                sq = z_flat[:, 0:T * 512].rearrange("p (h n) -> p h n", n=2 * DA_HD)
                v.tensor_tensor(sq, oa_heads, oa_heads, ALU.mult)
                dve.drain()
                v.tensor_reduce(oa_std[:], sq, AX.X, ALU.add).then_inc(oa_sq_ready.sem, 1)
                dve.wait_ge(oa_std_ready.sem, oa_std_ready.at(l))
                v.reciprocal(oa_std[:], oa_std[:])
                dve.drain()
                v.tensor_tensor(oa_heads, oa_heads, broadcast(oa_std[:], 2, 2 * DA_HD), ALU.mult)
                dve.drain()
                v.tensor_tensor(oa_heads, oa_heads, broadcast(gain_o[:], 1, T * DA_HEADS), ALU.mult)
                dve.drain().then_inc(oa_ready.sem, 1)
                dve.wait_ge(conv_sig_ready.sem, conv_sig_ready.at(l))
                v.tensor_tensor(yb_t[:], conv[:], conv_t[:], ALU.mult)
                dve.drain().then_inc(ybt_ready.sem, 1)
                n = 0
                for i in range(3):
                    for h in range(2):
                        for t in range(T):
                            col = slice(h * CHUNK, (h + 1) * CHUNK)
                            dve.wait_ge(sig_ready.sem, sig_ready.at(l, n + 1))
                            bank = full_of(("y", i, h, t), l)
                            sig = sig_g[:, n % 2, :]
                            if i == 0:
                                v.tensor_tensor(merged[:, t, col], bank[:], sig, ALU.mult).then_inc(B["y", i, h, t].free, 1)
                                dve.drain().then_inc(y_used.sem, 1)
                            else:
                                if i == 1:
                                    v.tensor_tensor(y_tmp[:], bank[:], proj_b_bias[:, col], ALU.add)\
                                        .then_inc(B["y", i, h, t].free, 1)
                                    dve.drain()
                                    v.tensor_tensor(y_tmp[:], y_tmp[:], sig, ALU.mult)
                                else:
                                    v.tensor_tensor(y_tmp[:], bank[:], sig, ALU.mult).then_inc(B["y", i, h, t].free, 1)
                                dve.drain().then_inc(y_used.sem, 1)
                                v.tensor_tensor(merged[:, t, col], merged[:, t, col], y_tmp[:], ALU.add)
                                dve.drain()
                            n += 1
                dve.drain().then_inc(merged_ready.sem, 1)
                for h in range(2):
                    for t in range(T):
                        col = slice(h * CHUNK, (h + 1) * CHUNK)
                        bank = full_of(("wo", h, t), l)
                        v.tensor_tensor(y_tmp[:], bank[:], gate[:, 0, col], ALU.mult).then_inc(B["wo", h, t].free, 1)
                        dve.drain()
                        v.tensor_tensor(K.x[:, t, col], K.x[:, t, col], y_tmp[:], ALU.add)
                        dve.drain()
                dve.drain().then_inc(x_mid.sem, 1)

                norm_x(1, l)
                modulate(1, l)
                dve.wait_ge(score_ready.sem, score_ready.at(l))
                v.tensor_tensor(biased[:], score[:], broadcast(rt_bias[:], 1, T), ALU.add)
                dve.drain()
                for t in range(T):
                    for g in range(N_GROUPS):
                        v.max(out=top[:, t, g, :], in_=biased[:, t, g * PER_GROUP:(g + 1) * PER_GROUP])
                dve.drain()
                v.tensor_tensor(g_score[:], top[:, :, :, 0], top[:, :, :, 1], ALU.add)
                dve.drain()
                for t in range(T):
                    other, own = broadcast(g_score[:, t, :], 1, N_GROUPS), broadcast(g_score[:, t, :], 2, N_GROUPS)
                    v.tensor_tensor(g_cmp[:, t], other, own, ALU.is_gt)
                    v.tensor_tensor(g_eq[:, t], other, own, ALU.is_equal)
                dve.drain()
                for t in range(T):
                    v.tensor_tensor(g_eq[:, t], g_eq[:, t], K.lower8[:], ALU.mult)
                dve.drain()
                v.tensor_tensor(g_cmp[:], g_cmp[:], g_eq[:], ALU.add)
                dve.drain()
                v.tensor_reduce(g_rank[:], g_cmp[:], AX.X, ALU.add)
                dve.drain()
                v.tensor_scalar(g_rank[:], g_rank[:], TOPK_GROUPS - 0.5, None, ALU.is_lt)
                dve.drain()
                v.tensor_scalar(g_neg[:], g_rank[:], -NEG, NEG, ALU.mult, ALU.add)
                by_group = biased[:].rearrange("p t (g e) -> p t g e", g=N_GROUPS)
                v.tensor_tensor(by_group, by_group, broadcast(g_rank[:], 3, PER_GROUP), ALU.mult)
                dve.drain()
                v.tensor_tensor(by_group, by_group, broadcast(g_neg[:], 3, PER_GROUP), ALU.add)
                dve.drain()
                for t in range(T):
                    v.max(out=top8[:, t, :], in_=biased[:, t, :])
                dve.drain()
                for t in range(T):
                    v.match_replace(out=rest[:, t, :], in_to_replace=top8[:, t, :], in_values=biased[:, t, :],
                                    imm_value=3.0 * NEG)
                dve.drain()
                v.tensor_tensor(chosen[:], broadcast(rest[:], 2, 2), broadcast(biased[:], 2, 2), ALU.not_equal)
                dve.drain().then_inc(chosen_ready.sem, 1)
                v.tensor_tensor(rest[:], chosen[:, :, 0, :], score[:], ALU.mult)
                dve.drain()
                v.tensor_reduce(w_sum[:], rest[:], AX.X, ALU.add)
                dve.drain()
                v.tensor_scalar(w_sum[:], w_sum[:], 1e-20, None, ALU.add)
                dve.drain()
                v.reciprocal(w_sum[:], w_sum[:])
                dve.drain()
                for t in range(T):
                    v.tensor_scalar(place[:, t, 1, 0:N_EXPERTS], rest[:, t, :], w_sum[:, t:t + 1], ROUTED_SCALE,
                                    ALU.mult, ALU.mult)
                for t in range(T):
                    dve.wait_ge(sh_sig_ready.sem, sh_sig_ready.at(l, t + 1))
                    v.tensor_tensor(act_h[:, t, :], sh_bank[t][:, 0:FF], sig_h[:, t, :], ALU.mult)
                    dve.drain()
                    v.tensor_tensor(act_h[:, t, :], act_h[:, t, :], sh_bank[t][:, FF:2 * FF], ALU.mult)\
                        .then_inc(sh_act_ready.sem, 1)
                dve.wait_ge(count_done.sem, count_done.at(l))
                v.scalar_tensor_tensor(place[:, :, 0, 0:N_EXPERTS], o_bank[:, 0:T * N_EXPERTS].rearrange("p (t e) -> p t e", t=T),
                                       1.0, chosen[:, :, 0, :], ALU.add, ALU.mult)
                v.tensor_tensor(more[:, 0:ROUNDS], K.full_rounds[:], o_bank[:, at_count:at_count + ROUNDS], ALU.is_lt)
                dve.drain()
                v.tensor_copy(place_64[:], place[:, :, :, 0:N_EXPERTS])
                for r in range(ROUNDS):
                    v.tensor_tensor(more_below[:, r + 1:r + 2], more_below[:, r:r + 1], more[:, r:r + 1], ALU.add)
                    dve.drain()
                dve.drain().then_inc(more_ready.sem, 1)
                dve.wait_ge(index_done.sem, index_done.at(l))
                v.tensor_copy(extra_at[:], o_bank[:, at_index:at_index + ROUNDS + 1])
                dve.drain()
                for r in range(ROUNDS):
                    v.tensor_scalar(extra_hot[:, r, :], K.ramp[:, 0:EXTRA], extra_at[:, r:r + 1], more[:, r:r + 1],
                                    ALU.is_equal, ALU.mult)
                dve.drain()
                v.tensor_tensor(extra_any[:], extra_hot[:, 0, :], extra_hot[:, 1, :], ALU.add)
                v.scalar_tensor_tensor(extra_round[:], extra_hot[:, 1, :], 2.0, extra_hot[:, 0, :], ALU.mult, ALU.add)
                dve.drain()
                v.tensor_tensor(extra_any[:], extra_any[:], extra_hot[:, 2, :], ALU.add)
                v.scalar_tensor_tensor(extra_round[:], extra_hot[:, 2, :], 3.0, extra_round[:], ALU.mult, ALU.add)
                dve.drain().then_inc(extra_ready.sem, 1)
                v.tensor_scalar(turns_cmp[:], K.ramp[:, 0:EXTRA:UNROLL], extra_at[:, ROUNDS:ROUNDS + 1], None, ALU.is_lt)
                dve.drain()
                v.tensor_reduce(turns_f[:], turns_cmp[:], AX.X, ALU.add)
                dve.drain()
                v.tensor_scalar(turns_f[:], turns_f[:], float(N_EXPERTS // UNROLL - 1), None, ALU.add)
                dve.drain()
                v.tensor_copy(K.last_turn[:, one], turns_f[:])
                v.scalar_tensor_tensor(K.first_turn_f[:, ds(l + 1, 1)], turns_f[:], 1.0, K.first_turn_f[:, one], ALU.add, ALU.add)
                dve.drain()
                v.tensor_copy(K.first_turn[:], K.first_turn_f[:])
                dve.wait_ge(list_done.sem, list_done.at(l))
                v.tensor_copy(K.table[:, N_EXPERTS:MAX_BLOCKS], o_bank[:, at_expert:at_expert + EXTRA])
                for i, (bank, c) in enumerate(((o_bank, at_place), (h_bank, at_weight))):
                    v.tensor_copy(place[:, :, i, N_EXPERTS:MAX_BLOCKS], bank[:, c:c + T * EXTRA].rearrange("p (t b) -> p t b", t=T))
                dve.drain().then_inc(table_ready.sem, 1)

                dve.wait_ge(table_ready.sem, table_ready.at(l))
                dve.sem_inc(wait_carrier, 1)
                last_turn, nth, pairs = block_count(dve, l)

                def one_hot(it, j):
                    col = ds(it * UNROLL + j, 1)
                    places = K.ramp[:, 1:1 + SLOTS]
                    for t in range(T):
                        v.tensor_scalar(pick_hot[:, j % 2, t, :], places, place[:, t, 0, col], None, ALU.is_equal)
                        v.tensor_scalar(spread[:, j // 2 % PAIRS, t, j % 2, :], places, place[:, t, 0, col], place[:, t, 1, col],
                                        ALU.is_equal, ALU.mult)
                    dve.drain().then_inc(hot_ready, 1)

                def block_x(it, j):
                    dve.wait_ge(gather_done, nth(it, j))
                    x = x_blk[:, j % 2]
                    v.tensor_tensor(x, x_bank[:].rearrange("p (k s) -> p k s", k=KT), broadcast(mod_col[:, 3, :], 2, SLOTS), ALU.mult)
                    dve.drain()
                    v.tensor_tensor(x, x, broadcast(mod_col[:, 2, :], 2, SLOTS), ALU.add).then_inc(x_ready, 1)

                def block_act(it, j):
                    dve.wait_ge(sig_ready_blk, nth(it, j))
                    v.tensor_tensor(act_blk, h_bank[:, 0:FF // 2], sig_blk, ALU.mult)
                    dve.drain()
                    v.tensor_tensor(act_blk, act_blk, h_bank[:, FF // 2:FF], ALU.mult).then_inc(act_ready, 1)

                def turn(it, last=False):
                    for i in range(PAIRS):
                        a, b = 2 * i, 2 * i + 1
                        end = last and i == PAIRS - 1
                        block_act(it, a)
                        block_x(it, b)
                        if not end:
                            one_hot(it, b + 1)
                            one_hot(it, b + 2)
                        block_act(it, b)
                        if not end:
                            block_x(it, b + 1)

                one_hot(0, 0)
                one_hot(0, 1)
                block_x(0, 0)
                with dve.Fori(0, last_turn) as it:
                    turn(it)
                turn(last_turn, last=True)
                dve.wait_ge(added, pairs(last_turn, PAIRS - 1))
                for t in range(T):
                    for h in range(2):
                        col = slice(h * CHUNK, (h + 1) * CHUNK)
                        v.tensor_tensor(y_tmp[:], y_bank[t][h][:], gate[:, 1, col], ALU.mult)\
                            .then_inc(B["=moe_y", t, h].free, 1)
                        dve.drain()
                        v.tensor_tensor(K.x[:, t, col], K.x[:, t, col], y_tmp[:], ALU.add)
                        dve.drain()
                dve.drain().then_inc(x_out.sem, 1)


HEADS_2 = MLA_H + MOBA_H
GROUPS_2 = (
    ["vec", "wsT"] + [("xT", g) for g in range(4)]
    + ["c_h", "c_b", "c_c", "g_b"]
    + [(n, t) for n in ("n0", "n1", "n2", "n3", "n4", "n5") for t in range(T)]
    + ["cqT", "ckT"] + [("q", t) for t in range(T)] + [("kv", t) for t in range(T)]
    + [("bT", w) for w in range(2)]
    + [("mT", w, i) for w in range(2) for i in range(2)]
    + [("mix", t) for t in range(T)]
    + [("sm1", i) for i in range(2)] + ["sm0"] + [("sb1", par) for par in range(2)] + [("sb0", par) for par in range(2)]
    + [("aT1", i) for i in range(4)] + [("aT0", i) for i in range(2)] + [("o", t) for t in range(T)]
    + [("yT", i) for i in range(3)] + [("wo", h, t) for h in range(2) for t in range(T)]
)
GROUPS_2 += ["-pad"] * (-len(GROUPS_2) % BANKS)
READERS_2 = {"t0": "c_b", "t1": "g_b"} | {n: (n, 1) for n in ("n0", "n1", "n2", "n3", "n4", "n5")}


def second_block(nc, A, K, out):
    ds = bass.ds
    with ExitStack() as ctx:
        def sb(name, shape, dt=F32):
            return ctx.enter_context(nc.sbuf_tensor(name, shape, dt))

        def sem(name):
            return ctx.enter_context(nc.semaphore(name))

        def signal(name, per_layer=1, credit=0):
            return Signal(sem(name), per_layer, credit)

        norm_g = sb("norm_g2", [P, KT])
        gain_cq = sb("gain_cq", [P, 256])
        gain_ckv = sb("gain_ckv", [P, 128])
        gain_q = sb("gain_q", [P, MLA_QK])
        gain_kn = sb("gain_kn", [P, MLA_NOPE])
        gain_kr = sb("gain_kr", [P, MLA_ROPE])
        sg_gain = sb("sg_gain", [P, GW])
        sg_bias = sb("sg_bias", [P, GW])
        gain_moba = sb("gain_moba", [P, 2, MOBA_HD])
        w_uq = sb("w_uq", [P, 2, MLA_H * MLA_QK])
        w_ukv = sb("w_ukv", [P, MLA_H * 2 * 64])
        sg_w = sb("sg_w", [P, SG_G, P])
        cw_rows = sb("cw_rows", [6, P])
        sb_rows = sb("sb_rows", [SG_G, P])
        vec_t = sb("vec_t2", [P, 6 + SG_G])
        ws_t = sb("ws_t", [P, SG_G, P])
        std = sb("std2", [P, T])
        sq_sum = sb("sq_sum2", [P, T])
        nat = sb("nat", [P, T, NAT_COLS])
        cbr = sb("cbr", [P, 4, 2, SEQ])
        sig_b = sb("sig_b", [P, 2, SEQ])
        zpad = sb("zpad", [P, 2, 2 + SEQ])
        cv = sb("cv", [P, 2, SEQ])
        sig = sb("sig_acd", [P, 3, T, GW])
        scr = sb("scr", [P, T, 512])
        stat = sb("stat", [P, T, 12])
        mean_v = sb("mean_v", [P, T])
        stat2 = sb("stat2", [P, T, 8])
        kr = sb("kr", [P, T, MLA_ROPE])
        c_t = sb("c_t", [P, 3, SEQ])
        q_nat = sb("q_nat", [P, T, MLA_H, MLA_QK])
        kv_nat = sb("kv_nat", [P, T, MLA_H, 2 * 64])
        k_nat = sb("k_nat", [P, T, MLA_H, MLA_QK])
        rope1 = sb("rope1", [P, T, 8, 16])
        rope2 = sb("rope2", [P, T, 8, 16])
        rope3 = sb("rope3", [P, T, 8, 16])
        mqk_t = sb("mqk_t", [MLA_QK, 2, MLA_H, SEQ])
        bqk_t = sb("bqk_t", [P, 2, 2, SEQ])
        e1 = sb("e1_2", [P, HEADS_2, SEQ])
        e0 = sb("e0_2", [P, HEADS_2, P])
        row16 = sb("row16_2", [P, 3, 2 * HEADS_2])
        a_t = sb("a_t2", [P, HEADS_2, 3, P])
        y_nat = K.h_t[:].rearrange("p k n -> p (k n)")[:, 0:T * 3 * GW].rearrange("p (t i n) -> p t i n", t=T, i=3)
        y_t = K.xn[:].rearrange("p t n -> p (t n)").rearrange("p (k n) -> p k n", n=SEQ)

        def seg(name, n):
            return nat[:, :, NAT[name]:NAT[name] + n]

        B, full, free = bank_plan(GROUPS_2, K.psum, sem, "2")
        filled = [Signal(sem(f"slot{s}_filled2")) for s in range(RING)]
        names = [c[0] for c in CHUNKS_2] + [("wo", 0), ("wo", 1)]
        names += [None] * (-len(names) % RING)
        readers = [READERS_2.get(n) if n in READERS_2 else ((n[0], n[1], 1) if n else None) for n in names]
        C, loads, arrived = {}, [], [0] * RING
        for i, name in enumerate(names):
            s = i % RING
            if name is None:
                continue
            arrived[s] += 32 if name == "n0" else 16
            C[name] = Chunk(K.slots[s], filled[s], arrived[s])
            earlier = [(j, readers[j]) for j in range(s, i, RING) if readers[j]]
            last = [readers[j] for j in range(s, len(names), RING) if readers[j]][-1]
            loads.append((name, s, earlier[-1][1] if earlier else None, last))
        for s in range(RING):
            filled[s].n = arrived[s]

        N_PARAMS = 15
        params = signal("params_loaded2", 16 * N_PARAMS)
        x_out = signal("x_after_layer2", 1, 1)
        std_ready, xn_ready, ht_ready = signal("x_std_ready_2"), signal("xn_ready_2"), signal("ht_ready_2")
        vec_ready, wst_ready = signal("vec_t_ready2"), signal("ws_t_ready")
        cbr_ready, nat_ready, sig_acd_ready = signal("cbr_ready"), signal("nat_ready"), signal("sig_acd_ready")
        stat_ready, stat_std_ready = signal("stat_ready"), signal("stat_std_ready")
        c_ready, ct_ready, qkv_ready = signal("c_normed_ready"), signal("c_t_ready"), signal("q_kv_ready")
        stat2_ready, stat2_std_ready = signal("stat2_ready"), signal("stat2_std_ready")
        moba_ready, mla_ready, vn_ready = signal("moba_qk_ready"), signal("mla_qk_ready"), signal("vn_ready")
        bt_ready, mt_ready = signal("moba_t_ready"), signal("mla_t_ready")
        max_ready, exp_ready, a_ready, at_ready = (signal("row_max_ready2"), signal("exp_ready2"), signal("a_ready2"),
                                                   signal("a_t_ready2"))
        yb_ready, y_ready, yt_ready = signal("yb_ready"), signal("y_nat_ready"), signal("y_t_ready")
        stored = sem("stored")

        block = ctx.enter_context(nc.Block())

        @block.sync
        def _(sp):
            for b in range(BANKS):
                sp.sem_inc(free[b].sem, 1)
                sp.sem_inc(full[b].sem, full[b].credit)
            sp.sem_inc(x_out.sem, 1)
            with sp.Fori(0, DEPTH) as l:
                for name, s, before, last in loads:
                    if before is None:
                        sp.wait_ge(B[last].full, B[last].full_before(l))
                    else:
                        sp.wait_ge(B[before].full, B[before].full_at(l))
                    if name in READERS_2:
                        _, col, n, _ = next(c for c in CHUNKS_2 if c[0] == name)
                        src = A["w_in_2"][ds(l, 1), :, col:col + n].rearrange("a (p k) n -> p (a k) n", k=KT)
                    else:
                        n = CHUNK
                        src = A["w_out_2"][ds(l, 1), :, name[1] * n:(name[1] + 1) * n].rearrange("a (k p) n -> p (a k) n", p=P)
                    for half in (slice(P // 2, P), slice(0, P // 2)) if name == "n0" else (slice(0, P),):
                        sp.dma_start(K.slots[s][half, :, 0:n], src[half]).then_inc(filled[s].sem, 16)
            sp.wait_ge(x_out.sem, x_out.credit + DEPTH)
            for t in range(T):
                sp.dma_start(out[0, t * P:(t + 1) * P, :], K.x[:, t, :]).then_inc(stored, 16)
            sp.wait_ge(stored, 16 * T)

        @block.gpsimd
        def _(pool):
            with pool.Fori(0, DEPTH) as l:
                pool.wait_ge(x_out.sem, x_out.at(l, 0))
                one = ds(l, 1)

                def load(dst, src):
                    pool.dma_start(dst, src).then_inc(params.sem, 16)

                load(norm_g[:], A["norm_g_2"][one].rearrange("a (p k) -> p (a k)", k=KT))
                load(cw_rows[:], A["conv_w_2"][one].rearrange("a k (c p) -> (a k c) p", p=P))
                load(sb_rows[:], A["sg_b_2"][one].rearrange("a g p -> (a g) p"))
                load(sg_w[:], A["sg_w_2"][one].rearrange("a g t s -> t (a g) s"))
                for dst, name in ((gain_cq, "mla_q_norm_g_2"), (gain_ckv, "mla_kv_norm_g_2"), (gain_q, "mla_q_g_2"),
                                  (gain_kn, "mla_k_nope_g_2"), (gain_kr, "mla_k_rope_g_2"), (sg_gain, "sg_ln_g_2"),
                                  (sg_bias, "sg_ln_b_2")):
                    load(dst[:], A[name][one].to_broadcast(list(dst.shape)))
                for w, name in enumerate(("moba_q_g_2", "moba_k_g_2")):
                    load(gain_moba[:, w, :], A[name][one].to_broadcast([P, MOBA_HD]))
                load(w_uq[:], A["mla_w_uq_2"][one].rearrange("a (k p) n -> p (a k) n", p=P))
                load(w_ukv[:], A["mla_w_ukv_2"][one].rearrange("a p n -> p (a n)"))

        @block.tensor
        def _(pe):
            def begin(name, l):
                pe.wait_ge(B[name].free, B[name].free_at(l))
                return B[name].tile

            def chunk(name, l):
                pe.wait_ge(C[name].filled, C[name].filled_at(l))
                return C[name].tile

            def rows(name, l, w, t, stationary, cols=CHUNK):
                bank = begin(name, l)
                for k in range(KT):
                    mm = nc.tensor.matmul(bank[:, 0:cols], stationary[:, k, t * P:(t + 1) * P], w[:, k, 0:cols],
                                          start=(k == 0), stop=(k == KT - 1))
                mm.then_inc(B[name].full, 1)

            def turn(name, l, pieces, size=P):
                bank = begin(name, l)
                for col, src in pieces:
                    mm = nc.tensor.transpose(bank[0:size, col:col + P], src, K.ident[:])
                mm.then_inc(B[name].full, 1)

            with pe.Fori(0, DEPTH) as l:
                pe.wait_ge(params.sem, params.at(l, params.n))
                bank = begin("vec", l)
                turn("wsT", l, [(g * P, sg_w[:, g, :]) for g in range(SG_G)])
                nc.tensor.transpose(bank[:, 0:6], cw_rows[:], K.ident[0:6, 0:6])
                nc.tensor.transpose(bank[:, 6:6 + SG_G], sb_rows[:], K.ident[0:SG_G, 0:SG_G]).then_inc(B["vec"].full, 1)
                pe.wait_ge(xn_ready.sem, xn_ready.at(l))
                for g in range(4):
                    turn(("xT", g), l, [(j * SEQ + t * P, K.xn[:, t, 2 * g + j::KT]) for j in range(2) for t in range(T)])
                pe.wait_ge(ht_ready.sem, ht_ready.at(l))
                for name, pair in (("t0", ("c_h", "c_b")), ("t1", ("c_c", "g_b"))):
                    w = chunk(name, l)
                    for i, group in enumerate(pair):
                        bank = begin(group, l)
                        for j in range(2):
                            c = 2 * i + j
                            for k in range(KT):
                                mm = nc.tensor.matmul(bank[:, j * SEQ:(j + 1) * SEQ], w[:, k, c * P:(c + 1) * P],
                                                      K.h_t[:, k, :], start=(k == 0), stop=(k == KT - 1))
                        mm.then_inc(B[group].full, 1)
                for name, _, n, place in CHUNKS_2:
                    if place is not None:
                        w = chunk(name, l)
                        for t in range(T):
                            rows((name, t), l, w, t, K.h_t, n)
                pe.wait_ge(c_ready.sem, c_ready.at(l))
                turn("cqT", l, [(k * SEQ + t * P, nat[:, t, k * P:(k + 1) * P]) for k in range(2) for t in range(T)])
                turn("ckT", l, [(t * P, nat[:, t, NAT["ckv"]:NAT["ckv"] + P]) for t in range(T)])
                pe.wait_ge(ct_ready.sem, ct_ready.at(l))
                for t in range(T):
                    bank = begin(("q", t), l)
                    for k in range(2):
                        mm = nc.tensor.matmul(bank[:, 0:MLA_H * MLA_QK], c_t[:, k, t * P:(t + 1) * P], w_uq[:, k, :],
                                              start=(k == 0), stop=(k == 1))
                    mm.then_inc(B["q", t].full, 1)
                for t in range(T):
                    bank = begin(("kv", t), l)
                    nc.tensor.matmul(bank[:], c_t[:, 2, t * P:(t + 1) * P], w_ukv[:], start=True, stop=True)\
                        .then_inc(B["kv", t].full, 1)
                pe.wait_ge(moba_ready.sem, moba_ready.at(l))
                for w, name in enumerate(("mq", "mk")):
                    turn(("bT", w), l, [(i * SEQ + t * P, nat[:, t, NAT[name] + i * P:NAT[name] + (i + 1) * P])
                                        for i in range(2) for t in range(T)])
                pe.wait_ge(mla_ready.sem, mla_ready.at(l))
                for w, src in enumerate((q_nat, k_nat)):
                    for i in range(2):
                        turn(("mT", w, i), l, [(j * SEQ + t * P, src[:, t, 2 * i + j, :]) for j in range(2) for t in range(T)],
                             MLA_QK)
                pe.wait_ge(wst_ready.sem, wst_ready.at(l))
                pe.wait_ge(vn_ready.sem, vn_ready.at(l))
                for t in range(T):
                    bank = begin(("mix", t), l)
                    for g in range(SG_G):
                        mm = nc.tensor.matmul(bank[:, g * 64:(g + 1) * 64], ws_t[:, g, :], seg("sv", GW)[:, t, g * 64:(g + 1) * 64],
                                              start=True, stop=True)
                    mm.then_inc(B["mix", t].full, 1)
                pe.wait_ge(mt_ready.sem, mt_ready.at(l))
                for i in range(2):
                    bank = begin(("sm1", i), l)
                    for j in range(2):
                        mm = nc.tensor.matmul(bank[:, j * SEQ:(j + 1) * SEQ], mqk_t[:, 0, 2 * i + j, P:SEQ],
                                              mqk_t[:, 1, 2 * i + j, :], start=True, stop=True)
                    mm.then_inc(B["sm1", i].full, 1)
                bank = begin("sm0", l)
                for h in range(MLA_H):
                    mm = nc.tensor.matmul(bank[:, h * P:(h + 1) * P], mqk_t[:, 0, h, 0:P], mqk_t[:, 1, h, 0:P],
                                          start=True, stop=True)
                mm.then_inc(B["sm0"].full, 1)
                pe.wait_ge(bt_ready.sem, bt_ready.at(l))
                for n, q0, keys in (("sb1", P, SEQ), ("sb0", 0, P)):
                    for par in range(2):
                        part = slice(64 * par, 64 * par + 64)
                        bank = begin((n, par), l)
                        for i in range(2):
                            mm = nc.tensor.matmul(bank[:, i * keys:(i + 1) * keys], bqk_t[part, 0, i, q0:q0 + P],
                                                  bqk_t[part, 1, i, 0:keys], start=True, stop=True)
                        mm.then_inc(B[n, par].full, 1)
                pe.wait_ge(a_ready.sem, a_ready.at(l))
                for i in range(4):
                    turn(("aT1", i), l, [((2 * j + b) * P, e1[:, 2 * i + j, b * P:(b + 1) * P])
                                         for j in range(2) for b in range(2)])
                for i in range(2):
                    turn(("aT0", i), l, [(j * P, e0[:, 4 * i + j, :]) for j in range(4)])
                pe.wait_ge(at_ready.sem, at_ready.at(l))
                for t in range(T):
                    bank = begin(("o", t), l)
                    for r in range(HEADS_2):
                        if r < MLA_H:
                            col, values = r * 64, lambda b, r=r: kv_nat[:, b, r, 64:128]
                        else:
                            head = 2 * ((r - MLA_H) % 2) + (r - MLA_H) // 2
                            col, values = (MLA_H + head) * 64, lambda b, head=head: seg("mv", GW)[:, b, head * 64:(head + 1) * 64]
                        o = bank[:, col:col + 64]
                        if t == 0:
                            mm = nc.tensor.matmul(o, a_t[:, r, 0, :], values(0), start=True, stop=True)
                        else:
                            nc.tensor.matmul(o, a_t[:, r, 1, :], values(0), start=True, stop=False)
                            mm = nc.tensor.matmul(o, a_t[:, r, 2, :], values(1), start=False, stop=True)
                    mm.then_inc(B["o", t].full, 1)
                pe.wait_ge(y_ready.sem, y_ready.at(l))
                for i in range(3):
                    turn(("yT", i), l, [(j * SEQ + t * P, y_nat[:, t, i, j * P:(j + 1) * P]) for j in range(2) for t in range(T)])
                pe.wait_ge(yb_ready.sem, yb_ready.at(l))
                pe.wait_ge(yt_ready.sem, yt_ready.at(l))
                for h in range(2):
                    w = chunk(("wo", h), l)
                    for t in range(T):
                        rows(("wo", h, t), l, w, t, y_t)

        @block.scalar
        def _(act):
            def full_of(name, l):
                act.wait_ge(B[name].full, B[name].full_at(l))
                return B[name].tile

            def copy_out(name, l, dst, src):
                nc.scalar.activation(dst, src, ACT.Copy).then_inc(B[name].free, 1)

            def pairs(bank):
                return bank[:].rearrange("p (c n) -> p c n", c=2)

            with act.Fori(0, DEPTH) as l:
                act.wait_ge(x_out.sem, x_out.at(l, 0))
                for t in range(T):
                    nc.scalar.activation(K.xn[:, t, :], K.x[:, t, :], ACT.Square, accum_out=sq_sum[:, t:t + 1])
                act.drain()
                nc.scalar.activation(std[:], sq_sum[:], ACT.Sqrt, scale=1.0 / D, bias=K.eps[:]).then_inc(std_ready.sem, 1)
                bank = full_of("vec", l)
                copy_out("vec", l, vec_t[:], bank[:, 0:6 + SG_G])
                act.drain().then_inc(vec_ready.sem, 1)
                for i, name in enumerate(("c_h", "c_b", "c_c", "g_b")):
                    bank = full_of(name, l)
                    if name == "g_b":
                        nc.scalar.activation(sig_b[:], pairs(bank), ACT.Sigmoid)
                    copy_out(name, l, cbr[:, i], pairs(bank))
                act.drain().then_inc(cbr_ready.sem, 1)
                for name, _, n, place in CHUNKS_2:
                    if place is not None:
                        for t in range(T):
                            bank = full_of((name, t), l)
                            copy_out((name, t), l, nat[:, t, place:place + n], bank[:, 0:n])
                act.drain().then_inc(nat_ready.sem, 1)
                for i, name in enumerate(("ga", "gc", "gd")):
                    nc.scalar.activation(sig[:, i], seg(name, GW), ACT.Sigmoid)
                act.drain().then_inc(sig_acd_ready.sem, 1)
                act.wait_ge(stat_ready.sem, stat_ready.at(l))
                nc.scalar.activation(stat[:], stat[:], ACT.Sqrt, bias=K.eps[:]).then_inc(stat_std_ready.sem, 1)
                bank = full_of("cqT", l)
                copy_out("cqT", l, c_t[:, 0:2, :], pairs(bank))
                bank = full_of("ckT", l)
                copy_out("ckT", l, c_t[:, 2, :], bank[:, 0:SEQ])
                act.drain().then_inc(ct_ready.sem, 1)
                for t in range(T):
                    bank = full_of(("q", t), l)
                    copy_out(("q", t), l, q_nat[:, t].rearrange("p h n -> p (h n)"), bank[:, 0:MLA_H * MLA_QK])
                for t in range(T):
                    bank = full_of(("kv", t), l)
                    copy_out(("kv", t), l, kv_nat[:, t].rearrange("p h n -> p (h n)"), bank[:])
                act.drain().then_inc(qkv_ready.sem, 1)
                act.wait_ge(stat2_ready.sem, stat2_ready.at(l))
                nc.scalar.activation(stat2[:], stat2[:], ACT.Sqrt, bias=K.eps[:]).then_inc(stat2_std_ready.sem, 1)
                for w in range(2):
                    bank = full_of(("bT", w), l)
                    copy_out(("bT", w), l, bqk_t[:, w], pairs(bank))
                act.drain().then_inc(bt_ready.sem, 1)
                for w in range(2):
                    for i in range(2):
                        bank = full_of(("mT", w, i), l)
                        copy_out(("mT", w, i), l, mqk_t[:, w, 2 * i:2 * i + 2, :],
                                 bank[0:MLA_QK, :].rearrange("p (c n) -> p c n", c=2))
                act.drain().then_inc(mt_ready.sem, 1)
                act.wait_ge(max_ready.sem, max_ready.at(l))
                for r in range(2 * HEADS_2):
                    e = e1[:, r, :] if r < HEADS_2 else e0[:, r - HEADS_2, :]
                    scale = (MLA_QK if r % HEADS_2 < MLA_H else MOBA_HD) ** -0.5
                    nc.scalar.activation(e, e, ACT.Exp, bias=row16[:, 0, r:r + 1], scale=scale,
                                         accum_out=row16[:, 1, r:r + 1])
                act.drain().then_inc(exp_ready.sem, 1)
                for i in range(4):
                    bank = full_of(("aT1", i), l)
                    copy_out(("aT1", i), l, a_t[:, 2 * i:2 * i + 2, 1:3, :],
                             bank[:].rearrange("p (h b n) -> p h b n", h=2, b=2))
                for i in range(2):
                    bank = full_of(("aT0", i), l)
                    copy_out(("aT0", i), l, a_t[:, 4 * i:4 * i + 4, 0, :], bank[:].rearrange("p (h n) -> p h n", h=4))
                act.drain().then_inc(at_ready.sem, 1)
                for i, k in enumerate((0, 4, 6)):
                    bank = full_of(("yT", i), l)
                    copy_out(("yT", i), l, y_t[:, k:k + 2, :], pairs(bank))
                act.drain().then_inc(yt_ready.sem, 1)

        @block.vector
        def _(dve):
            v = nc.vector

            def full_of(name, l):
                dve.wait_ge(B[name].full, B[name].full_at(l))
                return B[name].tile

            def square_sums(dst, src, scratch, n):
                v.tensor_tensor(scratch, src, src, ALU.mult)
                dve.drain()
                v.tensor_reduce(dst, scratch, AX.X, ALU.add)
                dve.drain()
                v.tensor_scalar(dst, dst, 1.0 / n, None, ALU.mult)
                dve.drain()

            def rotate(x1, x2, o1, o2, freqs, heads, half):
                cos, sin = K.cos[:, :, freqs:freqs + half], K.sin[:, :, freqs:freqs + half]
                if heads:
                    cos, sin = broadcast(cos, 2, heads), broadcast(sin, 2, heads)
                    r1, r2, r3 = (r[:, :, 0:heads, 0:half] for r in (rope1, rope2, rope3))
                else:
                    r1, r2, r3 = (r[:, :, 0, 0:half] for r in (rope1, rope2, rope3))
                v.tensor_tensor(r1, x1, cos, ALU.mult)
                v.tensor_tensor(r2, x2, sin, ALU.mult)
                v.tensor_tensor(r3, x1, sin, ALU.mult)
                dve.drain()
                v.tensor_tensor(r1, r1, r2, ALU.subtract)
                dve.drain()
                v.tensor_tensor(r2, x2, cos, ALU.mult)
                dve.drain()
                v.tensor_copy(o1, r1)
                v.tensor_tensor(o2, r2, r3, ALU.add)
                dve.drain()

            v.memset(zpad[:, :, 0:2], 0.0)
            with dve.Fori(0, DEPTH) as l:
                dve.wait_ge(std_ready.sem, std_ready.at(l))
                v.reciprocal(std[:], std[:])
                dve.drain()
                for t in range(T):
                    v.tensor_scalar(K.xn[:, t, :], K.x[:, t, :], std[:, t:t + 1], None, ALU.mult)
                dve.drain().then_inc(xn_ready.sem, 1)
                dve.wait_ge(params.sem, params.at(l, params.n))
                bank = full_of("wsT", l)
                v.tensor_tensor(ws_t[:], bank[:].rearrange("p (g n) -> p g n", g=SG_G), broadcast(K.head[:], 1, SG_G), ALU.mult)\
                    .then_inc(B["wsT"].free, 1)
                dve.drain().then_inc(wst_ready.sem, 1)
                for g in range(4):
                    bank = full_of(("xT", g), l)
                    for j in range(2):
                        k = 2 * g + j
                        ins = v.tensor_scalar(K.h_t[:, k, :], bank[:, j * SEQ:(j + 1) * SEQ], norm_g[:, k:k + 1], None, ALU.mult)
                    ins.then_inc(B["xT", g].free, 1)
                dve.drain().then_inc(ht_ready.sem, 1)
                dve.wait_ge(vec_ready.sem, vec_ready.at(l))
                dve.wait_ge(cbr_ready.sem, cbr_ready.at(l))
                v.tensor_tensor(zpad[:, :, 2:], cbr[:, 2], cbr[:, 0], ALU.mult)
                dve.drain()
                for k in range(3):
                    for c in range(2):
                        w = vec_t[:, 2 * k + c:2 * k + c + 1]
                        if k == 0:
                            v.tensor_scalar(cv[:, c, :], zpad[:, c, 0:SEQ], w, None, ALU.mult)
                        else:
                            v.scalar_tensor_tensor(cv[:, c, :], zpad[:, c, k:k + SEQ], w, cv[:, c, :], ALU.mult, ALU.add)
                    dve.drain()
                v.tensor_tensor(cv[:], cv[:], cbr[:, 1], ALU.mult)
                v.tensor_tensor(sig_b[:], sig_b[:], cbr[:, 3], ALU.mult)
                dve.drain()
                v.tensor_tensor(y_t[:, 2:4, :], cv[:], sig_b[:], ALU.mult)
                dve.drain().then_inc(yb_ready.sem, 1)
                dve.wait_ge(nat_ready.sem, nat_ready.at(l))
                v.tensor_reduce(mean_v[:], seg("sv", GW), AX.X, ALU.add)
                dve.drain()
                v.tensor_scalar(mean_v[:], mean_v[:], 1.0 / GW, None, ALU.mult)
                dve.drain()
                for t in range(T):
                    v.tensor_scalar(seg("sv", GW)[:, t, :], seg("sv", GW)[:, t, :], mean_v[:, t:t + 1], None, ALU.subtract)
                dve.drain()
                square_sums(stat[:, :, 11], seg("sv", GW), scr[:, :, 0:GW], GW)
                square_sums(stat[:, :, 0], seg("cq", 256), scr[:, :, 0:256], 256)
                square_sums(stat[:, :, 1], seg("ckv", 128), scr[:, :, 0:128], 128)
                square_sums(stat[:, :, 2], seg("kr", MLA_ROPE), scr[:, :, 0:MLA_ROPE], MLA_ROPE)
                moba = nat[:, :, NAT["mq"]:NAT["mq"] + 512].rearrange("p t (h n) -> p t h n", n=MOBA_HD)
                square_sums(stat[:, :, 3:11], moba, scr[:].rearrange("p t (h n) -> p t h n", n=MOBA_HD), MOBA_HD)
                dve.drain().then_inc(stat_ready.sem, 1)
                dve.wait_ge(stat_std_ready.sem, stat_std_ready.at(l))
                v.reciprocal(stat[:], stat[:])
                dve.drain()
                for i, (name, n, gain) in enumerate((("cq", 256, gain_cq), ("ckv", 128, gain_ckv), ("kr", MLA_ROPE, gain_kr))):
                    for t in range(T):
                        v.scalar_tensor_tensor(seg(name, n)[:, t, :], seg(name, n)[:, t, :], stat[:, t, i:i + 1], gain[:],
                                               ALU.mult, ALU.mult)
                dve.drain().then_inc(c_ready.sem, 1)
                v.tensor_tensor(moba, moba, broadcast(stat[:, :, 3:11], 3, MOBA_HD), ALU.mult)
                dve.drain()
                for w in range(2):
                    part = moba[:, :, 4 * w:4 * w + 4, :]
                    v.tensor_tensor(part, part, broadcast(broadcast(gain_moba[:, w, :], 1, 4), 1, T), ALU.mult)
                dve.drain()
                x1, x2 = moba[:, :, :, 0:8], moba[:, :, :, 8:16]
                rotate(x1, x2, x1, x2, ROPES[2][0], 8, 8)
                dve.drain().then_inc(moba_ready.sem, 1)
                for t in range(T):
                    v.scalar_tensor_tensor(seg("sv", GW)[:, t, :], seg("sv", GW)[:, t, :], stat[:, t, 11:12], sg_gain[:],
                                           ALU.mult, ALU.mult)
                dve.drain()
                v.tensor_tensor(seg("sv", GW), seg("sv", GW), broadcast(sg_bias[:], 1, T), ALU.add)
                dve.drain().then_inc(vn_ready.sem, 1)
                krs = seg("kr", MLA_ROPE)
                rotate(krs[:, :, 0:16], krs[:, :, 16:32], kr[:, :, 0:16], kr[:, :, 16:32], ROPES[1][0], None, 16)
                dve.wait_ge(qkv_ready.sem, qkv_ready.at(l))
                for t in range(T):
                    square_sums(stat2[:, t, 0:4], q_nat[:, t], scr[:, 0, 0:MLA_H * MLA_QK].rearrange("p (h n) -> p h n", h=MLA_H), MLA_QK)
                    square_sums(stat2[:, t, 4:8], kv_nat[:, t, :, 0:64], scr[:, 0, 0:MLA_H * 64].rearrange("p (h n) -> p h n", h=MLA_H), 64)
                dve.drain().then_inc(stat2_ready.sem, 1)
                dve.wait_ge(stat2_std_ready.sem, stat2_std_ready.at(l))
                v.reciprocal(stat2[:], stat2[:])
                dve.drain()
                for t in range(T):
                    v.tensor_tensor(q_nat[:, t], q_nat[:, t], broadcast(stat2[:, t, 0:4], 2, MLA_QK), ALU.mult)
                    v.tensor_tensor(k_nat[:, t, :, 0:64], kv_nat[:, t, :, 0:64], broadcast(stat2[:, t, 4:8], 2, 64), ALU.mult)
                    v.tensor_copy(k_nat[:, t, :, 64:], broadcast(kr[:, t, :], 1, MLA_H))
                dve.drain()
                for t in range(T):
                    v.tensor_tensor(q_nat[:, t], q_nat[:, t], broadcast(gain_q[:], 1, MLA_H), ALU.mult)
                    v.tensor_tensor(k_nat[:, t, :, 0:64], k_nat[:, t, :, 0:64], broadcast(gain_kn[:], 1, MLA_H), ALU.mult)
                dve.drain()
                q1, q2 = q_nat[:, :, :, 64:80], q_nat[:, :, :, 80:96]
                rotate(q1, q2, q1, q2, ROPES[1][0], MLA_H, 16)
                dve.drain().then_inc(mla_ready.sem, 1)
                dve.wait_ge(sig_acd_ready.sem, sig_acd_ready.at(l))
                for i, name in enumerate(("ga", "gc", "gd")):
                    v.tensor_tensor(sig[:, i], sig[:, i], seg(name, GW), ALU.mult)
                dve.drain()
                for t in range(T):
                    bank = full_of(("mix", t), l)
                    for g in range(SG_G):
                        col = slice(g * 64, (g + 1) * 64)
                        ins = v.scalar_tensor_tensor(y_nat[:, t, 1, col], bank[:, col], vec_t[:, 6 + g:7 + g],
                                                     seg("su", GW)[:, t, col], ALU.add, ALU.mult)
                    ins.then_inc(B["mix", t].free, 1)
                dve.drain()
                v.tensor_tensor(y_nat[:, :, 1], y_nat[:, :, 1], sig[:, 1], ALU.mult)
                for r0, groups in ((0, [("sm1", 0), ("sm1", 1)]), (MLA_H, [("sb1", 0), ("sb1", 1)])):
                    if r0:
                        src = full_of("sm0", l)[:].rearrange("p (h n) -> p h n", h=4)
                        v.tensor_tensor(e0[:, 0:4, :], src, broadcast(K.causal_neg[:], 1, 4), ALU.add).then_inc(B["sm0"].free, 1)
                    for i, name in enumerate(groups):
                        src = full_of(name, l)[:].rearrange("p (h n) -> p h n", h=2)
                        dst = e1[:, r0 + 2 * i:r0 + 2 * i + 2, :]
                        v.tensor_copy(dst[:, :, 0:P], src[:, :, 0:P])
                        v.tensor_tensor(dst[:, :, P:SEQ], src[:, :, P:SEQ], broadcast(K.causal_neg[:], 1, 2), ALU.add)\
                            .then_inc(B[name].free, 1)
                for par in range(2):
                    src = full_of(("sb0", par), l)[:, 0:2 * P].rearrange("p (h n) -> p h n", h=2)
                    v.tensor_tensor(e0[:, MLA_H + 2 * par:MLA_H + 2 * par + 2, :], src, broadcast(K.causal_neg[:], 1, 2), ALU.add)\
                        .then_inc(B["sb0", par].free, 1)
                dve.drain()
                v.tensor_reduce(row16[:, 0, 0:HEADS_2], e1[:], AX.X, ALU.max)
                v.tensor_reduce(row16[:, 0, HEADS_2:], e0[:], AX.X, ALU.max)
                dve.drain()
                for r0 in (0, HEADS_2):
                    v.tensor_scalar(row16[:, 0, r0:r0 + 4], row16[:, 0, r0:r0 + 4], -MLA_QK ** -0.5, None, ALU.mult)
                    v.tensor_scalar(row16[:, 0, r0 + 4:r0 + 8], row16[:, 0, r0 + 4:r0 + 8], -MOBA_HD ** -0.5, None, ALU.mult)
                dve.drain().then_inc(max_ready.sem, 1)
                dve.wait_ge(exp_ready.sem, exp_ready.at(l))
                v.reciprocal(row16[:, 2, :], row16[:, 1, :])
                dve.drain()
                for e, c, n in ((e1[:], 0, SEQ), (e0[:], HEADS_2, P)):
                    v.tensor_tensor(e, e, broadcast(row16[:, 2, c:c + HEADS_2], 2, n), ALU.mult)
                dve.drain().then_inc(a_ready.sem, 1)
                for t in range(T):
                    bank = full_of(("o", t), l)
                    v.tensor_tensor(y_nat[:, t, 0], bank[:, 0:GW], sig[:, 0, t], ALU.mult)
                    v.tensor_tensor(y_nat[:, t, 2], bank[:, GW:2 * GW], sig[:, 2, t], ALU.mult).then_inc(B["o", t].free, 1)
                dve.drain().then_inc(y_ready.sem, 1)
                for h in range(2):
                    for t in range(T):
                        col = slice(h * CHUNK, (h + 1) * CHUNK)
                        bank = full_of(("wo", h, t), l)
                        v.tensor_tensor(K.x[:, t, col], K.x[:, t, col], bank[:], ALU.add).then_inc(B["wo", h, t].free, 1)
                dve.drain().then_inc(x_out.sem, 1)


class Kept:
    pass


def build(nc, A, out):
    with ExitStack() as ctx:
        K = Kept()

        def keep(name, shape, dt=F32):
            return ctx.enter_context(nc.sbuf_tensor(name, shape, dt))

        K.x = keep("x_tokens", [P, T, D])
        K.xn = keep("xn", [P, T, D])
        K.h_t = keep("h_t", [P, KT, SEQ])
        ring = keep("weight_ring", [P, RING, KT, CHUNK])
        K.slots = [ring[:, s] for s in range(RING)]
        K.ident = keep("ident", [P, P])
        K.ones = keep("ones", [P, P])
        K.mean_conv = keep("mean_conv", [P, P])
        K.causal_neg = keep("causal_neg", [P, P])
        K.strict_neg = keep("strict_neg", [P, P])
        K.strict_01 = keep("strict_01", [P, P])
        K.tail = keep("tail", [P, P])
        K.head = keep("head", [P, P])
        K.lower8 = keep("lower8", [P, N_GROUPS, N_GROUPS])
        K.eps = keep("eps", [P, 1])
        K.lam_init = keep("lam_init", [P, DEPTH])
        K.lam_rest = keep("lam_rest", [P, DEPTH])
        K.sin = keep("sin", [P, T, N_FREQ])
        K.cos = keep("cos", [P, T, N_FREQ])
        K.c_act = keep("c_act", [P, KT])
        K.ramp = keep("ramp", [P, SLOTS + 1])
        K.part = keep("part", [P, 1])
        K.strict_twice = keep("strict_twice", [P, 2, N_EXPERTS])
        K.minus_slots = keep("minus_slots", [P, P])
        K.full_rounds = keep("full_rounds", [P, ROUNDS])
        K.table = keep("block_table", [P, BLOCK_COLS], I32)
        K.last_turn = keep("last_turn", [P, DEPTH], I32)
        K.first_turn = keep("first_turn", [P, DEPTH + 1], I32)
        K.first_turn_f = keep("first_turn_f", [P, DEPTH + 1])
        psum = ctx.enter_context(nc.psum_tensor("banks", [P, BANKS, 512], F32))
        K.psum = [psum[:, b] for b in range(BANKS)]
        constants(nc, A, K)
        first_block(nc, A, K)
        second_block(nc, A, K, out)


INPUTS = [
    "x", "c", "positions", "w_mod", "b_mod", "norm_mix_g", "norm_ffn_g", "w_in", "qn_g", "kn_g", "lam_q1", "lam_k1",
    "lam_q2", "lam_k2", "subln_g", "w_proj_a", "w_dw", "b_dw", "conv_ln_g", "conv_ln_b", "w_proj_b", "b_proj_b",
    "w_proj_c", "w_out", "w_router", "b_router", "w1", "w3", "w2", "ws1", "ws3", "ws2", "positions_2", "norm_g_2",
    "w_in_2", "mla_q_norm_g_2", "mla_w_uq_2", "mla_kv_norm_g_2", "mla_w_ukv_2", "mla_q_g_2", "mla_k_nope_g_2",
    "mla_k_rope_g_2", "conv_w_2", "sg_ln_g_2", "sg_ln_b_2", "sg_w_2", "sg_b_2", "moba_q_g_2", "moba_k_g_2", "w_out_2",
]


def kernel(**inputs):
    from concourse import bacc
    from concourse.bass_utils import run_bass_kernel_spmd

    nc = bacc.Bacc("TRN2", target_bir_lowering=False, num_devices=1)
    arrays, A = {}, {}
    for name in INPUTS:
        a = np.ascontiguousarray(inputs[name])
        arrays[f"in_{name}"] = a
        A[name] = nc.dram_tensor(f"in_{name}", a.shape, mybir.dt.from_np(a.dtype), kind="ExternalInput").ap()
    out = nc.dram_tensor("out", (1, SEQ, D), F32, kind="ExternalOutput").ap()
    build(nc, A, out)
    result = run_bass_kernel_spmd(nc, [arrays], core_ids=[0])
    return result.results[0]["out"]
```

```python
from contextlib import ExitStack
import math

import numpy as np
import concourse.bass as bass
from concourse import mybir

F32 = mybir.dt.float32
I32 = mybir.dt.int32
BF16 = mybir.dt.bfloat16
ALU = mybir.AluOpType
ACT = mybir.ActivationFunctionType
AX = mybir.AxisListType

P = 128
T = 2
SEQ = T * P
D = 1024
KT = D // P
DEPTH = 2
EPS = 1e-6
NEG = -1e30
CHUNK = 512
RING = 4
BANKS = 8

DA_HEADS, DA_HD = 4, 64
SB_HEADS, SB_HD = 8, 64
CONV_CH, TAPS = 512, 31
CT = CONV_CH // P
N_EXPERTS, N_GROUPS, TOPK_GROUPS, TOP_K, FF = 64, 8, 4, 8, 256
PER_GROUP = N_EXPERTS // N_GROUPS
ROUTED_SCALE = 2.5
UNROLL = 4
PAIRS = UNROLL // 2
SLOTS = 64
ROUNDS = SEQ // SLOTS - 1
EXTRA = SEQ * TOP_K // SLOTS
MAX_BLOCKS = N_EXPERTS + EXTRA
BLOCK_COLS = MAX_BLOCKS + 2 * UNROLL
PARTS = 3
MOD_CHUNKS = 6 * D // CHUNK

COLS_1 = {"qa": 0, "ka": 512, "va": 1024, "ug": 2048, "ua": 1536, "qc": 2560, "kc": 3072, "vc": 3584, "gt": 4096}
MOD_COL_PARTS = [0, 1, 3, 4]
MOD_ROW_PARTS = [2, 5]
MOD_ROWS = 32
MOD_GROUPS = P // MOD_ROWS
MOD_FIRST = 4
BRANCHES = [2, 0, 1]

MLA_H, MLA_NOPE, MLA_ROPE, MLA_QK = 4, 64, 32, 96
MOBA_H, MOBA_HD, MOBA_ROT = 4, 64, 16
SG_G, GW = 4, 256
D_IN_2 = 3488
NAT = {"cq": 0, "ckv": 256, "kr": 384, "ga": 416, "su": 672, "sv": 928, "gc": 1184, "mq": 1440, "mk": 1696,
       "mv": 1952, "gd": 2208}
NAT_COLS = 2464
CHUNKS_2 = [("n0", 0, 512, 0), ("n3", 2208, 512, 1184), ("n4", 2720, 512, 1696), ("n2", 1696, 512, 672),
            ("t0", 672, 512, None), ("t1", 1184, 512, None), ("n1", 512, 160, 512), ("n5", 3232, 256, 2208)]
ROPES = [(0, 32, 0), (32, 16, 1), (48, 8, 1)]
N_FREQ = 56


class Signal:

    def __init__(self, sem, per_layer=1, credit=0):
        self.sem, self.n, self.credit = sem, per_layer, credit

    def at(self, layer, k=1):
        return layer * self.n + (self.credit + k)


class Use:

    def __init__(self, tile, full, free, k_full, k_free):
        self.tile, self._full, self._free, self.k_full, self.k_free = tile, full, free, k_full, k_free
        self.full, self.free = full.sem, free.sem

    def free_at(self, layer):
        return self._free.at(layer, self.k_free)

    def consumed_at(self, layer):
        return self._free.at(layer, self.k_free + 1)

    def full_at(self, layer):
        return self._full.at(layer, self.k_full + 1)

    def full_before(self, layer):
        return self._full.at(layer, self.k_full + 1 - self._full.n)


class Chunk:

    def __init__(self, tile, filled, cum):
        self.tile, self._filled, self.cum, self.filled = tile, filled, cum, filled.sem

    def filled_at(self, layer):
        return self._filled.at(layer, self.cum)


def bank_plan(names, psum, sem, tag):
    fulls, frees = [0] * BANKS, [0] * BANKS
    places = []
    for i, name in enumerate(names):
        b = i % BANKS
        key = name if isinstance(name, str) else name[0]
        places.append((name, b, fulls[b], frees[b]))
        if not key.startswith("-"):
            frees[b] += 1
            if not key.startswith("="):
                fulls[b] += 1
    full = [Signal(sem(f"bank{b}_full_{tag}"), fulls[b], fulls[b]) for b in range(BANKS)]
    free = [Signal(sem(f"bank{b}_free_{tag}"), frees[b], 1) for b in range(BANKS)]
    uses = {name: Use(psum[b], full[b], free[b], kf, ke) for name, b, kf, ke in places}
    return uses, full, free


def broadcast(ap, axis, n):
    a = ap.unsqueeze(axis)
    shape = list(a.shape)
    shape[axis] = n
    return a.to_broadcast(shape)


def constants(nc, A, K, scratch, sem):
    two_pi = 2 * math.pi
    c1 = 6.28125
    c2 = float(np.float32(round((two_pi - c1) * 2 ** 21) / 2 ** 21))
    c3 = two_pi - c1 - c2
    magic = 1.5 * 2 ** 23
    pi_in = 3.1415925
    at = [0]

    def sb(*shape, dt=F32):
        n = int(np.prod(shape))
        piece = scratch[:, at[0]:at[0] + n]
        at[0] += n
        piece = piece if dt == F32 else piece.bitcast(dt)
        return piece.rearrange("p (a b) -> p a b", b=shape[1]) if len(shape) == 2 else piece

    pos_i, pos_f = sb(2, T, dt=I32), sb(2, T)
    inv = sb(N_FREQ)
    ang, turns, red, wrap = (sb(T, N_FREQ) for _ in range(4))
    c_col, c_sig = sb(KT), sb(KT)
    ramp_i, part_i = sb(SLOTS + 1, dt=I32), sb(1, dt=I32)
    loaded, inv_ready, ang_ready, c_loaded, c_sig_ready, x_loaded = [
        sem(n) for n in ("loaded", "inv_ready", "ang_ready", "c_loaded", "c_sig_ready", "x_loaded")]
    turns_zeroed, masks_ready, c_act_ready, tables_ready = [
        sem(n) for n in ("turns_zeroed", "masks_ready", "c_act_ready", "tables_ready")]

    def sync_part(sp):
        for w, name in enumerate(("positions", "positions_2")):
            with nc.allow_non_contiguous_dma(reason="256 positions, one per partition"):
                sp.dma_start(pos_i[:, w, :], A[name].rearrange("o (t p) -> p (o t)", p=P)).then_inc(loaded, 16)
        sp.dma_start(c_col[:], A["c"].rearrange("o (p k) -> p (o k)", k=KT)).then_inc(c_loaded, 16)
        for t in range(T):
            sp.dma_start(K.x[:, t, :], A["x"][0, t * P:(t + 1) * P, :]).then_inc(x_loaded, 16)
        sp.wait_ge(turns_zeroed, 1)

    def pool_part(pool):
        nc.gpsimd.memset(K.first_turn[:], 0)
        pool.drain().then_inc(turns_zeroed, 1)
        for (first, count, _), theta, dim in zip(ROPES, (10000.0, 500000.0, 500000.0), (64, 32, 16)):
            for i in range(count):
                value = float(np.float32(theta) ** np.float32(-2.0 * i / dim))
                last = nc.gpsimd.memset(inv[:, first + i:first + i + 1], value)
        last.then_inc(inv_ready, 1)
        nc.gpsimd.memset(K.eps[:], EPS)
        nc.gpsimd.memset(K.ones[:], 1.0)
        nc.gpsimd.memset(K.mean_conv[:], 1.0 / CONV_CH)
        for m in (K.ident, K.causal_neg, K.strict_neg):
            nc.gpsimd.memset(m[:], 0.0)
        for layer in range(DEPTH):
            li = 0.8 - 0.6 * math.exp(-0.3 * layer)
            nc.gpsimd.memset(K.lam_init[:, layer:layer + 1], li)
            nc.gpsimd.memset(K.lam_rest[:, layer:layer + 1], 1.0 - li)
        nc.gpsimd.memset(K.lower8[:], 1.0)
        nc.gpsimd.iota(K.table[:], pattern=[[1, BLOCK_COLS]], base=0, channel_multiplier=0)
        nc.gpsimd.memset(K.first_turn_f[:], 0.0)
        nc.gpsimd.iota(ramp_i[:], pattern=[[1, SLOTS + 1]], base=0, channel_multiplier=0)
        nc.gpsimd.iota(part_i[:], pattern=[[0, 1]], base=0, channel_multiplier=1)
        nc.gpsimd.memset(K.minus_slots[:], -float(SLOTS))
        nc.gpsimd.memset(K.part_share[:], 1.0 / MOD_ROWS)
        for r in range(ROUNDS):
            nc.gpsimd.memset(K.full_rounds[:, r:r + 1], float((r + 1) * SLOTS))
        pool.drain()
        nc.gpsimd.tensor_copy(K.ramp[:], ramp_i[:])
        nc.gpsimd.tensor_copy(K.part[:], part_i[:])
        for g in range(2):
            nc.gpsimd.affine_select(out=K.strict_twice[:, g, :], in_=K.ones[:, 0:N_EXPERTS], compare_op=ALU.is_gt, fill=0.0,
                                    base=0, pattern=[[1, N_EXPERTS]], channel_multiplier=-1)
        square = [[-1, P]]
        nc.gpsimd.affine_select(out=K.ident[:], in_=K.ident[:], compare_op=ALU.not_equal, fill=1.0, base=0,
                                pattern=square, channel_multiplier=1)
        nc.gpsimd.affine_select(out=K.causal_neg[:], in_=K.causal_neg[:], compare_op=ALU.is_ge, fill=NEG, base=0,
                                pattern=square, channel_multiplier=1)
        nc.gpsimd.affine_select(out=K.strict_neg[:], in_=K.strict_neg[:], compare_op=ALU.is_gt, fill=NEG, base=0,
                                pattern=[[1, P]], channel_multiplier=-1)
        nc.gpsimd.affine_select(out=K.strict_01[:], in_=K.ones[:], compare_op=ALU.is_gt, fill=0.0, base=0,
                                pattern=[[1, P]], channel_multiplier=-1)
        nc.gpsimd.affine_select(out=K.tail[:], in_=K.ones[:], compare_op=ALU.is_ge, fill=0.0, base=0,
                                pattern=square, channel_multiplier=1)
        nc.gpsimd.affine_select(out=K.head[:], in_=K.ones[:], compare_op=ALU.is_ge, fill=0.0, base=0,
                                pattern=[[1, P]], channel_multiplier=-1)
        nc.gpsimd.affine_select(out=K.lower8[:], in_=K.lower8[:], compare_op=ALU.is_gt, fill=0.0, base=0,
                                pattern=[[1, N_GROUPS], [-1, N_GROUPS]], channel_multiplier=0)
        pool.drain().then_inc(masks_ready, 1)

    def vector_part(dve):
        dve.wait_ge(c_sig_ready, 1)
        nc.vector.tensor_tensor(K.c_act[:], c_col[:], c_sig[:], ALU.mult)
        dve.drain().then_inc(c_act_ready, 1)
        dve.wait_ge(loaded, 32)
        nc.vector.tensor_copy(pos_f[:], pos_i[:])
        dve.drain()
        dve.wait_ge(inv_ready, 1)
        for first, count, which in ROPES:
            for t in range(T):
                nc.vector.tensor_scalar(ang[:, t, first:first + count], inv[:, first:first + count],
                                        pos_f[:, which, t:t + 1], None, ALU.mult)
        dve.drain()
        nc.vector.tensor_scalar(turns[:], ang[:], 1.0 / two_pi, magic, ALU.mult, ALU.add)
        dve.drain()
        nc.vector.tensor_scalar(turns[:], turns[:], magic, None, ALU.subtract)
        dve.drain()
        nc.vector.scalar_tensor_tensor(red[:], turns[:], -c1, ang[:], ALU.mult, ALU.add)
        dve.drain()
        nc.vector.scalar_tensor_tensor(ang[:], turns[:], -c2, red[:], ALU.mult, ALU.add)
        dve.drain()
        nc.vector.scalar_tensor_tensor(red[:], turns[:], -c3, ang[:], ALU.mult, ALU.add)
        dve.drain()
        nc.vector.tensor_scalar(ang[:], red[:], math.pi / 2, None, ALU.add)
        dve.drain()
        nc.vector.tensor_scalar(wrap[:], ang[:], math.pi, -two_pi, ALU.is_gt, ALU.mult)
        dve.drain()
        nc.vector.tensor_tensor(ang[:], ang[:], wrap[:], ALU.add)
        nc.vector.tensor_scalar(red[:], red[:], pi_in, -pi_in, ALU.min, ALU.max)
        dve.drain()
        nc.vector.tensor_scalar(ang[:], ang[:], pi_in, -pi_in, ALU.min, ALU.max)
        dve.drain().then_inc(ang_ready, 1)
        dve.wait_ge(masks_ready, 1)
        dve.wait_ge(tables_ready, 1)

    def scalar_part(act):
        act.wait_ge(c_loaded, 16)
        nc.scalar.activation(c_sig[:], c_col[:], ACT.Sigmoid).then_inc(c_sig_ready, 1)
        act.wait_ge(ang_ready, 1)
        nc.scalar.activation(K.sin[:], red[:], ACT.Sin)
        nc.scalar.activation(K.cos[:], ang[:], ACT.Sin)
        act.drain().then_inc(tables_ready, 1)
        act.wait_ge(x_loaded, 16 * T)
        act.wait_ge(masks_ready, 1)

    def tensor_part(pe):
        pe.wait_ge(masks_ready, 1)
        pe.wait_ge(c_act_ready, 1)

    return sync_part, pool_part, vector_part, scalar_part, tensor_part


def branch_groups(i, h, t):
    return [("gt", i, h, t), ("y", i, h, t)]


MOD_STEPS = {
    "start": [("part", 0), ("part", 1), ("sum", 0), ("part", 2), ("sum", 1), ("part", 3), ("sum", 2), ("sum", 3)],
    "z": [("part", 4)], "qa": [("part", 5)], "ka": [("part", 6)],
    "aT": [("sum", 4), ("sum", 5), ("part", 7), ("sum", 6)],
    "oa": [("part", 8), ("sum", 7), ("part", 9), ("sum", 8)],
    "oaT": [("part", 10), ("sum", 9), ("part", 11), ("sum", 10), ("sum", 11)],
}


def mod_groups(steps):
    return [("mod_" + what, c) for what, c in steps]


GROUPS_1 = (
    mod_groups(MOD_STEPS["start"]) + ["vec"] + [("xT", 0, g) for g in range(4)]
    + [(n, i) for n in ("ug", "ua", "qc", "kc") for i in range(2)]
    + [("z0", par, i) for par in range(2) for i in range(2)] + [("z1", par) for par in range(2)]
    + mod_groups(MOD_STEPS["z"]) + [("qa", t) for t in range(T)] + mod_groups(MOD_STEPS["qa"])
    + [("ka", t) for t in range(T)] + mod_groups(MOD_STEPS["ka"])
    + [("suf", r, par) for r in range(3) for par in range(2)]
    + [(n, t) for n in ("vc", "va") for t in range(T)]
    + [("oc", i) for i in range(2)]
    + [("qkT", w, i) for w in range(2) for i in range(2)]
    + [("s1", m, i) for m in range(2) for i in range(2)] + [("s0", m) for m in range(2)]
    + [x for h in range(2) for t in range(T) for x in branch_groups(2, h, t)]
    + [("aT1", i) for i in range(2)] + ["aT0"] + mod_groups(MOD_STEPS["aT"])
    + [("oa", t) for t in range(T)] + mod_groups(MOD_STEPS["oa"]) + [("oaT", i) for i in range(2)]
    + mod_groups(MOD_STEPS["oaT"])
    + [x for t in range(T) for x in branch_groups(0, 0, t)] + ["cmean"]
    + branch_groups(0, 1, 0) + ["cvar"] + branch_groups(0, 1, 1)
    + [x for h in range(2) for t in range(T) for x in branch_groups(1, h, t)]
    + [("mT", g) for g in range(4)] + [("wo", h, t) for t in range(T) for h in range(2)]
    + [("xT", 1, g) for g in range(4)] + ["rt"]
    + [("=moe_y", t, h) for t in range(T) for h in range(2)] + ["-moe_h", "-moe_x"] + [("-moe_o", h) for h in range(2)]
)
GROUPS_1 += ["-pad"] * (-len(GROUPS_1) % BANKS)

def branch_chunks(i):
    return [(("gt", i, 0), ("gt", i, 0, 1)), (("p", i), ("y", i, 1, 1)), (("gt", i, 1), ("gt", i, 1, 1))]


def mod_chunks(*chunks):
    return [(("mod", c), ("mod_part", c)) for c in chunks]


CHUNKS_1 = (
    mod_chunks(*range(MOD_FIRST)) + [(n, (n, 1)) for n in ("ug", "ua", "qc", "kc")]
    + mod_chunks(4) + [("qa", ("qa", 1))] + mod_chunks(5) + [("ka", ("ka", 1))] + mod_chunks(6)
    + [(n, (n, 1)) for n in ("vc", "va")] + branch_chunks(2) + mod_chunks(*range(7, MOD_CHUNKS))
    + branch_chunks(0) + branch_chunks(1)
    + [(("wo", h), ("wo", h, 1)) for h in range(2)] + [("shared", None)]
)
assert len(CHUNKS_1) % RING == 0 and N_EXPERTS % UNROLL == 0 and UNROLL == RING


def first_block(nc, A, K):
    ds = bass.ds
    with ExitStack() as ctx:
        def sb(name, shape, dt=F32):
            return ctx.enter_context(nc.sbuf_tensor(name, shape, dt))

        def sem(name):
            return ctx.enter_context(nc.semaphore(name))

        def signal(name, per_layer=1, credit=0):
            return Signal(sem(name), per_layer, credit)

        norm_g = sb("norm_g", [P, 2, KT])
        mod_b = sb("mod_b", [P, 4, KT])
        gain_qk = sb("gain_qk", [P, 2, DA_HD])
        lam4 = sb("lam4", [P, 4, DA_HD])
        subln = sb("subln", [P, 2 * DA_HD])
        dw_rows = sb("dw_rows", [TAPS * CT, P])
        ch_rows = sb("ch_rows", [3 * CT, P])
        proj_b_bias = sb("proj_b_bias", [P, D])
        w_rt = sb("w_rt", [P, KT, N_EXPERTS])
        rt_bias = sb("rt_bias", [P, N_EXPERTS])
        gate = sb("gate", [P, 2, D])
        col4 = sb("col4", [P, 4, 2, KT])
        mod_col = sb("mod_col", [P, 4, KT])
        vec_t = sb("vec_t", [P, TAPS * CT + 3 * CT])
        std = sb("std", [P, T])
        sq_sum = sb("sq_sum", [P, T])
        hpad = sb("hpad", [P, CT, TAPS - 1 + SEQ])
        conv = sb("conv", [P, CT, SEQ])
        conv_t = sb("conv_t", [P, CT, SEQ])
        conv_std = sb("conv_std", [P, SEQ])
        qk = sb("qk", [P, T, 2 * 512])
        slots2 = sb("slots2", [P, 2, 2, D])
        work = slots2[:].rearrange("p s f n -> p (s f) n")
        va, vc = (work[:, i].rearrange("p (t n) -> p t n", t=T) for i in range(2))
        qc_t, kc_t = (work[:, i].rearrange("p (c n) -> p c n", c=CT) for i in (2, 3))
        qa_t = sb("qa_t", [P, DA_HEADS, SEQ])
        ka_t = sb("ka_t", [P, DA_HEADS, SEQ])
        z = sb("z", [P, SB_HEADS, SEQ + P])
        sp_ = sb("sp_", [P, SB_HEADS, SEQ + P])
        qk_std = sb("qk_std", [P, T * 16])
        row16 = sb("row16", [P, 3, 16])
        lam_p = sb("lam_p", [P, 2, DA_HD])
        lam_s = sb("lam_s", [P, 2])
        lam_e = sb("lam_e", [P, 2])
        lam = sb("lam", [P, 1])
        gain_o = sb("gain_o", [P, 2 * DA_HD])
        oa_std = sb("oa_std", [P, T * DA_HEADS])
        sig_g = sb("sig_g", [P, 2, CHUNK])
        y_tmp = sb("y_tmp", [P, CHUNK])
        pick = y_tmp[:].rearrange("p (q k) -> p q k", k=KT)
        score = sb("score", [P, T, N_EXPERTS])
        biased = sb("biased", [P, T, N_EXPERTS])
        top = sb("top", [P, T, N_GROUPS, 8])
        g_score = sb("g_score", [P, T, N_GROUPS])
        g_cmp = sb("g_cmp", [P, T, N_GROUPS, N_GROUPS])
        g_eq = sb("g_eq", [P, T, N_GROUPS, N_GROUPS])
        g_rank = sb("g_rank", [P, T, N_GROUPS])
        g_neg = sb("g_neg", [P, T, N_GROUPS])
        top8 = sb("top8", [P, T, 8])
        rest = sb("rest", [P, T, N_EXPERTS])
        w_sum = sb("w_sum", [P, T])
        chosen = sb("chosen", [P, T, 2, N_EXPERTS])
        place_64 = sb("place_64", [P, T, 2, N_EXPERTS])
        place = sb("place", [P, T, 2, BLOCK_COLS])
        more = sb("more", [P, ROUNDS + 1])
        more_below = sb("more_below", [P, ROUNDS + 1])
        extra_at = sb("extra_at", [P, ROUNDS + 1])
        extra_hot = sb("extra_hot", [P, ROUNDS, EXTRA])
        extra_any = sb("extra_any", [P, EXTRA])
        extra_round = sb("extra_round", [P, EXTRA])
        turns_cmp = sb("turns_cmp", [P, EXTRA // UNROLL])
        turns_f = sb("turns_f", [P, 1])
        sig_h = sb("sig_h", [P, T, FF])
        act_h = sb("act_h", [P, T, FF])
        act_t = sb("act_t", [P, T, 2, P])

        mod_buffers = [b[:].rearrange("p t n -> p (t n)") for b in (sig_h, act_h)] + [act_t[:].rearrange("p t f n -> p (t f n)")]
        mod_part = {c: mod_buffers[(c % 2) if c < MOD_FIRST else (c - MOD_FIRST) % 3] for c in range(MOD_CHUNKS)}

        z_flat = z[:].rearrange("p h n -> p (h n)")
        e1 = z_flat[:, 0:8 * SEQ].rearrange("p (h n) -> p h n", h=8)
        e0 = z_flat[:, 8 * SEQ:8 * SEQ + 8 * P].rearrange("p (h n) -> p h n", h=8)
        a_t = sp_[:].rearrange("p h n -> p (h n)")[:, 0:DA_HEADS * 3 * P].rearrange("p (h b n) -> p h b n", h=DA_HEADS, b=3)
        oa = qa_t[:].rearrange("p h n -> p (h n)").rearrange("p (t n) -> p t n", t=T)
        oa_t = ka_t
        yc_t = kc_t
        yb_t = conv
        merged = qk
        m_t = K.h_t
        qk_rot = K.xn[:].rearrange("p t (h n) -> p t h n", n=DA_HD)
        qk_heads = qk[:].rearrange("p t (h n) -> p t h n", n=DA_HD)
        cut, at = [], T * D
        for n in (2 * T * 2 * SLOTS, 2 * T * SLOTS // 2, FF // 2, FF // 2):
            cut.append(z_flat[:, at:at + n])
            at += n
        assert at <= SB_HEADS * (SEQ + P)
        spread = cut[0].rearrange("p (i t b s) -> p i t b s", i=2, t=T, b=2)
        pick_hot = cut[1].bitcast(BF16).rearrange("p (b t s) -> p b t s", b=2, t=T)
        sig_blk, act_blk = cut[2:4]
        x_blk = qa_t[:].rearrange("p h n -> p (h n)").rearrange("p (b k s) -> p b k s", b=2, k=KT)
        place_t = ka_t[:].rearrange("p h n -> p (h n)")[:, 0:T * P].rearrange("p (t n) -> p t n", t=T)
        turned = conv[:].rearrange("p c n -> p (c n)").rearrange("p (i b n) -> p i b n", i=2, b=2)
        o_blk = conv_t[:].rearrange("p c n -> p (c n)")
        w2_slots = [slots2[:, 0], slots2[:, 1], qk[:].rearrange("p t n -> p (t n)").rearrange("p (f n) -> p f n", f=2),
                    z_flat[:, 0:T * D].rearrange("p (f n) -> p f n", f=2)]
        xn_parts = sp_[:].rearrange("p h n -> p (h n)").bitcast(BF16).rearrange("p (t c k q) -> p t c k q", t=T, c=PARTS, k=KT)
        xn_rest = qk[:].rearrange("p t (k q) -> p t k q", k=KT)
        oa_heads = oa.rearrange("p t (h n) -> p (t h) n", n=2 * DA_HD)

        B, full, free = bank_plan(GROUPS_1, K.psum, sem, "1")
        filled = [Signal(sem(f"slot{s}_filled")) for s in range(RING)]
        C, loads, arrived = {}, [], [0] * RING
        for i, (name, reader) in enumerate(CHUNKS_1):
            s = i % RING
            arrived[s] += 32 if name in ("shared", "qa") else 16
            C[name] = Chunk(K.slots[s], filled[s], arrived[s])
            loads.append((name, s, CHUNKS_1[i - RING][1] if i >= RING else None, reader))
        for s in range(RING):
            filled[s].n = arrived[s]
        shared2_filled = Signal(sem("shared_w2_filled"), 16)
        w13_filled = [sem(f"slot{s}_w13_filled") for s in range(RING)]
        w2_filled = [sem(f"w2_slot{s}_filled") for s in range(RING)]

        N_PARAMS = 2 + len(MOD_COL_PARTS) + 2 + 4 + 1 + 1 + 3 + 1 + 1 + 1
        params = signal("params_loaded", 16 * N_PARAMS)
        gate_loaded = signal("gate_bias_loaded", 16 * len(MOD_ROW_PARTS))
        x_mid, x_out = signal("x_after_mixer", T), signal("x_after_layer", T, T)
        std_ready = [signal(f"x_std_ready{i}", T) for i in range(2)]
        xn_ready = [signal(f"xn_ready{i}", T) for i in range(2)]
        ht_ready = [signal(f"ht_ready{i}") for i in range(2)]
        ug_ready = signal("ug_sigmoid_ready", 2)
        qk_ready, qkc_ready, v_ready = signal("qk_ready"), signal("qkc_t_ready"), signal("v_ready")
        qk_sq_ready, qk_std_ready, qk_rot_ready = signal("qk_sq_ready"), signal("qk_std_ready"), signal("qk_rot_ready")
        log_ready, sp_ready, d_ready = signal("softplus_log_ready"), signal("softplus_ready"), signal("stick_log_ready")
        qkt_ready = signal("qk_t_ready")
        lam_s_ready = signal("lam_sums_ready")
        max_ready, exp_ready, a_ready, at_ready = (signal("row_max_ready"), signal("exp_ready"), signal("a_ready"),
                                                   signal("a_t_ready"))
        oa_sq_ready, oa_std_ready, oa_ready, oat_ready = (signal("oa_sq_ready"), signal("oa_std_ready"),
                                                          signal("oa_ready"), signal("oa_t_ready"))
        conv_sq_ready, conv_std_ready = signal("conv_sq_ready"), signal("conv_std_ready")
        conv_ln_ready, conv_sig_ready, ybt_ready = signal("conv_ln_ready"), signal("conv_sig_ready"), signal("yb_t_ready")
        sig_ready, y_used = signal("gate_sig_ready", 12), signal("gate_sig_used", 12)
        merged_ready, mt_ready = signal("merged_ready"), signal("merged_t_ready")
        score_ready, chosen_ready = signal("score_ready"), signal("chosen_ready")
        sh_h_done, sh_sig_ready, sh_act_ready, sh_turned, sh_act_t_ready, sh_done = (
            signal(f"shared_{n}", T) for n in ("h_done", "sigmoid_ready", "act_ready", "act_turned", "act_t_ready", "w2_done"))
        count_done, more_ready, index_done = signal("count_done"), signal("more_ready"), signal("index_done")
        extra_ready, place_t_ready, list_done = signal("extra_ready"), signal("place_t_ready"), signal("list_done")
        table_ready, parts_ready = signal("table_ready"), signal("xn_parts_ready")
        hot_ready, gather_done, x_ready, h_done, sig_ready_blk, act_ready, turn_done, turned_ready = (
            sem(f"block_{n}") for n in ("hot_ready", "gather_done", "x_ready", "h_done", "sigmoid_ready", "act_ready",
                                        "turn_done", "turned_ready"))
        o_done, o_ready, added = (sem(f"pair_{n}") for n in ("o_done", "o_ready", "added"))
        wait_carrier = sem("wait_carrier")

        y_bank = [[B["=moe_y", t, h].tile for h in range(2)] for t in range(T)]
        h_bank, x_bank, o_bank, o_bank2 = (B[n].tile for n in ("-moe_h", "-moe_x", ("-moe_o", 0), ("-moe_o", 1)))
        o_banks = [o_bank, o_bank2]
        sh_bank = [h_bank, x_bank]
        sh_turn_bank = [o_bank2, x_bank]
        order = list(GROUPS_1)
        moe_before = [B[order[order.index(n) - BANKS]] for n in ("-moe_h", "-moe_x", ("-moe_o", 0), ("-moe_o", 1))]
        at_count, at_index, at_expert, at_place, at_weight = 128, 132, 136, 168, 256

        def block_count(eng, l):
            last_turn = eng.value_load(K.last_turn[0:1, ds(l, 1)], min_val=0, max_val=MAX_BLOCKS // UNROLL - 1)
            before = eng.value_load(K.first_turn[0:1, ds(l, 1)], min_val=0, max_val=DEPTH * MAX_BLOCKS // UNROLL)

            def nth(it, j):
                return (before + it) * UNROLL + (j + 1)

            def pairs(it, i):
                return (before + it) * PAIRS + (i + 1)

            return last_turn, nth, pairs

        const_sync, const_pool, const_vector, const_scalar, const_tensor = constants(nc, A, K, z_flat, sem)
        block = ctx.enter_context(nc.Block())

        @block.sync
        def _(sp):
            const_sync(sp)
            for b in range(BANKS):
                sp.sem_inc(free[b].sem, 1)
                sp.sem_inc(full[b].sem, full[b].credit)
            sp.sem_inc(h_done, RING)
            sp.sem_inc(x_out.sem, T)

            def expert13(l, e, s):
                for i, name in enumerate(("w1", "w3")):
                    sp.dma_start(K.slots[s][:, 4 * i:4 * i + 4, :].rearrange("p k n -> p (k n)"),
                                 A[name][ds(l, 1), ds(e, 1)].rearrange("a b (p k) n -> p (a b k n)", k=KT))\
                        .then_inc(w13_filled[s], 16)

            def expert2(l, e, s):
                sp.dma_start(w2_slots[s], A["w2"][ds(l, 1), ds(e, 1)].rearrange("a b (f p) n -> p (a b f) n", p=P))\
                    .then_inc(w2_filled[s], 16)

            def parameters(one):
                def load(dst, src):
                    sp.dma_start(dst, src).then_inc(params.sem, 16)

                for i, name in enumerate(("norm_mix_g", "norm_ffn_g")):
                    load(norm_g[:, i, :], A[name][one].rearrange("a (p k) -> p (a k)", k=KT))
                for i, part in enumerate(MOD_COL_PARTS):
                    load(mod_b[:, i, :], A["b_mod"][one, part * D:(part + 1) * D].rearrange("a (p k) -> p (a k)", k=KT))
                for i, name in enumerate(("qn_g", "kn_g")):
                    load(gain_qk[:, i, :], A[name][one].to_broadcast([P, DA_HD]))
                for i, name in enumerate(("lam_q1", "lam_k1", "lam_q2", "lam_k2")):
                    load(lam4[:, i, :], A[name][one].to_broadcast([P, DA_HD]))
                load(subln[:], A["subln_g"][one].to_broadcast([P, 2 * DA_HD]))
                load(dw_rows[:], A["w_dw"][one].rearrange("a k (c p) -> (a k c) p", p=P))
                for i, name in enumerate(("b_dw", "conv_ln_g", "conv_ln_b")):
                    load(ch_rows[i * CT:(i + 1) * CT, :], A[name][one].rearrange("a (c p) -> (a c) p", p=P))
                load(proj_b_bias[:], A["b_proj_b"][one].to_broadcast([P, D]))
                load(w_rt[:], A["w_router"][one].rearrange("a (p k) n -> p (a k) n", k=KT))
                load(rt_bias[:], A["b_router"][one].to_broadcast([P, N_EXPERTS]))

            with sp.Fori(0, DEPTH) as l:
                one = ds(l, 1)
                turns_before = sp.value_load(K.first_turn[0:1, ds(l, 1)], min_val=0, max_val=DEPTH * MAX_BLOCKS // UNROLL)
                for name, s, before, reader in loads:
                    if before is None:
                        sp.wait_ge(h_done, turns_before * UNROLL + (s + 1))
                    else:
                        sp.wait_ge(B[before].full, B[before].full_at(l))
                    slot = K.slots[s]
                    key = name[0] if isinstance(name, tuple) else name
                    if key == "mod":
                        src = A["w_mod"][ds(l, 1), :, name[1] * CHUNK:(name[1] + 1) * CHUNK].rearrange(
                            "a (p k) n -> p (a k) n", k=KT)
                    elif key in ("gt", "ug", "ua", "qa", "ka", "qc", "kc", "va", "vc"):
                        col = COLS_1[key] + (name[1] * D + name[2] * CHUNK if key == "gt" else 0)
                        src = A["w_in"][ds(l, 1), :, col:col + CHUNK].rearrange("a (p k) n -> p (a k) n", k=KT)
                    elif key == "p":
                        slot = slot.rearrange("p k n -> p (k n)").rearrange("p (k n) -> p k n", n=D)
                        src = A[("w_proj_a", "w_proj_b", "w_proj_c")[name[1]]][ds(l, 1)].rearrange(
                            "a (k p) n -> p (a k) n", p=P)
                    elif key == "wo":
                        src = A["w_out"][ds(l, 1), :, name[1] * CHUNK:(name[1] + 1) * CHUNK].rearrange(
                            "a (k p) n -> p (a k) n", p=P)
                    if key == "shared":
                        for i, w in enumerate(("ws1", "ws3")):
                            sp.dma_start(slot[:, 4 * i:4 * i + 4, :].rearrange("p k n -> p (k n)"),
                                         A[w][ds(l, 1)].rearrange("a (p k) n -> p (a k n)", k=KT))\
                                .then_inc(filled[s].sem, 16)
                    elif key == "qa":
                        for half in (slice(P // 2, P), slice(0, P // 2)):
                            sp.dma_start(slot[half], src[half]).then_inc(filled[s].sem, 16)
                    else:
                        sp.dma_start(slot, src).then_inc(filled[s].sem, 16)
                    if name == ("mod", MOD_FIRST - 1):
                        parameters(one)
                    if name == ("mod", MOD_FIRST):
                        sp.wait_ge(x_out.sem, x_out.at(l, 0))
                        sp.sem_inc(wait_carrier, 1)
                        for i, part in enumerate(MOD_ROW_PARTS):
                            sp.dma_start(gate[:, i, :], A["b_mod"][one, part * D:(part + 1) * D].to_broadcast([P, D]))\
                                .then_inc(gate_loaded.sem, 16)
                sp.wait_ge(B["y", 1, 1, 1].full, B["y", 1, 1, 1].full_at(l))
                sp.dma_start(slots2[:, 1].rearrange("p f n -> p (f n)"),
                             A["ws2"][ds(l, 1)].rearrange("a (p f) n -> p (a f n)", f=2)).then_inc(shared2_filled.sem, 16)
                for e in range(UNROLL):
                    before = loads[len(loads) - RING + e][3]
                    if before is None:
                        sp.wait_ge(sh_h_done.sem, sh_h_done.at(l, T))
                    else:
                        sp.wait_ge(B[before].full, B[before].full_at(l))
                    expert13(l, e, e)
                expert2(l, 0, 0)
                sp.wait_ge(sh_done.sem, sh_done.at(l, T))
                expert2(l, 1, 1)
                sp.wait_ge(parts_ready.sem, parts_ready.at(l))
                expert2(l, 2, 2)
                expert2(l, 3, 3)
                sp.wait_ge(table_ready.sem, table_ready.at(l))
                sp.sem_inc(wait_carrier, 1)
                last_turn, nth, pairs = block_count(sp, l)
                with sp.Fori(1, last_turn + 1) as it:
                    for j in range(UNROLL):
                        e = sp.value_load(K.table[0:1, ds(it * UNROLL + j, 1)], min_val=0, max_val=N_EXPERTS - 1)
                        sp.wait_ge(h_done, nth(it, j))
                        sp.sem_inc(wait_carrier, 1)
                        expert13(l, e, j)
                        sp.wait_ge(o_done, pairs(it, j // 2 - PAIRS))
                        sp.sem_inc(wait_carrier, 1)
                        expert2(l, e, j)

        @block.gpsimd
        def _(pool):
            const_pool(pool)
            with pool.Fori(0, DEPTH) as l:
                pool.wait_ge(xn_ready[1].sem, xn_ready[1].at(l, T))
                pool.sem_inc(wait_carrier, 1)
                by_k = K.xn[:].rearrange("p t (q k) -> p t k q", k=KT)
                for c in range(PARTS):
                    for t in range(T):
                        nc.gpsimd.tensor_copy(xn_parts[:, t, c], by_k[:, t] if c == 0 else xn_rest[:, t])
                    pool.drain()
                    if c < PARTS - 1:
                        for t in range(T):
                            nc.gpsimd.tensor_tensor(xn_rest[:, t], by_k[:, t] if c == 0 else xn_rest[:, t], xn_parts[:, t, c],
                                                    ALU.subtract)
                        pool.drain()
                pool.drain().then_inc(parts_ready.sem, 1)

        @block.tensor
        def _(pe):
            def begin(name, l):
                pe.wait_ge(B[name].free, B[name].free_at(l))
                return B[name].tile

            def chunk(name, l):
                pe.wait_ge(C[name].filled, C[name].filled_at(l))
                return C[name].tile

            def rows(name, l, w, t, stationary, cols=CHUNK):
                bank = begin(name, l)
                for k in range(KT):
                    mm = nc.tensor.matmul(bank[:, 0:cols], stationary[:, k, t * P:(t + 1) * P], w[:, k, 0:cols],
                                          start=(k == 0), stop=(k == KT - 1))
                mm.then_inc(B[name].full, 1)

            def columns(name, l, w, i):
                bank = begin(name, l)
                for j in range(2):
                    c = 2 * i + j
                    for k in range(KT):
                        mm = nc.tensor.matmul(bank[:, j * SEQ:(j + 1) * SEQ], w[:, k, c * P:(c + 1) * P], K.h_t[:, k, :],
                                              start=(k == 0), stop=(k == KT - 1))
                mm.then_inc(B[name].full, 1)

            def norm_turn(i, l):
                for t in range(T):
                    pe.wait_ge(xn_ready[i].sem, xn_ready[i].at(l, t + 1))
                    for g in range(4):
                        bank = begin(("xT", i, g), l) if t == 0 else B["xT", i, g].tile
                        for j in range(2):
                            mm = nc.tensor.transpose(bank[:, j * SEQ + t * P:j * SEQ + (t + 1) * P],
                                                     K.xn[:, t, 2 * g + j::KT], K.ident[:])
                        if t == T - 1:
                            mm.then_inc(B["xT", i, g].full, 1)

            const_tensor(pe)
            with pe.Fori(0, DEPTH) as l:
                def mod(place):
                    for what, c in MOD_STEPS[place]:
                        w = chunk(("mod", c), l) if what == "part" else None
                        bank = begin(("mod_" + what, c), l)
                        if what == "part":
                            for j in range(KT // MOD_GROUPS):
                                for g in range(MOD_GROUPS):
                                    k = g * (KT // MOD_GROUPS) + j
                                    mm = nc.tensor.matmul(bank[g * MOD_ROWS:(g + 1) * MOD_ROWS, :],
                                                          K.c_act[:, k:k + 1].to_broadcast([P, MOD_ROWS]), w[:, k, :],
                                                          start=(j == 0), stop=(j == KT // MOD_GROUPS - 1), skip_group_check=True)
                        else:
                            pe.wait_ge(B["mod_part", c].free, B["mod_part", c].consumed_at(l))
                            mm = nc.tensor.matmul(bank[:], K.part_share[:].to_broadcast([P, P]), mod_part[c], start=True, stop=True)
                        mm.then_inc(B["mod_" + what, c].full, 1)

                def branch(i, h, t):
                    feat, ready = ((oa_t, oat_ready), (yb_t, ybt_ready), (yc_t, qkt_ready))[i]
                    rows(("gt", i, h, t), l, chunk(("gt", i, h), l), t, K.h_t)
                    w = chunk(("p", i), l).rearrange("p k n -> p (k n)").rearrange("p (k n) -> p k n", n=D)
                    pe.wait_ge(ready.sem, ready.at(l))
                    bank = begin(("y", i, h, t), l)
                    for k in range(4):
                        mm = nc.tensor.matmul(bank[:], feat[:, k, t * P:(t + 1) * P], w[:, k, h * CHUNK:(h + 1) * CHUNK],
                                              start=(k == 0), stop=(k == 3))
                    mm.then_inc(B["y", i, h, t].full, 1)

                def by_rows(name):
                    w = chunk(name, l)
                    for t in range(T):
                        rows((name, t), l, w, t, K.h_t)

                mod("start")
                pe.wait_ge(params.sem, params.at(l, params.n))
                bank = begin("vec", l)
                nc.tensor.transpose(bank[:, 0:TAPS * CT], dw_rows[:], K.ident[0:TAPS * CT, 0:TAPS * CT])
                nc.tensor.transpose(bank[:, TAPS * CT:(TAPS + 3) * CT], ch_rows[:], K.ident[0:3 * CT, 0:3 * CT])\
                    .then_inc(B["vec"].full, 1)
                norm_turn(0, l)
                pe.wait_ge(ht_ready[0].sem, ht_ready[0].at(l))
                for name in ("ug", "ua", "qc", "kc"):
                    w = chunk(name, l)
                    for i in range(2):
                        columns((name, i), l, w, i)
                pe.wait_ge(qkc_ready.sem, qkc_ready.at(l))
                for par in range(2):
                    part = slice(64 * par, 64 * par + 64)
                    for i in range(2):
                        bank = begin(("z0", par, i), l)
                        for j in range(2):
                            c = 2 * i + j
                            mm = nc.tensor.matmul(bank[:, j * SEQ:(j + 1) * SEQ], kc_t[part, c, 0:P], qc_t[part, c, :],
                                                  start=True, stop=True)
                        mm.then_inc(B["z0", par, i].full, 1)
                for par in range(2):
                    part = slice(64 * par, 64 * par + 64)
                    bank = begin(("z1", par), l)
                    for c in range(CT):
                        mm = nc.tensor.matmul(bank[:, c * P:(c + 1) * P], kc_t[part, c, P:SEQ], qc_t[part, c, P:SEQ],
                                              start=True, stop=True)
                    mm.then_inc(B["z1", par].full, 1)
                mod("z")
                by_rows("qa")
                mod("qa")
                by_rows("ka")
                mod("ka")
                pe.wait_ge(sp_ready.sem, sp_ready.at(l))
                for r, parts in enumerate(([(K.tail, 0)], [(K.tail, P), (K.ones, 2 * P)], [(K.tail, 2 * P)])):
                    for par in range(2):
                        bank = begin(("suf", r, par), l)
                        for n, (m, c) in enumerate(parts):
                            mm = nc.tensor.matmul(bank[:], m[:], sp_[:, 4 * par:4 * par + 4, c:c + P],
                                                  start=(n == 0), stop=(n == len(parts) - 1))
                        mm.then_inc(B["suf", r, par].full, 1)
                by_rows("vc")
                by_rows("va")
                pe.wait_ge(v_ready.sem, v_ready.at(l))
                for i in range(2):
                    bank = begin(("oc", i), l)
                    for j in range(2):
                        for par in range(2):
                            c = 2 * i + j
                            col = (2 * c + par) * SB_HD
                            out = bank[64 * par:64 * par + 64, j * SEQ:(j + 1) * SEQ]
                            nc.tensor.matmul(out, vc[:, 0, col:col + SB_HD], z[:, 4 * par + c, 0:SEQ],
                                             start=True, stop=False, skip_group_check=True)
                            mm = nc.tensor.matmul(out[:, P:SEQ], vc[:, 1, col:col + SB_HD], z[:, 4 * par + c, SEQ:SEQ + P],
                                                  start=False, stop=True, skip_group_check=True)
                    mm.then_inc(B["oc", i].full, 1)

                pe.wait_ge(qk_rot_ready.sem, qk_rot_ready.at(l))
                for w in range(2):
                    for i in range(2):
                        bank = begin(("qkT", w, i), l)
                        for j in range(2):
                            for t in range(T):
                                col = w * 512 + (2 * i + j) * P
                                mm = nc.tensor.transpose(bank[:, j * SEQ + t * P:j * SEQ + (t + 1) * P],
                                                         K.xn[:, t, col:col + P], K.ident[:])
                        mm.then_inc(B["qkT", w, i].full, 1)
                pe.wait_ge(qkt_ready.sem, qkt_ready.at(l))
                for m in range(2):
                    part = slice(64 * m, 64 * m + 64)
                    for i in range(2):
                        bank = begin(("s1", m, i), l)
                        for j in range(2):
                            mm = nc.tensor.matmul(bank[:, j * SEQ:(j + 1) * SEQ], qa_t[part, 2 * i + j, P:SEQ],
                                                  ka_t[part, 2 * i + j, :], start=True, stop=True)
                        mm.then_inc(B["s1", m, i].full, 1)
                for m in range(2):
                    part = slice(64 * m, 64 * m + 64)
                    bank = begin(("s0", m), l)
                    for h in range(DA_HEADS):
                        mm = nc.tensor.matmul(bank[:, h * P:(h + 1) * P], qa_t[part, h, 0:P], ka_t[part, h, 0:P],
                                              start=True, stop=True)
                    mm.then_inc(B["s0", m].full, 1)
                for h in range(2):
                    for t in range(T):
                        branch(2, h, t)
                pe.wait_ge(a_ready.sem, a_ready.at(l))
                for i in range(2):
                    bank = begin(("aT1", i), l)
                    for j in range(2):
                        for b in range(2):
                            mm = nc.tensor.transpose(bank[:, (2 * j + b) * P:(2 * j + b + 1) * P],
                                                     e1[:, 2 * i + j, b * P:(b + 1) * P], K.ident[:])
                    mm.then_inc(B["aT1", i].full, 1)
                bank = begin("aT0", l)
                for h in range(DA_HEADS):
                    mm = nc.tensor.transpose(bank[:, h * P:(h + 1) * P], e0[:, h, :], K.ident[:])
                mm.then_inc(B["aT0"].full, 1)
                mod("aT")
                pe.wait_ge(at_ready.sem, at_ready.at(l))
                for t in range(T):
                    bank = begin(("oa", t), l)
                    for h in range(DA_HEADS):
                        col = slice(h * P, (h + 1) * P)
                        if t == 0:
                            mm = nc.tensor.matmul(bank[:, col], a_t[:, h, 0, :], va[:, 0, col], start=True, stop=True)
                        else:
                            nc.tensor.matmul(bank[:, col], a_t[:, h, 1, :], va[:, 0, col], start=True, stop=False)
                            mm = nc.tensor.matmul(bank[:, col], a_t[:, h, 2, :], va[:, 1, col], start=False, stop=True)
                    mm.then_inc(B["oa", t].full, 1)
                mod("oa")
                pe.wait_ge(oa_ready.sem, oa_ready.at(l))
                for i in range(2):
                    bank = begin(("oaT", i), l)
                    for j in range(2):
                        for t in range(T):
                            mm = nc.tensor.transpose(bank[:, j * SEQ + t * P:j * SEQ + (t + 1) * P],
                                                     oa[:, t, (2 * i + j) * P:(2 * i + j + 1) * P], K.ident[:])
                    mm.then_inc(B["oaT", i].full, 1)

                mod("oaT")
                for t in range(T):
                    branch(0, 0, t)
                bank = begin("cmean", l)
                for c in range(CT):
                    mm = nc.tensor.matmul(bank[:, 0:SEQ], K.mean_conv[:], conv[:, c, :], start=(c == 0), stop=(c == CT - 1))
                mm.then_inc(B["cmean"].full, 1)
                branch(0, 1, 0)
                pe.wait_ge(conv_sq_ready.sem, conv_sq_ready.at(l))
                bank = begin("cvar", l)
                for c in range(CT):
                    mm = nc.tensor.matmul(bank[:, 0:SEQ], K.mean_conv[:], conv_t[:, c, :], start=(c == 0), stop=(c == CT - 1))
                mm.then_inc(B["cvar"].full, 1)
                branch(0, 1, 1)
                for h in range(2):
                    for t in range(T):
                        branch(1, h, t)
                pe.wait_ge(merged_ready.sem, merged_ready.at(l))
                for g in range(4):
                    bank = begin(("mT", g), l)
                    for j in range(2):
                        for t in range(T):
                            k = 2 * g + j
                            mm = nc.tensor.transpose(bank[:, j * SEQ + t * P:j * SEQ + (t + 1) * P],
                                                     merged[:, t, k * P:(k + 1) * P], K.ident[:])
                    mm.then_inc(B["mT", g].full, 1)
                pe.wait_ge(mt_ready.sem, mt_ready.at(l))
                for t in range(T):
                    for h in range(2):
                        rows(("wo", h, t), l, chunk(("wo", h), l), t, m_t)

                norm_turn(1, l)
                pe.wait_ge(ht_ready[1].sem, ht_ready[1].at(l))
                bank = begin("rt", l)
                for t in range(T):
                    for k in range(KT):
                        mm = nc.tensor.matmul(bank[:, t * N_EXPERTS:(t + 1) * N_EXPERTS], K.h_t[:, k, t * P:(t + 1) * P],
                                              w_rt[:, k, :], start=(k == 0), stop=(k == KT - 1))
                mm.then_inc(B["rt"].full, 1)

                def shared_h(t, w):
                    for k in range(KT):
                        mm = nc.tensor.matmul(sh_bank[t][:], K.h_t[:, k, t * P:(t + 1) * P], w[:, :, k, :],
                                              start=(k == 0), stop=(k == KT - 1))
                    mm.then_inc(sh_h_done.sem, 1)

                def shared_turn(t):
                    pe.wait_ge(sh_act_ready.sem, sh_act_ready.at(l, t + 1))
                    for f in range(2):
                        mm = nc.tensor.transpose(sh_turn_bank[t][:, f * P:(f + 1) * P], act_h[:, t, f::2], K.ident[:])
                    mm.then_inc(sh_turned.sem, 1)

                def shared_w2(t, w):
                    pe.wait_ge(sh_act_t_ready.sem, sh_act_t_ready.at(l, t + 1))
                    for f in range(2):
                        for h in range(2):
                            mm = nc.tensor.matmul(y_bank[t][h][:], act_t[:, t, f, :], w[:, f, h * CHUNK:(h + 1) * CHUNK],
                                                  start=(f == 0), stop=(f == 1), skip_group_check=True)
                    mm.then_inc(sh_done.sem, 1)

                def w13(s):
                    return K.slots[s].rearrange("p (i k) n -> p i (k n)", i=2).rearrange("p i (k n) -> p i k n", n=FF)

                for b in list(B["=moe_y", t, h] for t in range(T) for h in range(2)):
                    pe.wait_ge(b.free, b.free_at(l))
                for b in moe_before:
                    pe.wait_ge(b.free, b.consumed_at(l))
                pe.wait_ge(C["shared"].filled, C["shared"].filled_at(l))
                for t in range(T):
                    shared_h(t, w13(len(CHUNKS_1) % RING - 1))
                pe.wait_ge(chosen_ready.sem, chosen_ready.at(l))
                nc.tensor.matmul(o_bank[:, 0:N_EXPERTS], K.strict_01[:], chosen[:, 0, 0, :], start=True, stop=True)
                nc.tensor.matmul(o_bank[:, N_EXPERTS:2 * N_EXPERTS], K.strict_01[:], chosen[:, 1, 0, :], start=True, stop=False)
                nc.tensor.matmul(o_bank[:, N_EXPERTS:2 * N_EXPERTS], K.ones[:], chosen[:, 0, 0, :], start=False, stop=True)
                for t in range(T):
                    mm = nc.tensor.matmul(o_bank[:, at_count:at_count + 4], chosen[:, t].rearrange("p g e -> p (g e)"), K.ones[:, 0:4],
                                          start=(t == 0), stop=(t == T - 1))
                mm.then_inc(count_done.sem, 1)
                for t in range(T):
                    shared_turn(t)
                pe.wait_ge(more_ready.sem, more_ready.at(l))
                e64 = slice(0, N_EXPERTS)
                index = o_bank[:, at_index:at_index + ROUNDS + 1]
                nc.tensor.matmul(index, K.strict_twice[e64].rearrange("p g e -> p (g e)"), more[e64, :], start=True, stop=False)
                nc.tensor.matmul(index, K.ones[e64, :], more_below[e64, :], start=False, stop=True)
                for t in range(T):
                    mm = nc.tensor.transpose(h_bank[:, t * P:(t + 1) * P], place_64[:, t].rearrange("p i e -> p (i e)"),
                                             K.ident[:])
                mm.then_inc(index_done.sem, 1)
                pe.wait_ge(shared2_filled.sem, shared2_filled.at(l, 16))
                shared_w2(0, slots2[:, 1])
                pe.wait_ge(extra_ready.sem, extra_ready.at(l))
                pe.wait_ge(place_t_ready.sem, place_t_ready.at(l))
                nc.tensor.matmul(o_bank[:, at_expert:at_expert + EXTRA], K.part[e64, 0:1].to_broadcast([N_EXPERTS, P]),
                                 extra_any[e64, :], start=True, stop=True)
                for t in range(T):
                    out = o_bank[:, at_place + t * EXTRA:at_place + (t + 1) * EXTRA]
                    nc.tensor.matmul(out, place_t[e64, t, :], extra_any[e64, :], start=True, stop=False)
                    nc.tensor.matmul(out, K.minus_slots[e64, :], extra_round[e64, :], start=False, stop=True)
                for t in range(T):
                    mm = nc.tensor.matmul(h_bank[:, at_weight + t * EXTRA:at_weight + (t + 1) * EXTRA],
                                          place_t[N_EXPERTS:P, t, :], extra_any[N_EXPERTS:P, :], start=True, stop=True)
                mm.then_inc(list_done.sem, 1)
                shared_w2(1, slots2[:, 1])

                pe.wait_ge(table_ready.sem, table_ready.at(l))
                pe.wait_ge(parts_ready.sem, parts_ready.at(l))
                last_turn, nth, pairs = block_count(pe, l)

                def gather(it, j):
                    pe.wait_ge(hot_ready, nth(it, j))
                    for k in range(KT):
                        for t in range(T):
                            for c in range(PARTS):
                                mm = nc.tensor.matmul(x_bank[:, k * SLOTS:(k + 1) * SLOTS], xn_parts[:, t, c, k, :],
                                                      pick_hot[:, j % 2, t, :], start=(t == 0 and c == 0),
                                                      stop=(t == T - 1 and c == PARTS - 1))
                    mm.then_inc(gather_done, 1)

                def block_h(it, j):
                    pe.wait_ge(x_ready, nth(it, j))
                    pe.wait_ge(w13_filled[j], nth(it, -1) * (32 // UNROLL) + 32)
                    for k in range(KT):
                        for g in range(2):
                            mm = nc.tensor.matmul(h_bank[g * SLOTS:(g + 1) * SLOTS, 0:FF], x_blk[:, j % 2, k, :],
                                                  w13(j)[:, :, k, g * (FF // 2):(g + 1) * (FF // 2)],
                                                  start=(k == 0), stop=(k == KT - 1), skip_group_check=True)
                    mm.then_inc(h_done, 1)

                def block_turn(it, j):
                    pe.wait_ge(act_ready, nth(it, j))
                    nc.tensor.transpose(h_bank[:, FF:FF + P], act_blk, K.ident[:])
                    nc.tensor.transpose(h_bank[:, FF + P:FF + 2 * P],
                                        spread[:, j // 2, j % 2].rearrange("p b s -> p (b s)"), K.ident[:]).then_inc(turn_done, 1)

                def pair_w2(it, i):
                    for b in range(2):
                        pe.wait_ge(w2_filled[2 * i + b], nth(it, -1) * (16 // UNROLL) + 16)
                    for f in range(2):
                        for h in range(2):
                            for b in range(2):
                                mm = nc.tensor.matmul(o_banks[h][b * SLOTS:(b + 1) * SLOTS, :],
                                                      turned[:, i, b, f * SLOTS:(f + 1) * SLOTS],
                                                      w2_slots[2 * i + b][:, f, h * CHUNK:(h + 1) * CHUNK],
                                                      start=(f == 0), stop=(f == 1), skip_group_check=True)
                    mm.then_inc(o_done, 1)

                def pair_add(it, i, t):
                    pe.wait_ge(o_ready, pairs(it, i))
                    for h in range(2):
                        mm = nc.tensor.matmul(y_bank[t][h][:], turned[:, i % PAIRS, t, P:2 * P], o_blk[:, h * CHUNK:(h + 1) * CHUNK],
                                              start=False, stop=True, skip_group_check=True)
                    if t == T - 1:
                        mm.then_inc(added, 1)

                def turn(it, first=False, last=False):
                    for i in range(PAIRS):
                        a, b = 2 * i, 2 * i + 1
                        block_h(it, a)
                        gather(it, b)
                        block_turn(it, a)
                        if not (first and i == 0):
                            pair_add(it, i - 1, 0)
                        pe.wait_ge(turned_ready, nth(it, a))
                        block_h(it, b)
                        if not (first and i == 0):
                            pair_add(it, i - 1, 1)
                        block_turn(it, b)
                        if not (last and i == PAIRS - 1):
                            gather(it, b + 1)
                        pe.wait_ge(turned_ready, nth(it, b))
                        pair_w2(it, i)

                gather(0, 0)
                turn(0, first=True)
                with pe.Fori(1, last_turn) as it:
                    turn(it)
                turn(last_turn, last=True)
                for t in range(T):
                    pair_add(last_turn, PAIRS - 1, t)

        @block.scalar
        def _(act):
            def full_of(name, l):
                act.wait_ge(B[name].full, B[name].full_at(l))
                return B[name].tile

            def row_norm(i, l):
                for t in range(T):
                    if i == 0:
                        act.wait_ge(x_out.sem, x_out.at(l, t + 1 - T))
                    else:
                        act.wait_ge(x_mid.sem, x_mid.at(l, t + 1))
                    nc.scalar.activation(K.xn[:, t, :], K.x[:, t, :], ACT.Square, accum_out=sq_sum[:, t:t + 1])
                    act.drain()
                    nc.scalar.activation(std[:, t:t + 1], sq_sum[:, t:t + 1], ACT.Sqrt, scale=1.0 / D, bias=K.eps[:])\
                        .then_inc(std_ready[i].sem, 1)

            def copy_out(name, l, dst, src, last=None, scale=1.0):
                nc.scalar.activation(dst, src, ACT.Copy, scale=scale).then_inc(B[name].free, 1)

            const_scalar(act)
            with act.Fori(0, DEPTH) as l:
                def gate_sig(i, h, t):
                    n = 4 * BRANCHES.index(i) + 2 * h + t
                    bank = full_of(("gt", i, h, t), l)
                    if n >= 2:
                        act.wait_ge(y_used.sem, y_used.at(l, n - 1))
                    nc.scalar.activation(sig_g[:, n % 2, :], bank[:], ACT.Sigmoid).then_inc(B["gt", i, h, t].free, 1)
                    act.drain().then_inc(sig_ready.sem, 1)

                def copy_mod(c):
                    bank = full_of(("mod_part", c), l)
                    copy_out(("mod_part", c), l, mod_part[c], bank[:])

                copy_mod(0)
                copy_mod(1)
                row_norm(0, l)
                copy_mod(2)
                copy_mod(3)
                bank = full_of("vec", l)
                copy_out("vec", l, vec_t[:], bank[:, 0:(TAPS + 3) * CT])
                act.drain()
                for i in range(2):
                    bank = full_of(("ug", i), l)
                    nc.scalar.activation(conv_t[:, 2 * i:2 * i + 2, :], bank[:].rearrange("p (c n) -> p c n", c=2),
                                         ACT.Sigmoid).then_inc(B["ug", i].free, 1)
                act.drain().then_inc(ug_ready.sem, 2)
                for name, dst, scale in (("qc", qc_t, SB_HD ** -0.5), ("kc", kc_t, 1.0)):
                    for i in range(2):
                        bank = full_of((name, i), l)
                        copy_out((name, i), l, dst[:, 2 * i:2 * i + 2, :], bank[:].rearrange("p (c n) -> p c n", c=2),
                                 scale=scale)
                act.drain().then_inc(qkc_ready.sem, 1)
                for name, h0, nh, c0, n in ([(("z0", par, i), 4 * par + 2 * i, 2, 0, SEQ) for par in range(2) for i in range(2)]
                                            + [(("z1", par), 4 * par, 4, SEQ, P) for par in range(2)]):
                    src = full_of(name, l)[:].rearrange("p (h n) -> p h n", h=nh)
                    nc.scalar.activation(sp_[:, h0:h0 + nh, c0:c0 + n], src, ACT.Abs)
                    copy_out(name, l, z[:, h0:h0 + nh, c0:c0 + n], src)
                act.drain()
                nc.scalar.activation(sp_[:], sp_[:], ACT.Exp, scale=-1.0)
                act.drain()
                nc.scalar.activation(sp_[:], sp_[:], ACT.Ln, bias=1.0).then_inc(log_ready.sem, 1)
                copy_mod(4)
                for w, name in enumerate(("qa", "ka")):
                    for t in range(T):
                        bank = full_of((name, t), l)
                        copy_out((name, t), l, qk[:, t, w * 512:(w + 1) * 512], bank[:])
                    copy_mod(5 + w)
                act.drain().then_inc(qk_ready.sem, 1)
                act.wait_ge(d_ready.sem, d_ready.at(l))
                nc.scalar.activation(z[:], z[:], ACT.Exp)
                act.wait_ge(qk_sq_ready.sem, qk_sq_ready.at(l))
                nc.scalar.activation(qk_std[:], qk_std[:], ACT.Sqrt, scale=1.0 / DA_HD, bias=K.eps[:])\
                    .then_inc(qk_std_ready.sem, 1)
                for name, dst in (("vc", vc), ("va", va)):
                    for t in range(T):
                        bank = full_of((name, t), l)
                        copy_out((name, t), l, dst[:, t, :], bank[:])
                act.drain().then_inc(v_ready.sem, 1)
                for i in range(2):
                    bank = full_of(("oc", i), l)
                    copy_out(("oc", i), l, yc_t[:, 2 * i:2 * i + 2, :], bank[:].rearrange("p (c n) -> p c n", c=2))
                for w, dst in enumerate((qa_t, ka_t)):
                    for i in range(2):
                        bank = full_of(("qkT", w, i), l)
                        copy_out(("qkT", w, i), l, dst[:, 2 * i:2 * i + 2, :], bank[:].rearrange("p (c n) -> p c n", c=2))
                act.drain().then_inc(qkt_ready.sem, 1)
                act.wait_ge(lam_s_ready.sem, lam_s_ready.at(l))
                nc.scalar.activation(lam_e[:], lam_s[:], ACT.Exp)
                gate_sig(2, 0, 0)
                act.wait_ge(max_ready.sem, max_ready.at(l))
                for r in range(16):
                    e = e1[:, r, :] if r < 8 else e0[:, r - 8, :]
                    nc.scalar.activation(e, e, ACT.Exp, bias=row16[:, 0, r:r + 1], scale=DA_HD ** -0.5,
                                         accum_out=row16[:, 1, r:r + 1])
                act.drain().then_inc(exp_ready.sem, 1)
                for h, t in ((0, 1), (1, 0), (1, 1)):
                    gate_sig(2, h, t)
                for i in range(2):
                    bank = full_of(("aT1", i), l)
                    copy_out(("aT1", i), l, a_t[:, 2 * i:2 * i + 2, 1:3, :],
                             bank[:].rearrange("p (h b n) -> p h b n", h=2, b=2))
                bank = full_of("aT0", l)
                copy_out("aT0", l, a_t[:, :, 0, :], bank[:].rearrange("p (h n) -> p h n", h=DA_HEADS))
                act.drain().then_inc(at_ready.sem, 1)
                for c in (7, 8, 9):
                    copy_mod(c)
                act.wait_ge(oa_sq_ready.sem, oa_sq_ready.at(l))
                nc.scalar.activation(oa_std[:], oa_std[:], ACT.Sqrt, scale=1.0 / (2 * DA_HD), bias=K.eps[:])\
                    .then_inc(oa_std_ready.sem, 1)
                for i in range(2):
                    bank = full_of(("oaT", i), l)
                    copy_out(("oaT", i), l, oa_t[:, 2 * i:2 * i + 2, :], bank[:].rearrange("p (c n) -> p c n", c=2))
                act.drain().then_inc(oat_ready.sem, 1)
                for c in (10, 11):
                    copy_mod(c)
                for h, t in ((0, 0), (0, 1), (1, 0)):
                    gate_sig(0, h, t)
                src = full_of("cvar", l)
                nc.scalar.activation(conv_std[:], src[:, 0:SEQ], ACT.Sqrt, bias=K.eps[:]).then_inc(B["cvar"].free, 1)
                act.drain().then_inc(conv_std_ready.sem, 1)
                act.wait_ge(conv_ln_ready.sem, conv_ln_ready.at(l))
                nc.scalar.activation(conv_t[:], conv[:], ACT.Sigmoid).then_inc(conv_sig_ready.sem, 1)
                gate_sig(0, 1, 1)
                for h in range(2):
                    for t in range(T):
                        gate_sig(1, h, t)
                for g in range(4):
                    bank = full_of(("mT", g), l)
                    copy_out(("mT", g), l, m_t[:, 2 * g:2 * g + 2, :], bank[:].rearrange("p (c n) -> p c n", c=2))
                act.drain().then_inc(mt_ready.sem, 1)
                row_norm(1, l)
                bank = full_of("rt", l)
                nc.scalar.activation(score[:], bank[:, 0:T * N_EXPERTS].rearrange("p (t n) -> p t n", t=T), ACT.Sigmoid)\
                    .then_inc(B["rt"].free, 1)
                act.drain().then_inc(score_ready.sem, 1)

                for t in range(T):
                    act.wait_ge(sh_h_done.sem, sh_h_done.at(l, t + 1))
                    nc.scalar.activation(sig_h[:, t, :], sh_bank[t][:, 0:FF], ACT.Sigmoid).then_inc(sh_sig_ready.sem, 1)
                for t in range(T):
                    act.wait_ge(sh_turned.sem, sh_turned.at(l, t + 1))
                    nc.scalar.activation(act_t[:, t], sh_turn_bank[t][:, 0:2 * P].rearrange("p (f n) -> p f n", f=2), ACT.Copy)\
                        .then_inc(sh_act_t_ready.sem, 1)
                act.wait_ge(index_done.sem, index_done.at(l))
                nc.scalar.activation(place_t, h_bank[:, 0:T * P].rearrange("p (t n) -> p t n", t=T), ACT.Copy)\
                    .then_inc(place_t_ready.sem, 1)

                act.wait_ge(table_ready.sem, table_ready.at(l))
                last_turn, nth, pairs = block_count(act, l)

                def sigmoid(it, j):
                    act.wait_ge(h_done, nth(it, j) + RING)
                    nc.scalar.activation(sig_blk, h_bank[:, 0:FF // 2], ACT.Sigmoid).then_inc(sig_ready_blk, 1)

                def copy_turned(it, j):
                    act.wait_ge(turn_done, nth(it, j))
                    nc.scalar.activation(turned[:, j // 2, j % 2], h_bank[:, FF:FF + 2 * P], ACT.Copy).then_inc(turned_ready, 1)

                def turn(it):
                    for i in range(PAIRS):
                        for j in (2 * i, 2 * i + 1):
                            sigmoid(it, j)
                            copy_turned(it, j)
                        act.wait_ge(o_done, pairs(it, i))
                        for h in range(2):
                            cp = nc.scalar.activation(o_blk[:, h * CHUNK:(h + 1) * CHUNK], o_banks[h][:], ACT.Copy)
                        cp.then_inc(o_ready, 1)

                with act.Fori(0, last_turn + 1) as it:
                    turn(it)

        @block.vector
        def _(dve):
            v = nc.vector

            def full_of(name, l):
                dve.wait_ge(B[name].full, B[name].full_at(l))
                return B[name].tile

            def norm_x(i, l):
                for t in range(T):
                    dve.wait_ge(std_ready[i].sem, std_ready[i].at(l, t + 1))
                    v.reciprocal(std[:, t:t + 1], std[:, t:t + 1])
                    dve.drain()
                    v.tensor_scalar(K.xn[:, t, :], K.x[:, t, :], std[:, t:t + 1], None, ALU.mult)
                    dve.drain().then_inc(xn_ready[i].sem, 1)

            def modulate(i, l):
                for g in range(4):
                    bank = full_of(("xT", i, g), l)
                    for j in range(2):
                        k = 2 * g + j
                        ins = v.tensor_scalar(K.h_t[:, k, :], bank[:, j * SEQ:(j + 1) * SEQ],
                                              mod_col[:, 2 * i + 1, k:k + 1], mod_col[:, 2 * i, k:k + 1], ALU.mult, ALU.add)
                    ins.then_inc(B["xT", i, g].free, 1)
                dve.drain().then_inc(ht_ready[i].sem, 1)

            const_vector(dve)
            v.memset(hpad[:, :, 0:TAPS - 1], 0.0)
            v.memset(more[:], 0.0)
            v.memset(more_below[:], 0.0)
            with dve.Fori(0, DEPTH) as l:
                one = ds(l, 1)

                def mod(chunks):
                    for c in chunks:
                        part, half = divmod(c, 2)
                        bank = full_of(("mod_sum", c), l)
                        if part in MOD_ROW_PARTS:
                            g = gate[:, MOD_ROW_PARTS.index(part), half * CHUNK:(half + 1) * CHUNK]
                            v.tensor_tensor(g, bank[:], g, ALU.add).then_inc(B["mod_sum", c].free, 1)
                        else:
                            v.tensor_tensor(pick, bank[:].rearrange("p (q k) -> p q k", k=KT),
                                            broadcast(K.ident[:, 64 * half:64 * half + 64], 2, KT), ALU.mult)\
                                .then_inc(B["mod_sum", c].free, 1)
                            dve.drain()
                            v.tensor_reduce(col4[:, MOD_COL_PARTS.index(part), half, :], pick.rearrange("p q k -> p k q"),
                                            AX.X, ALU.add)
                            dve.drain()

                def mod_columns(i):
                    pair = slice(2 * i, 2 * i + 2)
                    v.tensor_tensor(mod_col[:, pair, :], col4[:, pair, 0, :], col4[:, pair, 1, :], ALU.add)
                    dve.drain()
                    v.tensor_tensor(mod_col[:, pair, :], mod_col[:, pair, :], mod_b[:, pair, :], ALU.add)
                    dve.drain()
                    v.scalar_tensor_tensor(mod_col[:, 2 * i + 1, :], mod_col[:, 2 * i + 1, :], 1.0, norm_g[:, i, :],
                                           ALU.add, ALU.mult)
                    dve.drain()

                ch = TAPS * CT

                def conv_taps(k0, k1):
                    for k in range(k0, k1):
                        for c in range(CT):
                            w = vec_t[:, k * CT + c:k * CT + c + 1]
                            if k == 0:
                                v.tensor_scalar(conv[:, c, :], hpad[:, c, 0:SEQ], w, vec_t[:, ch + c:ch + c + 1], ALU.mult, ALU.add)
                            else:
                                v.scalar_tensor_tensor(conv[:, c, :], hpad[:, c, k:k + SEQ], w, conv[:, c, :], ALU.mult, ALU.add)
                        dve.drain()

                def merge(i, h, t):
                    n = 4 * BRANCHES.index(i) + 2 * h + t
                    col = slice(h * CHUNK, (h + 1) * CHUNK)
                    dve.wait_ge(sig_ready.sem, sig_ready.at(l, n + 1))
                    bank = full_of(("y", i, h, t), l)
                    sig = sig_g[:, n % 2, :]
                    if i == BRANCHES[0]:
                        v.tensor_tensor(merged[:, t, col], bank[:], sig, ALU.mult).then_inc(B["y", i, h, t].free, 1)
                        dve.drain().then_inc(y_used.sem, 1)
                        return
                    if i == 1:
                        v.tensor_tensor(y_tmp[:], bank[:], proj_b_bias[:, col], ALU.add).then_inc(B["y", i, h, t].free, 1)
                        dve.drain()
                        v.tensor_tensor(y_tmp[:], y_tmp[:], sig, ALU.mult)
                    else:
                        v.tensor_tensor(y_tmp[:], bank[:], sig, ALU.mult).then_inc(B["y", i, h, t].free, 1)
                    dve.drain().then_inc(y_used.sem, 1)
                    v.tensor_tensor(merged[:, t, col], merged[:, t, col], y_tmp[:], ALU.add)
                    dve.drain()

                norm_x(0, l)
                dve.wait_ge(params.sem, params.at(l, params.n))
                v.tensor_tensor(lam_p[:], lam4[:, 0::2, :], lam4[:, 1::2, :], ALU.mult)
                dve.drain()
                v.tensor_reduce(lam_s[:], lam_p[:], AX.X, ALU.add).then_inc(lam_s_ready.sem, 1)
                v.tensor_scalar(gain_o[:], subln[:], K.lam_rest[:, one], None, ALU.mult)
                mod(range(MOD_FIRST))
                mod_columns(0)
                modulate(0, l)
                dve.wait_ge(ug_ready.sem, ug_ready.at(l, 2))
                for i in range(2):
                    bank = full_of(("ua", i), l)
                    v.tensor_tensor(hpad[:, 2 * i:2 * i + 2, TAPS - 1:], bank[:].rearrange("p (c n) -> p c n", c=2),
                                    conv_t[:, 2 * i:2 * i + 2, :], ALU.mult).then_inc(B["ua", i].free, 1)
                dve.drain()
                conv_taps(0, 24)
                dve.wait_ge(log_ready.sem, log_ready.at(l))
                v.scalar_tensor_tensor(sp_[:].rearrange("p h n -> p (h n)"), z_flat, 0.0,
                                       sp_[:].rearrange("p h n -> p (h n)"), ALU.max, ALU.add)
                dve.drain()
                diagonal = (0, 2 * P)
                for c in diagonal:
                    v.tensor_tensor(sp_[:, :, c:c + P], sp_[:, :, c:c + P], broadcast(K.strict_01[:], 1, SB_HEADS), ALU.mult)
                dve.drain().then_inc(sp_ready.sem, 1)
                conv_taps(24, 28)
                for r in range(3):
                    for par in range(2):
                        bank = full_of(("suf", r, par), l)
                        zz = z[:, 4 * par:4 * par + 4, r * P:(r + 1) * P]
                        v.tensor_tensor(zz, zz, bank[:].rearrange("p (h n) -> p h n", h=4), ALU.subtract)\
                            .then_inc(B["suf", r, par].free, 1)
                dve.drain()
                for c in diagonal:
                    v.scalar_tensor_tensor(z[:, :, c:c + P], z[:, :, c:c + P], 0.0, broadcast(K.strict_neg[:], 1, SB_HEADS),
                                           ALU.min, ALU.add)
                v.tensor_scalar(z[:, :, P:2 * P], z[:, :, P:2 * P], 0.0, None, ALU.min)
                dve.drain().then_inc(d_ready.sem, 1)
                dve.wait_ge(qk_ready.sem, qk_ready.at(l))
                sq = K.xn[:].rearrange("p t n -> p (t n)")
                qk_all = qk[:].rearrange("p t n -> p (t n)")
                v.tensor_tensor(sq, qk_all, qk_all, ALU.mult)
                dve.drain()
                v.tensor_reduce(qk_std[:], sq.rearrange("p (h n) -> p h n", n=DA_HD), AX.X, ALU.add)\
                    .then_inc(qk_sq_ready.sem, 1)
                dve.wait_ge(qk_std_ready.sem, qk_std_ready.at(l))
                v.reciprocal(qk_std[:], qk_std[:])
                dve.drain()
                heads = qk_all.rearrange("p (h n) -> p h n", n=DA_HD)
                v.tensor_tensor(heads, heads, broadcast(qk_std[:], 2, DA_HD), ALU.mult)
                dve.drain()
                for w in range(2):
                    part = qk_heads[:, :, 8 * w:8 * w + 8, :]
                    v.tensor_tensor(part, part, broadcast(broadcast(gain_qk[:, w, :], 1, 8), 1, T), ALU.mult)
                dve.drain()
                half = DA_HD // 2
                cos, sin = (broadcast(tab[:, :, 0:half], 2, 16) for tab in (K.cos, K.sin))
                s1, s2 = (b[:].rearrange("p h n -> p (h n)").rearrange("p (t h n) -> p t h n", t=T, h=16) for b in (qa_t, ka_t))
                x1, x2 = qk_heads[:, :, :, 0:half], qk_heads[:, :, :, half:]
                r1, r2 = qk_rot[:, :, :, 0:half], qk_rot[:, :, :, half:]
                v.tensor_tensor(r1, x1, cos, ALU.mult)
                v.tensor_tensor(s1, x2, sin, ALU.mult)
                v.tensor_tensor(r2, x2, cos, ALU.mult)
                v.tensor_tensor(s2, x1, sin, ALU.mult)
                dve.drain()
                v.tensor_tensor(r1, r1, s1, ALU.subtract)
                v.tensor_tensor(r2, r2, s2, ALU.add)
                dve.drain().then_inc(qk_rot_ready.sem, 1)
                conv_taps(28, TAPS)
                for m in range(2):
                    for i in range(2):
                        src = full_of(("s1", m, i), l)[:].rearrange("p (h n) -> p h n", h=2)
                        dst = e1[:, 4 * m + 2 * i:4 * m + 2 * i + 2, :]
                        v.tensor_copy(dst[:, :, 0:P], src[:, :, 0:P])
                        v.tensor_tensor(dst[:, :, P:SEQ], src[:, :, P:SEQ], broadcast(K.causal_neg[:], 1, 2), ALU.add)\
                            .then_inc(B["s1", m, i].free, 1)
                for m in range(2):
                    src = full_of(("s0", m), l)[:].rearrange("p (h n) -> p h n", h=4)
                    v.tensor_tensor(e0[:, 4 * m:4 * m + 4, :], src, broadcast(K.causal_neg[:], 1, 4), ALU.add)\
                        .then_inc(B["s0", m].free, 1)
                dve.drain()
                v.tensor_reduce(row16[:, 0, 0:8], e1, AX.X, ALU.max)
                v.tensor_reduce(row16[:, 0, 8:16], e0, AX.X, ALU.max)
                dve.drain()
                v.tensor_scalar(row16[:, 0, :], row16[:, 0, :], -DA_HD ** -0.5, None, ALU.mult)
                dve.drain().then_inc(max_ready.sem, 1)
                for t in range(T):
                    merge(2, 0, t)
                dve.wait_ge(exp_ready.sem, exp_ready.at(l))
                v.tensor_tensor(lam[:], lam_e[:, 0:1], lam_e[:, 1:2], ALU.subtract)
                dve.drain()
                v.tensor_scalar(lam[:], lam[:], K.lam_init[:, one], None, ALU.add)
                v.reciprocal(row16[:, 2, :], row16[:, 1, :])
                dve.drain()
                for c in (4, 12):
                    v.tensor_scalar(row16[:, 2, c:c + 4], row16[:, 2, c:c + 4], lam[:], None, ALU.mult)
                dve.drain()
                for e, c, n in ((e1, 0, SEQ), (e0, 8, P)):
                    v.tensor_tensor(e, e, broadcast(row16[:, 2, c:c + 8], 2, n), ALU.mult)
                dve.drain()
                for e in (e1, e0):
                    v.tensor_tensor(e[:, 0:4, :], e[:, 0:4, :], e[:, 4:8, :], ALU.subtract)
                dve.drain().then_inc(a_ready.sem, 1)
                for t in range(T):
                    merge(2, 1, t)
                dve.wait_ge(gate_loaded.sem, gate_loaded.at(l, gate_loaded.n))
                mod((4, 5, 6))
                for t in range(T):
                    bank = full_of(("oa", t), l)
                    v.tensor_copy(oa[:, t, :], bank[:]).then_inc(B["oa", t].free, 1)
                dve.drain()
                sq = z_flat[:, 0:T * 512].rearrange("p (h n) -> p h n", n=2 * DA_HD)
                v.tensor_tensor(sq, oa_heads, oa_heads, ALU.mult)
                dve.drain()
                v.tensor_reduce(oa_std[:], sq, AX.X, ALU.add).then_inc(oa_sq_ready.sem, 1)
                dve.wait_ge(oa_std_ready.sem, oa_std_ready.at(l))
                v.reciprocal(oa_std[:], oa_std[:])
                dve.drain()
                v.tensor_tensor(oa_heads, oa_heads, broadcast(oa_std[:], 2, 2 * DA_HD), ALU.mult)
                dve.drain()
                v.tensor_tensor(oa_heads, oa_heads, broadcast(gain_o[:], 1, T * DA_HEADS), ALU.mult)
                dve.drain().then_inc(oa_ready.sem, 1)
                mod(range(7, MOD_CHUNKS))
                mod_columns(1)
                for t in range(T):
                    merge(0, 0, t)
                bank = full_of("cmean", l)
                v.tensor_tensor(conv[:], conv[:], broadcast(bank[:, 0:SEQ], 1, CT), ALU.subtract).then_inc(B["cmean"].free, 1)
                dve.drain()
                v.tensor_tensor(conv_t[:], conv[:], conv[:], ALU.mult)
                dve.drain().then_inc(conv_sq_ready.sem, 1)
                merge(0, 1, 0)
                dve.wait_ge(conv_std_ready.sem, conv_std_ready.at(l))
                v.reciprocal(conv_std[:], conv_std[:])
                dve.drain()
                v.tensor_tensor(conv[:], conv[:], broadcast(conv_std[:], 1, CT), ALU.mult)
                dve.drain()
                for c in range(CT):
                    v.tensor_scalar(conv[:, c, :], conv[:, c, :], vec_t[:, ch + CT + c:ch + CT + c + 1],
                                    vec_t[:, ch + 2 * CT + c:ch + 2 * CT + c + 1], ALU.mult, ALU.add)
                dve.drain().then_inc(conv_ln_ready.sem, 1)
                dve.wait_ge(conv_sig_ready.sem, conv_sig_ready.at(l))
                v.tensor_tensor(yb_t[:], conv[:], conv_t[:], ALU.mult)
                dve.drain().then_inc(ybt_ready.sem, 1)
                merge(0, 1, 1)
                for h in range(2):
                    for t in range(T):
                        merge(1, h, t)
                dve.drain().then_inc(merged_ready.sem, 1)
                for t in range(T):
                    for h in range(2):
                        col = slice(h * CHUNK, (h + 1) * CHUNK)
                        bank = full_of(("wo", h, t), l)
                        v.tensor_tensor(y_tmp[:], bank[:], gate[:, 0, col], ALU.mult).then_inc(B["wo", h, t].free, 1)
                        dve.drain()
                        v.tensor_tensor(K.x[:, t, col], K.x[:, t, col], y_tmp[:], ALU.add)
                        dve.drain()
                    dve.drain().then_inc(x_mid.sem, 1)

                norm_x(1, l)
                modulate(1, l)
                dve.wait_ge(score_ready.sem, score_ready.at(l))
                v.tensor_tensor(biased[:], score[:], broadcast(rt_bias[:], 1, T), ALU.add)
                dve.drain()
                for t in range(T):
                    for g in range(N_GROUPS):
                        v.max(out=top[:, t, g, :], in_=biased[:, t, g * PER_GROUP:(g + 1) * PER_GROUP])
                dve.drain()
                v.tensor_tensor(g_score[:], top[:, :, :, 0], top[:, :, :, 1], ALU.add)
                dve.drain()
                for t in range(T):
                    other, own = broadcast(g_score[:, t, :], 1, N_GROUPS), broadcast(g_score[:, t, :], 2, N_GROUPS)
                    v.tensor_tensor(g_cmp[:, t], other, own, ALU.is_gt)
                    v.tensor_tensor(g_eq[:, t], other, own, ALU.is_equal)
                dve.drain()
                for t in range(T):
                    v.tensor_tensor(g_eq[:, t], g_eq[:, t], K.lower8[:], ALU.mult)
                dve.drain()
                v.tensor_tensor(g_cmp[:], g_cmp[:], g_eq[:], ALU.add)
                dve.drain()
                v.tensor_reduce(g_rank[:], g_cmp[:], AX.X, ALU.add)
                dve.drain()
                v.tensor_scalar(g_rank[:], g_rank[:], TOPK_GROUPS - 0.5, None, ALU.is_lt)
                dve.drain()
                v.tensor_scalar(g_neg[:], g_rank[:], -NEG, NEG, ALU.mult, ALU.add)
                by_group = biased[:].rearrange("p t (g e) -> p t g e", g=N_GROUPS)
                v.tensor_tensor(by_group, by_group, broadcast(g_rank[:], 3, PER_GROUP), ALU.mult)
                dve.drain()
                v.tensor_tensor(by_group, by_group, broadcast(g_neg[:], 3, PER_GROUP), ALU.add)
                dve.drain()
                for t in range(T):
                    v.max(out=top8[:, t, :], in_=biased[:, t, :])
                dve.drain()
                for t in range(T):
                    v.match_replace(out=rest[:, t, :], in_to_replace=top8[:, t, :], in_values=biased[:, t, :],
                                    imm_value=3.0 * NEG)
                dve.drain()
                v.tensor_tensor(chosen[:], broadcast(rest[:], 2, 2), broadcast(biased[:], 2, 2), ALU.not_equal)
                dve.drain().then_inc(chosen_ready.sem, 1)
                v.tensor_tensor(rest[:], chosen[:, :, 0, :], score[:], ALU.mult)
                dve.drain()
                v.tensor_reduce(w_sum[:], rest[:], AX.X, ALU.add)
                dve.drain()
                v.tensor_scalar(w_sum[:], w_sum[:], 1e-20, None, ALU.add)
                dve.drain()
                v.reciprocal(w_sum[:], w_sum[:])
                dve.drain()
                for t in range(T):
                    v.tensor_scalar(place[:, t, 1, 0:N_EXPERTS], rest[:, t, :], w_sum[:, t:t + 1], ROUTED_SCALE,
                                    ALU.mult, ALU.mult)
                for t in range(T):
                    dve.wait_ge(sh_sig_ready.sem, sh_sig_ready.at(l, t + 1))
                    v.tensor_tensor(act_h[:, t, :], sh_bank[t][:, 0:FF], sig_h[:, t, :], ALU.mult)
                    dve.drain()
                    v.tensor_tensor(act_h[:, t, :], act_h[:, t, :], sh_bank[t][:, FF:2 * FF], ALU.mult)\
                        .then_inc(sh_act_ready.sem, 1)
                dve.wait_ge(count_done.sem, count_done.at(l))
                v.scalar_tensor_tensor(place[:, :, 0, 0:N_EXPERTS], o_bank[:, 0:T * N_EXPERTS].rearrange("p (t e) -> p t e", t=T),
                                       1.0, chosen[:, :, 0, :], ALU.add, ALU.mult)
                v.tensor_tensor(more[:, 0:ROUNDS], K.full_rounds[:], o_bank[:, at_count:at_count + ROUNDS], ALU.is_lt)
                dve.drain()
                v.tensor_copy(place_64[:], place[:, :, :, 0:N_EXPERTS])
                for r in range(ROUNDS):
                    v.tensor_tensor(more_below[:, r + 1:r + 2], more_below[:, r:r + 1], more[:, r:r + 1], ALU.add)
                    dve.drain()
                dve.drain().then_inc(more_ready.sem, 1)
                dve.wait_ge(index_done.sem, index_done.at(l))
                v.tensor_copy(extra_at[:], o_bank[:, at_index:at_index + ROUNDS + 1])
                dve.drain()
                for r in range(ROUNDS):
                    v.tensor_scalar(extra_hot[:, r, :], K.ramp[:, 0:EXTRA], extra_at[:, r:r + 1], more[:, r:r + 1],
                                    ALU.is_equal, ALU.mult)
                dve.drain()
                v.tensor_tensor(extra_any[:], extra_hot[:, 0, :], extra_hot[:, 1, :], ALU.add)
                v.scalar_tensor_tensor(extra_round[:], extra_hot[:, 1, :], 2.0, extra_hot[:, 0, :], ALU.mult, ALU.add)
                dve.drain()
                v.tensor_tensor(extra_any[:], extra_any[:], extra_hot[:, 2, :], ALU.add)
                v.scalar_tensor_tensor(extra_round[:], extra_hot[:, 2, :], 3.0, extra_round[:], ALU.mult, ALU.add)
                dve.drain().then_inc(extra_ready.sem, 1)
                v.tensor_scalar(turns_cmp[:], K.ramp[:, 0:EXTRA:UNROLL], extra_at[:, ROUNDS:ROUNDS + 1], None, ALU.is_lt)
                dve.drain()
                v.tensor_reduce(turns_f[:], turns_cmp[:], AX.X, ALU.add)
                dve.drain()
                v.tensor_scalar(turns_f[:], turns_f[:], float(N_EXPERTS // UNROLL - 1), None, ALU.add)
                dve.drain()
                v.tensor_copy(K.last_turn[:, one], turns_f[:])
                v.scalar_tensor_tensor(K.first_turn_f[:, ds(l + 1, 1)], turns_f[:], 1.0, K.first_turn_f[:, one], ALU.add, ALU.add)
                dve.drain()
                v.tensor_copy(K.first_turn[:], K.first_turn_f[:])
                dve.wait_ge(list_done.sem, list_done.at(l))
                v.tensor_copy(K.table[:, N_EXPERTS:MAX_BLOCKS], o_bank[:, at_expert:at_expert + EXTRA])
                for i, (bank, c) in enumerate(((o_bank, at_place), (h_bank, at_weight))):
                    v.tensor_copy(place[:, :, i, N_EXPERTS:MAX_BLOCKS], bank[:, c:c + T * EXTRA].rearrange("p (t b) -> p t b", t=T))
                dve.drain().then_inc(table_ready.sem, 1)

                dve.wait_ge(table_ready.sem, table_ready.at(l))
                dve.sem_inc(wait_carrier, 1)
                last_turn, nth, pairs = block_count(dve, l)

                def one_hot(it, j):
                    col = ds(it * UNROLL + j, 1)
                    places = K.ramp[:, 1:1 + SLOTS]
                    for t in range(T):
                        v.tensor_scalar(pick_hot[:, j % 2, t, :], places, place[:, t, 0, col], None, ALU.is_equal)
                        v.tensor_scalar(spread[:, j // 2 % PAIRS, t, j % 2, :], places, place[:, t, 0, col], place[:, t, 1, col],
                                        ALU.is_equal, ALU.mult)
                    dve.drain().then_inc(hot_ready, 1)

                def block_x(it, j):
                    dve.wait_ge(gather_done, nth(it, j))
                    x = x_blk[:, j % 2]
                    v.tensor_tensor(x, x_bank[:].rearrange("p (k s) -> p k s", k=KT), broadcast(mod_col[:, 3, :], 2, SLOTS), ALU.mult)
                    dve.drain()
                    v.tensor_tensor(x, x, broadcast(mod_col[:, 2, :], 2, SLOTS), ALU.add).then_inc(x_ready, 1)

                def block_act(it, j):
                    dve.wait_ge(sig_ready_blk, nth(it, j))
                    v.tensor_tensor(act_blk, h_bank[:, 0:FF // 2], sig_blk, ALU.mult)
                    dve.drain()
                    v.tensor_tensor(act_blk, act_blk, h_bank[:, FF // 2:FF], ALU.mult).then_inc(act_ready, 1)

                def turn(it, last=False):
                    for i in range(PAIRS):
                        a, b = 2 * i, 2 * i + 1
                        end = last and i == PAIRS - 1
                        block_act(it, a)
                        block_x(it, b)
                        if not end:
                            one_hot(it, b + 1)
                            one_hot(it, b + 2)
                        block_act(it, b)
                        if not end:
                            block_x(it, b + 1)

                one_hot(0, 0)
                one_hot(0, 1)
                block_x(0, 0)
                with dve.Fori(0, last_turn) as it:
                    turn(it)
                turn(last_turn, last=True)
                dve.wait_ge(added, pairs(last_turn, PAIRS - 1))
                for t in range(T):
                    for h in range(2):
                        col = slice(h * CHUNK, (h + 1) * CHUNK)
                        v.tensor_tensor(y_tmp[:], y_bank[t][h][:], gate[:, 1, col], ALU.mult)\
                            .then_inc(B["=moe_y", t, h].free, 1)
                        dve.drain()
                        v.tensor_tensor(K.x[:, t, col], K.x[:, t, col], y_tmp[:], ALU.add)
                        dve.drain()
                    dve.drain().then_inc(x_out.sem, 1)


HEADS_2 = MLA_H + MOBA_H
GROUPS_2 = (
    [("xT", g) for g in range(4)]
    + [(n, t) for n in ("n0", "n3") for t in range(T)] + ["cqT", "ckT"] + [("n4", t) for t in range(T)]
    + [("q", t) for t in range(T)] + [("kv", t) for t in range(T)] + ["vec", "wsT"] + [("n2", t) for t in range(T)]
    + ["c_h", "c_b"] + [("bT", w) for w in range(2)] + [("mT", w, i) for w in range(2) for i in range(2)]
    + [("sm1", i) for i in range(2)] + ["sm0"] + [("sb1", par) for par in range(2)] + [("sb0", par) for par in range(2)]
    + ["c_c", "g_b"] + [(n, t) for n in ("n1", "n5") for t in range(T)] + [("mix", t) for t in range(T)]
    + [("aT1", i) for i in range(4)] + [("aT0", i) for i in range(2)] + [("o", t) for t in range(T)]
    + [("yT", i) for i in range(3)] + [("wo", h, t) for t in range(T) for h in range(2)]
)
GROUPS_2 += ["-pad"] * (-len(GROUPS_2) % BANKS)
READERS_2 = {"t0": "c_b", "t1": "g_b"} | {n: (n, 1) for n in ("n0", "n1", "n2", "n3", "n4", "n5")}


def second_block(nc, A, K, out):
    ds = bass.ds
    with ExitStack() as ctx:
        def sb(name, shape, dt=F32):
            return ctx.enter_context(nc.sbuf_tensor(name, shape, dt))

        def sem(name):
            return ctx.enter_context(nc.semaphore(name))

        def signal(name, per_layer=1, credit=0):
            return Signal(sem(name), per_layer, credit)

        norm_g = sb("norm_g2", [P, KT])
        gain_cq = sb("gain_cq", [P, 256])
        gain_ckv = sb("gain_ckv", [P, 128])
        gain_q = sb("gain_q", [P, MLA_QK])
        gain_kn = sb("gain_kn", [P, MLA_NOPE])
        gain_kr = sb("gain_kr", [P, MLA_ROPE])
        sg_gain = sb("sg_gain", [P, GW])
        sg_bias = sb("sg_bias", [P, GW])
        gain_moba = sb("gain_moba", [P, 2, MOBA_HD])
        w_uq = sb("w_uq", [P, 2, MLA_H * MLA_QK])
        w_ukv = sb("w_ukv", [P, MLA_H * 2 * 64])
        sg_w = sb("sg_w", [P, SG_G, P])
        cw_rows = sb("cw_rows", [6, P])
        sb_rows = sb("sb_rows", [SG_G, P])
        vec_t = sb("vec_t2", [P, 6 + SG_G])
        ws_t = sb("ws_t", [P, SG_G, P])
        std = sb("std2", [P, T])
        sq_sum = sb("sq_sum2", [P, T])
        nat = sb("nat", [P, T, NAT_COLS])
        cbr = sb("cbr", [P, 4, 2, SEQ])
        sig_b = sb("sig_b", [P, 2, SEQ])
        zpad = sb("zpad", [P, 2, 2 + SEQ])
        cv = sb("cv", [P, 2, SEQ])
        sig = sb("sig_acd", [P, 3, T, GW])
        scr = sb("scr", [P, T, 512])
        stat = sb("stat", [P, T, 12])
        mean_v = sb("mean_v", [P, T])
        stat2 = sb("stat2", [P, T, 8])
        kr = sb("kr", [P, T, MLA_ROPE])
        c_t = sb("c_t", [P, 3, SEQ])
        q_nat = sb("q_nat", [P, T, MLA_H, MLA_QK])
        kv_nat = sb("kv_nat", [P, T, MLA_H, 2 * 64])
        k_nat = sb("k_nat", [P, T, MLA_H, MLA_QK])
        rope1 = sb("rope1", [P, T, 8, 16])
        rope2 = sb("rope2", [P, T, 8, 16])
        rope3 = sb("rope3", [P, T, 8, 16])
        mqk_t = sb("mqk_t", [MLA_QK, 2, MLA_H, SEQ])
        bqk_t = sb("bqk_t", [P, 2, 2, SEQ])
        e1 = sb("e1_2", [P, HEADS_2, SEQ])
        e0 = sb("e0_2", [P, HEADS_2, P])
        row16 = sb("row16_2", [P, 3, 2 * HEADS_2])
        a_t = sb("a_t2", [P, HEADS_2, 3, P])
        y_nat = K.h_t[:].rearrange("p k n -> p (k n)")[:, 0:T * 3 * GW].rearrange("p (t i n) -> p t i n", t=T, i=3)
        y_t = e1

        def seg(name, n):
            return nat[:, :, NAT[name]:NAT[name] + n]

        B, full, free = bank_plan(GROUPS_2, K.psum, sem, "2")
        filled = [Signal(sem(f"slot{s}_filled2")) for s in range(RING)]
        names = [c[0] for c in CHUNKS_2] + [("wo", 0), ("wo", 1)]
        names += [None] * (-len(names) % RING)
        readers = [READERS_2.get(n) if n in READERS_2 else ((n[0], n[1], 1) if n else None) for n in names]
        C, loads, arrived = {}, [], [0] * RING
        for i, name in enumerate(names):
            s = i % RING
            if name is None:
                continue
            arrived[s] += 32 if name == "n0" else 16
            C[name] = Chunk(K.slots[s], filled[s], arrived[s])
            earlier = [(j, readers[j]) for j in range(s, i, RING) if readers[j]]
            last = [readers[j] for j in range(s, len(names), RING) if readers[j]][-1]
            loads.append((name, s, earlier[-1][1] if earlier else None, last))
        for s in range(RING):
            filled[s].n = arrived[s]

        N_PARAMS = 14
        params = signal("params_loaded2", 16 * N_PARAMS)
        norm_loaded = signal("norm_g_loaded2", 16)
        x_out = signal("x_after_layer2", T, T)
        std_ready, xn_ready, ht_ready = signal("x_std_ready_2", T), signal("xn_ready_2", T), signal("ht_ready_2")
        vec_ready, wst_ready = signal("vec_t_ready2"), signal("ws_t_ready")
        cbr_ready, sig_acd_ready = signal("cbr_ready"), signal("sig_acd_ready")
        n0_ready, moba_nat_ready, sg_nat_ready = signal("n0_ready"), signal("moba_nat_ready"), signal("sg_nat_ready")
        stat_ready, stat_std_ready = signal("stat_ready", 3), signal("stat_std_ready", 3)
        stat_cols = [slice(0, 3), slice(3, 11), slice(11, 12)]
        c_ready, ct_ready, qkv_ready = signal("c_normed_ready"), signal("c_t_ready"), signal("q_kv_ready")
        stat2_ready, stat2_std_ready = signal("stat2_ready"), signal("stat2_std_ready")
        moba_ready, mla_ready, vn_ready = signal("moba_qk_ready"), signal("mla_qk_ready"), signal("vn_ready", 1, 1)
        qk_t_ready = signal("qk_t_ready2")
        max_ready, exp_ready, a_ready, at_ready = (signal("row_max_ready2"), signal("exp_ready2"), signal("a_ready2"),
                                                   signal("a_t_ready2"))
        y_ready, yt_ready = signal("y_nat_ready", 2), signal("y_t_ready")
        stored = sem("stored")

        block = ctx.enter_context(nc.Block())

        @block.sync
        def _(sp):
            for b in range(BANKS):
                sp.sem_inc(free[b].sem, 1)
                sp.sem_inc(full[b].sem, full[b].credit)
            sp.sem_inc(x_out.sem, T)
            sp.sem_inc(vn_ready.sem, 1)
            with sp.Fori(0, DEPTH) as l:
                for name, s, before, last in loads:
                    if before is None:
                        sp.wait_ge(B[last].full, B[last].full_before(l))
                    else:
                        sp.wait_ge(B[before].full, B[before].full_at(l))
                    if name in READERS_2:
                        _, col, n, _ = next(c for c in CHUNKS_2 if c[0] == name)
                        src = A["w_in_2"][ds(l, 1), :, col:col + n].rearrange("a (p k) n -> p (a k) n", k=KT)
                    else:
                        n = CHUNK
                        src = A["w_out_2"][ds(l, 1), :, name[1] * n:(name[1] + 1) * n].rearrange("a (k p) n -> p (a k) n", p=P)
                    for half in (slice(P // 2, P), slice(0, P // 2)) if name == "n0" else (slice(0, P),):
                        sp.dma_start(K.slots[s][half, :, 0:n], src[half]).then_inc(filled[s].sem, 16)
            for t in range(T):
                sp.wait_ge(x_out.sem, x_out.credit + (DEPTH - 1) * T + t + 1)
                sp.dma_start(out[0, t * P:(t + 1) * P, :], K.x[:, t, :]).then_inc(stored, 16)
            sp.wait_ge(stored, 16 * T)

        @block.gpsimd
        def _(pool):
            with pool.Fori(0, DEPTH) as l:
                pool.wait_ge(vn_ready.sem, vn_ready.at(l, 0))
                one = ds(l, 1)

                def load(dst, src):
                    pool.dma_start(dst, src).then_inc(params.sem, 16)

                pool.dma_start(norm_g[:], A["norm_g_2"][one].rearrange("a (p k) -> p (a k)", k=KT)).then_inc(norm_loaded.sem, 16)
                for dst, name in ((gain_cq, "mla_q_norm_g_2"), (gain_ckv, "mla_kv_norm_g_2"), (gain_kr, "mla_k_rope_g_2")):
                    load(dst[:], A[name][one].to_broadcast(list(dst.shape)))
                load(w_uq[:], A["mla_w_uq_2"][one].rearrange("a (k p) n -> p (a k) n", p=P))
                load(w_ukv[:], A["mla_w_ukv_2"][one].rearrange("a p n -> p (a n)"))
                load(cw_rows[:], A["conv_w_2"][one].rearrange("a k (c p) -> (a k c) p", p=P))
                load(sb_rows[:], A["sg_b_2"][one].rearrange("a g p -> (a g) p"))
                load(sg_w[:], A["sg_w_2"][one].rearrange("a g t s -> t (a g) s"))
                for w, name in enumerate(("moba_q_g_2", "moba_k_g_2")):
                    load(gain_moba[:, w, :], A[name][one].to_broadcast([P, MOBA_HD]))
                for dst, name in ((gain_q, "mla_q_g_2"), (gain_kn, "mla_k_nope_g_2"), (sg_gain, "sg_ln_g_2"), (sg_bias, "sg_ln_b_2")):
                    load(dst[:], A[name][one].to_broadcast(list(dst.shape)))

        @block.tensor
        def _(pe):
            def begin(name, l):
                pe.wait_ge(B[name].free, B[name].free_at(l))
                return B[name].tile

            def chunk(name, l):
                pe.wait_ge(C[name].filled, C[name].filled_at(l))
                return C[name].tile

            def rows(name, l, w, t, stationary, cols=CHUNK):
                bank = begin(name, l)
                for k in range(KT):
                    mm = nc.tensor.matmul(bank[:, 0:cols], stationary[:, k, t * P:(t + 1) * P], w[:, k, 0:cols],
                                          start=(k == 0), stop=(k == KT - 1))
                mm.then_inc(B[name].full, 1)

            def turn(name, l, pieces, size=P):
                bank = begin(name, l)
                for col, src in pieces:
                    mm = nc.tensor.transpose(bank[0:size, col:col + P], src, K.ident[:])
                mm.then_inc(B[name].full, 1)

            with pe.Fori(0, DEPTH) as l:
                def natural(name):
                    n = next(c[2] for c in CHUNKS_2 if c[0] == name)
                    w = chunk(name, l)
                    for t in range(T):
                        rows((name, t), l, w, t, K.h_t, n)

                def by_columns(name, pair):
                    w = chunk(name, l)
                    for i, group in enumerate(pair):
                        bank = begin(group, l)
                        for j in range(2):
                            c = 2 * i + j
                            for k in range(KT):
                                mm = nc.tensor.matmul(bank[:, j * SEQ:(j + 1) * SEQ], w[:, k, c * P:(c + 1) * P],
                                                      K.h_t[:, k, :], start=(k == 0), stop=(k == KT - 1))
                        mm.then_inc(B[group].full, 1)

                for t in range(T):
                    pe.wait_ge(xn_ready.sem, xn_ready.at(l, t + 1))
                    for g in range(4):
                        bank = begin(("xT", g), l) if t == 0 else B["xT", g].tile
                        for j in range(2):
                            mm = nc.tensor.transpose(bank[:, j * SEQ + t * P:j * SEQ + (t + 1) * P],
                                                     K.xn[:, t, 2 * g + j::KT], K.ident[:])
                        if t == T - 1:
                            mm.then_inc(B["xT", g].full, 1)
                pe.wait_ge(ht_ready.sem, ht_ready.at(l))
                natural("n0")
                natural("n3")
                pe.wait_ge(c_ready.sem, c_ready.at(l))
                turn("cqT", l, [(k * SEQ + t * P, nat[:, t, k * P:(k + 1) * P]) for k in range(2) for t in range(T)])
                turn("ckT", l, [(t * P, nat[:, t, NAT["ckv"]:NAT["ckv"] + P]) for t in range(T)])
                natural("n4")
                pe.wait_ge(params.sem, params.at(l, params.n))
                pe.wait_ge(ct_ready.sem, ct_ready.at(l))
                for t in range(T):
                    bank = begin(("q", t), l)
                    for k in range(2):
                        mm = nc.tensor.matmul(bank[:, 0:MLA_H * MLA_QK], c_t[:, k, t * P:(t + 1) * P], w_uq[:, k, :],
                                              start=(k == 0), stop=(k == 1))
                    mm.then_inc(B["q", t].full, 1)
                for t in range(T):
                    bank = begin(("kv", t), l)
                    nc.tensor.matmul(bank[:], c_t[:, 2, t * P:(t + 1) * P], w_ukv[:], start=True, stop=True)\
                        .then_inc(B["kv", t].full, 1)
                bank = begin("vec", l)
                turn("wsT", l, [(g * P, sg_w[:, g, :]) for g in range(SG_G)])
                nc.tensor.transpose(bank[:, 0:6], cw_rows[:], K.ident[0:6, 0:6])
                nc.tensor.transpose(bank[:, 6:6 + SG_G], sb_rows[:], K.ident[0:SG_G, 0:SG_G]).then_inc(B["vec"].full, 1)
                natural("n2")
                by_columns("t0", ("c_h", "c_b"))
                pe.wait_ge(moba_ready.sem, moba_ready.at(l))
                for w, name in enumerate(("mq", "mk")):
                    turn(("bT", w), l, [(i * SEQ + t * P, nat[:, t, NAT[name] + i * P:NAT[name] + (i + 1) * P])
                                        for i in range(2) for t in range(T)])
                pe.wait_ge(mla_ready.sem, mla_ready.at(l))
                for w, src in enumerate((q_nat, k_nat)):
                    for i in range(2):
                        turn(("mT", w, i), l, [(j * SEQ + t * P, src[:, t, 2 * i + j, :]) for j in range(2) for t in range(T)],
                             MLA_QK)
                pe.wait_ge(qk_t_ready.sem, qk_t_ready.at(l))
                for i in range(2):
                    bank = begin(("sm1", i), l)
                    for j in range(2):
                        mm = nc.tensor.matmul(bank[:, j * SEQ:(j + 1) * SEQ], mqk_t[:, 0, 2 * i + j, P:SEQ],
                                              mqk_t[:, 1, 2 * i + j, :], start=True, stop=True)
                    mm.then_inc(B["sm1", i].full, 1)
                bank = begin("sm0", l)
                for h in range(MLA_H):
                    mm = nc.tensor.matmul(bank[:, h * P:(h + 1) * P], mqk_t[:, 0, h, 0:P], mqk_t[:, 1, h, 0:P],
                                          start=True, stop=True)
                mm.then_inc(B["sm0"].full, 1)
                for n, q0, keys in (("sb1", P, SEQ), ("sb0", 0, P)):
                    for par in range(2):
                        part = slice(64 * par, 64 * par + 64)
                        bank = begin((n, par), l)
                        for i in range(2):
                            mm = nc.tensor.matmul(bank[:, i * keys:(i + 1) * keys], bqk_t[part, 0, i, q0:q0 + P],
                                                  bqk_t[part, 1, i, 0:keys], start=True, stop=True)
                        mm.then_inc(B[n, par].full, 1)
                by_columns("t1", ("c_c", "g_b"))
                natural("n1")
                natural("n5")
                pe.wait_ge(wst_ready.sem, wst_ready.at(l))
                pe.wait_ge(vn_ready.sem, vn_ready.at(l))
                for t in range(T):
                    bank = begin(("mix", t), l)
                    for g in range(SG_G):
                        mm = nc.tensor.matmul(bank[:, g * 64:(g + 1) * 64], ws_t[:, g, :], seg("sv", GW)[:, t, g * 64:(g + 1) * 64],
                                              start=True, stop=True)
                    mm.then_inc(B["mix", t].full, 1)
                pe.wait_ge(a_ready.sem, a_ready.at(l))
                for i in range(4):
                    turn(("aT1", i), l, [((2 * j + b) * P, e1[:, 2 * i + j, b * P:(b + 1) * P])
                                         for j in range(2) for b in range(2)])
                for i in range(2):
                    turn(("aT0", i), l, [(j * P, e0[:, 4 * i + j, :]) for j in range(4)])
                pe.wait_ge(at_ready.sem, at_ready.at(l))
                for t in range(T):
                    bank = begin(("o", t), l)
                    for r in range(HEADS_2):
                        if r < MLA_H:
                            col, values = r * 64, lambda b, r=r: kv_nat[:, b, r, 64:128]
                        else:
                            head = 2 * ((r - MLA_H) % 2) + (r - MLA_H) // 2
                            col, values = (MLA_H + head) * 64, lambda b, head=head: seg("mv", GW)[:, b, head * 64:(head + 1) * 64]
                        o = bank[:, col:col + 64]
                        if t == 0:
                            mm = nc.tensor.matmul(o, a_t[:, r, 0, :], values(0), start=True, stop=True)
                        else:
                            nc.tensor.matmul(o, a_t[:, r, 1, :], values(0), start=True, stop=False)
                            mm = nc.tensor.matmul(o, a_t[:, r, 2, :], values(1), start=False, stop=True)
                    mm.then_inc(B["o", t].full, 1)
                pe.wait_ge(y_ready.sem, y_ready.at(l, 1))
                for i in range(3):
                    turn(("yT", i), l, [(j * SEQ + t * P, y_nat[:, t, i, j * P:(j + 1) * P]) for j in range(2) for t in range(T)])
                pe.wait_ge(yt_ready.sem, yt_ready.at(l))
                pe.wait_ge(y_ready.sem, y_ready.at(l, 2))
                for t in range(T):
                    for h in range(2):
                        rows(("wo", h, t), l, chunk(("wo", h), l), t, y_t)

        @block.scalar
        def _(act):
            def full_of(name, l):
                act.wait_ge(B[name].full, B[name].full_at(l))
                return B[name].tile

            def copy_out(name, l, dst, src):
                nc.scalar.activation(dst, src, ACT.Copy).then_inc(B[name].free, 1)

            def pairs(bank):
                return bank[:].rearrange("p (c n) -> p c n", c=2)

            with act.Fori(0, DEPTH) as l:
                for t in range(T):
                    act.wait_ge(x_out.sem, x_out.at(l, t + 1 - T))
                    nc.scalar.activation(K.xn[:, t, :], K.x[:, t, :], ACT.Square, accum_out=sq_sum[:, t:t + 1])
                    act.drain()
                    nc.scalar.activation(std[:, t:t + 1], sq_sum[:, t:t + 1], ACT.Sqrt, scale=1.0 / D, bias=K.eps[:])\
                        .then_inc(std_ready.sem, 1)

                def natural(name):
                    _, _, n, place = next(c for c in CHUNKS_2 if c[0] == name)
                    for t in range(T):
                        bank = full_of((name, t), l)
                        copy_out((name, t), l, nat[:, t, place:place + n], bank[:, 0:n])

                def std_of(i):
                    act.wait_ge(stat_ready.sem, stat_ready.at(l, i + 1))
                    part = stat[:, :, stat_cols[i]]
                    nc.scalar.activation(part, part, ACT.Sqrt, bias=K.eps[:]).then_inc(stat_std_ready.sem, 1)

                natural("n0")
                act.drain().then_inc(n0_ready.sem, 1)
                std_of(0)
                natural("n3")
                bank = full_of("cqT", l)
                copy_out("cqT", l, c_t[:, 0:2, :], pairs(bank))
                bank = full_of("ckT", l)
                copy_out("ckT", l, c_t[:, 2, :], bank[:, 0:SEQ])
                act.drain().then_inc(ct_ready.sem, 1)
                natural("n4")
                act.drain().then_inc(moba_nat_ready.sem, 1)
                for t in range(T):
                    bank = full_of(("q", t), l)
                    copy_out(("q", t), l, q_nat[:, t].rearrange("p h n -> p (h n)"), bank[:, 0:MLA_H * MLA_QK])
                for t in range(T):
                    bank = full_of(("kv", t), l)
                    copy_out(("kv", t), l, kv_nat[:, t].rearrange("p h n -> p (h n)"), bank[:])
                act.drain().then_inc(qkv_ready.sem, 1)
                bank = full_of("vec", l)
                copy_out("vec", l, vec_t[:], bank[:, 0:6 + SG_G])
                act.drain().then_inc(vec_ready.sem, 1)
                std_of(1)
                natural("n2")
                act.drain().then_inc(sg_nat_ready.sem, 1)
                act.wait_ge(stat2_ready.sem, stat2_ready.at(l))
                nc.scalar.activation(stat2[:], stat2[:], ACT.Sqrt, bias=K.eps[:]).then_inc(stat2_std_ready.sem, 1)
                for i, name in enumerate(("c_h", "c_b")):
                    bank = full_of(name, l)
                    copy_out(name, l, cbr[:, i], pairs(bank))
                for w in range(2):
                    bank = full_of(("bT", w), l)
                    copy_out(("bT", w), l, bqk_t[:, w], pairs(bank))
                for w in range(2):
                    for i in range(2):
                        bank = full_of(("mT", w, i), l)
                        copy_out(("mT", w, i), l, mqk_t[:, w, 2 * i:2 * i + 2, :],
                                 bank[0:MLA_QK, :].rearrange("p (c n) -> p c n", c=2))
                act.drain().then_inc(qk_t_ready.sem, 1)
                std_of(2)
                bank = full_of("c_c", l)
                copy_out("c_c", l, cbr[:, 2], pairs(bank))
                act.wait_ge(max_ready.sem, max_ready.at(l))
                for r in range(2 * HEADS_2):
                    e = e1[:, r, :] if r < HEADS_2 else e0[:, r - HEADS_2, :]
                    scale = (MLA_QK if r % HEADS_2 < MLA_H else MOBA_HD) ** -0.5
                    nc.scalar.activation(e, e, ACT.Exp, bias=row16[:, 0, r:r + 1], scale=scale,
                                         accum_out=row16[:, 1, r:r + 1])
                act.drain().then_inc(exp_ready.sem, 1)
                bank = full_of("g_b", l)
                nc.scalar.activation(sig_b[:], pairs(bank), ACT.Sigmoid)
                copy_out("g_b", l, cbr[:, 3], pairs(bank))
                act.drain().then_inc(cbr_ready.sem, 1)
                natural("n1")
                natural("n5")
                act.drain()
                for i, name in enumerate(("ga", "gc", "gd")):
                    nc.scalar.activation(sig[:, i], seg(name, GW), ACT.Sigmoid)
                act.drain().then_inc(sig_acd_ready.sem, 1)
                for i in range(4):
                    bank = full_of(("aT1", i), l)
                    copy_out(("aT1", i), l, a_t[:, 2 * i:2 * i + 2, 1:3, :],
                             bank[:].rearrange("p (h b n) -> p h b n", h=2, b=2))
                for i in range(2):
                    bank = full_of(("aT0", i), l)
                    copy_out(("aT0", i), l, a_t[:, 4 * i:4 * i + 4, 0, :], bank[:].rearrange("p (h n) -> p h n", h=4))
                act.drain().then_inc(at_ready.sem, 1)
                for i, k in enumerate((0, 4, 6)):
                    bank = full_of(("yT", i), l)
                    copy_out(("yT", i), l, y_t[:, k:k + 2, :], pairs(bank))
                act.drain().then_inc(yt_ready.sem, 1)

        @block.vector
        def _(dve):
            v = nc.vector

            def full_of(name, l):
                dve.wait_ge(B[name].full, B[name].full_at(l))
                return B[name].tile

            def square_sums(dst, src, scratch, n):
                v.tensor_tensor(scratch, src, src, ALU.mult)
                dve.drain()
                v.tensor_reduce(dst, scratch, AX.X, ALU.add)
                dve.drain()
                v.tensor_scalar(dst, dst, 1.0 / n, None, ALU.mult)
                dve.drain()

            def rotate(x1, x2, o1, o2, freqs, heads, half):
                cos, sin = K.cos[:, :, freqs:freqs + half], K.sin[:, :, freqs:freqs + half]
                if heads:
                    cos, sin = broadcast(cos, 2, heads), broadcast(sin, 2, heads)
                    r1, r2, r3 = (r[:, :, 0:heads, 0:half] for r in (rope1, rope2, rope3))
                else:
                    r1, r2, r3 = (r[:, :, 0, 0:half] for r in (rope1, rope2, rope3))
                v.tensor_tensor(r1, x1, cos, ALU.mult)
                v.tensor_tensor(r2, x2, sin, ALU.mult)
                v.tensor_tensor(r3, x1, sin, ALU.mult)
                dve.drain()
                v.tensor_tensor(r1, r1, r2, ALU.subtract)
                dve.drain()
                v.tensor_tensor(r2, x2, cos, ALU.mult)
                dve.drain()
                v.tensor_copy(o1, r1)
                v.tensor_tensor(o2, r2, r3, ALU.add)
                dve.drain()

            v.memset(zpad[:, :, 0:2], 0.0)
            with dve.Fori(0, DEPTH) as l:
                for t in range(T):
                    dve.wait_ge(std_ready.sem, std_ready.at(l, t + 1))
                    v.reciprocal(std[:, t:t + 1], std[:, t:t + 1])
                    dve.drain()
                    v.tensor_scalar(K.xn[:, t, :], K.x[:, t, :], std[:, t:t + 1], None, ALU.mult)
                    dve.drain().then_inc(xn_ready.sem, 1)
                dve.wait_ge(norm_loaded.sem, norm_loaded.at(l, 16))
                for g in range(4):
                    bank = full_of(("xT", g), l)
                    for j in range(2):
                        k = 2 * g + j
                        ins = v.tensor_scalar(K.h_t[:, k, :], bank[:, j * SEQ:(j + 1) * SEQ], norm_g[:, k:k + 1], None, ALU.mult)
                    ins.then_inc(B["xT", g].free, 1)
                dve.drain().then_inc(ht_ready.sem, 1)
                dve.wait_ge(n0_ready.sem, n0_ready.at(l))
                square_sums(stat[:, :, 0], seg("cq", 256), scr[:, :, 0:256], 256)
                square_sums(stat[:, :, 1], seg("ckv", 128), scr[:, :, 0:128], 128)
                square_sums(stat[:, :, 2], seg("kr", MLA_ROPE), scr[:, :, 0:MLA_ROPE], MLA_ROPE)
                dve.drain().then_inc(stat_ready.sem, 1)
                dve.wait_ge(stat_std_ready.sem, stat_std_ready.at(l, 1))
                v.reciprocal(stat[:, :, stat_cols[0]], stat[:, :, stat_cols[0]])
                dve.drain()
                dve.wait_ge(params.sem, params.at(l, params.n))
                for i, (name, n, gain) in enumerate((("cq", 256, gain_cq), ("ckv", 128, gain_ckv), ("kr", MLA_ROPE, gain_kr))):
                    for t in range(T):
                        v.scalar_tensor_tensor(seg(name, n)[:, t, :], seg(name, n)[:, t, :], stat[:, t, i:i + 1], gain[:],
                                               ALU.mult, ALU.mult)
                dve.drain().then_inc(c_ready.sem, 1)
                krs = seg("kr", MLA_ROPE)
                rotate(krs[:, :, 0:16], krs[:, :, 16:32], kr[:, :, 0:16], kr[:, :, 16:32], ROPES[1][0], None, 16)
                dve.wait_ge(moba_nat_ready.sem, moba_nat_ready.at(l))
                moba = nat[:, :, NAT["mq"]:NAT["mq"] + 512].rearrange("p t (h n) -> p t h n", n=MOBA_HD)
                square_sums(stat[:, :, 3:11], moba, scr[:].rearrange("p t (h n) -> p t h n", n=MOBA_HD), MOBA_HD)
                dve.drain().then_inc(stat_ready.sem, 1)
                dve.wait_ge(stat_std_ready.sem, stat_std_ready.at(l, 2))
                v.reciprocal(stat[:, :, stat_cols[1]], stat[:, :, stat_cols[1]])
                dve.drain()
                v.tensor_tensor(moba, moba, broadcast(stat[:, :, 3:11], 3, MOBA_HD), ALU.mult)
                dve.drain()
                for w in range(2):
                    part = moba[:, :, 4 * w:4 * w + 4, :]
                    v.tensor_tensor(part, part, broadcast(broadcast(gain_moba[:, w, :], 1, 4), 1, T), ALU.mult)
                dve.drain()
                x1, x2 = moba[:, :, :, 0:8], moba[:, :, :, 8:16]
                rotate(x1, x2, x1, x2, ROPES[2][0], 8, 8)
                dve.drain().then_inc(moba_ready.sem, 1)
                bank = full_of("wsT", l)
                v.tensor_tensor(ws_t[:], bank[:].rearrange("p (g n) -> p g n", g=SG_G), broadcast(K.head[:], 1, SG_G), ALU.mult)\
                    .then_inc(B["wsT"].free, 1)
                dve.drain().then_inc(wst_ready.sem, 1)
                dve.wait_ge(qkv_ready.sem, qkv_ready.at(l))
                for t in range(T):
                    square_sums(stat2[:, t, 0:4], q_nat[:, t], scr[:, 0, 0:MLA_H * MLA_QK].rearrange("p (h n) -> p h n", h=MLA_H), MLA_QK)
                    square_sums(stat2[:, t, 4:8], kv_nat[:, t, :, 0:64], scr[:, 0, 0:MLA_H * 64].rearrange("p (h n) -> p h n", h=MLA_H), 64)
                dve.drain().then_inc(stat2_ready.sem, 1)
                dve.wait_ge(stat2_std_ready.sem, stat2_std_ready.at(l))
                v.reciprocal(stat2[:], stat2[:])
                dve.drain()
                for t in range(T):
                    v.tensor_tensor(q_nat[:, t], q_nat[:, t], broadcast(stat2[:, t, 0:4], 2, MLA_QK), ALU.mult)
                    v.tensor_tensor(k_nat[:, t, :, 0:64], kv_nat[:, t, :, 0:64], broadcast(stat2[:, t, 4:8], 2, 64), ALU.mult)
                    v.tensor_copy(k_nat[:, t, :, 64:], broadcast(kr[:, t, :], 1, MLA_H))
                dve.drain()
                for t in range(T):
                    v.tensor_tensor(q_nat[:, t], q_nat[:, t], broadcast(gain_q[:], 1, MLA_H), ALU.mult)
                    v.tensor_tensor(k_nat[:, t, :, 0:64], k_nat[:, t, :, 0:64], broadcast(gain_kn[:], 1, MLA_H), ALU.mult)
                dve.drain()
                q1, q2 = q_nat[:, :, :, 64:80], q_nat[:, :, :, 80:96]
                rotate(q1, q2, q1, q2, ROPES[1][0], MLA_H, 16)
                dve.drain().then_inc(mla_ready.sem, 1)
                dve.wait_ge(sg_nat_ready.sem, sg_nat_ready.at(l))
                v.tensor_reduce(mean_v[:], seg("sv", GW), AX.X, ALU.add)
                dve.drain()
                v.tensor_scalar(mean_v[:], mean_v[:], 1.0 / GW, None, ALU.mult)
                dve.drain()
                for t in range(T):
                    v.tensor_scalar(seg("sv", GW)[:, t, :], seg("sv", GW)[:, t, :], mean_v[:, t:t + 1], None, ALU.subtract)
                dve.drain()
                square_sums(stat[:, :, 11], seg("sv", GW), scr[:, :, 0:GW], GW)
                dve.drain().then_inc(stat_ready.sem, 1)
                dve.wait_ge(stat_std_ready.sem, stat_std_ready.at(l, 3))
                v.reciprocal(stat[:, :, stat_cols[2]], stat[:, :, stat_cols[2]])
                dve.drain()
                for t in range(T):
                    v.scalar_tensor_tensor(seg("sv", GW)[:, t, :], seg("sv", GW)[:, t, :], stat[:, t, 11:12], sg_gain[:],
                                           ALU.mult, ALU.mult)
                dve.drain()
                v.tensor_tensor(seg("sv", GW), seg("sv", GW), broadcast(sg_bias[:], 1, T), ALU.add)
                dve.drain().then_inc(vn_ready.sem, 1)
                for r0, groups in ((0, [("sm1", 0), ("sm1", 1)]), (MLA_H, [("sb1", 0), ("sb1", 1)])):
                    if r0:
                        src = full_of("sm0", l)[:].rearrange("p (h n) -> p h n", h=4)
                        v.tensor_tensor(e0[:, 0:4, :], src, broadcast(K.causal_neg[:], 1, 4), ALU.add).then_inc(B["sm0"].free, 1)
                    for i, name in enumerate(groups):
                        src = full_of(name, l)[:].rearrange("p (h n) -> p h n", h=2)
                        dst = e1[:, r0 + 2 * i:r0 + 2 * i + 2, :]
                        v.tensor_copy(dst[:, :, 0:P], src[:, :, 0:P])
                        v.tensor_tensor(dst[:, :, P:SEQ], src[:, :, P:SEQ], broadcast(K.causal_neg[:], 1, 2), ALU.add)\
                            .then_inc(B[name].free, 1)
                for par in range(2):
                    src = full_of(("sb0", par), l)[:, 0:2 * P].rearrange("p (h n) -> p h n", h=2)
                    v.tensor_tensor(e0[:, MLA_H + 2 * par:MLA_H + 2 * par + 2, :], src, broadcast(K.causal_neg[:], 1, 2), ALU.add)\
                        .then_inc(B["sb0", par].free, 1)
                dve.drain()
                v.tensor_reduce(row16[:, 0, 0:HEADS_2], e1[:], AX.X, ALU.max)
                v.tensor_reduce(row16[:, 0, HEADS_2:], e0[:], AX.X, ALU.max)
                dve.drain()
                for r0 in (0, HEADS_2):
                    v.tensor_scalar(row16[:, 0, r0:r0 + 4], row16[:, 0, r0:r0 + 4], -MLA_QK ** -0.5, None, ALU.mult)
                    v.tensor_scalar(row16[:, 0, r0 + 4:r0 + 8], row16[:, 0, r0 + 4:r0 + 8], -MOBA_HD ** -0.5, None, ALU.mult)
                dve.drain().then_inc(max_ready.sem, 1)
                dve.wait_ge(exp_ready.sem, exp_ready.at(l))
                v.reciprocal(row16[:, 2, :], row16[:, 1, :])
                dve.drain()
                for e, c, n in ((e1[:], 0, SEQ), (e0[:], HEADS_2, P)):
                    v.tensor_tensor(e, e, broadcast(row16[:, 2, c:c + HEADS_2], 2, n), ALU.mult)
                dve.drain().then_inc(a_ready.sem, 1)
                dve.wait_ge(sig_acd_ready.sem, sig_acd_ready.at(l))
                for i, name in enumerate(("ga", "gc", "gd")):
                    v.tensor_tensor(sig[:, i], sig[:, i], seg(name, GW), ALU.mult)
                dve.drain()
                dve.wait_ge(vec_ready.sem, vec_ready.at(l))
                dve.wait_ge(cbr_ready.sem, cbr_ready.at(l))
                v.tensor_tensor(zpad[:, :, 2:], cbr[:, 2], cbr[:, 0], ALU.mult)
                dve.drain()
                for k in range(3):
                    for c in range(2):
                        w = vec_t[:, 2 * k + c:2 * k + c + 1]
                        if k == 0:
                            v.tensor_scalar(cv[:, c, :], zpad[:, c, 0:SEQ], w, None, ALU.mult)
                        else:
                            v.scalar_tensor_tensor(cv[:, c, :], zpad[:, c, k:k + SEQ], w, cv[:, c, :], ALU.mult, ALU.add)
                    dve.drain()
                v.tensor_tensor(cv[:], cv[:], cbr[:, 1], ALU.mult)
                v.tensor_tensor(sig_b[:], sig_b[:], cbr[:, 3], ALU.mult)
                dve.drain()
                for t in range(T):
                    bank = full_of(("mix", t), l)
                    for g in range(SG_G):
                        col = slice(g * 64, (g + 1) * 64)
                        ins = v.scalar_tensor_tensor(y_nat[:, t, 1, col], bank[:, col], vec_t[:, 6 + g:7 + g],
                                                     seg("su", GW)[:, t, col], ALU.add, ALU.mult)
                    ins.then_inc(B["mix", t].free, 1)
                dve.drain()
                v.tensor_tensor(y_nat[:, :, 1], y_nat[:, :, 1], sig[:, 1], ALU.mult)
                for t in range(T):
                    bank = full_of(("o", t), l)
                    v.tensor_tensor(y_nat[:, t, 0], bank[:, 0:GW], sig[:, 0, t], ALU.mult)
                    v.tensor_tensor(y_nat[:, t, 2], bank[:, GW:2 * GW], sig[:, 2, t], ALU.mult).then_inc(B["o", t].free, 1)
                dve.drain().then_inc(y_ready.sem, 1)
                v.tensor_tensor(y_t[:, 2:4, :], cv[:], sig_b[:], ALU.mult)
                dve.drain().then_inc(y_ready.sem, 1)
                for t in range(T):
                    for h in range(2):
                        col = slice(h * CHUNK, (h + 1) * CHUNK)
                        bank = full_of(("wo", h, t), l)
                        v.tensor_tensor(K.x[:, t, col], K.x[:, t, col], bank[:], ALU.add).then_inc(B["wo", h, t].free, 1)
                    dve.drain().then_inc(x_out.sem, 1)


class Kept:
    pass


def build(nc, A, out):
    with ExitStack() as ctx:
        K = Kept()

        def keep(name, shape, dt=F32):
            return ctx.enter_context(nc.sbuf_tensor(name, shape, dt))

        K.x = keep("x_tokens", [P, T, D])
        K.xn = keep("xn", [P, T, D])
        K.h_t = keep("h_t", [P, KT, SEQ])
        ring = keep("weight_ring", [P, RING, KT, CHUNK])
        K.slots = [ring[:, s] for s in range(RING)]
        K.ident = keep("ident", [P, P])
        K.ones = keep("ones", [P, P])
        K.mean_conv = keep("mean_conv", [P, P])
        K.causal_neg = keep("causal_neg", [P, P])
        K.strict_neg = keep("strict_neg", [P, P])
        K.strict_01 = keep("strict_01", [P, P])
        K.tail = keep("tail", [P, P])
        K.head = keep("head", [P, P])
        K.lower8 = keep("lower8", [P, N_GROUPS, N_GROUPS])
        K.eps = keep("eps", [P, 1])
        K.lam_init = keep("lam_init", [P, DEPTH])
        K.lam_rest = keep("lam_rest", [P, DEPTH])
        K.sin = keep("sin", [P, T, N_FREQ])
        K.cos = keep("cos", [P, T, N_FREQ])
        K.c_act = keep("c_act", [P, KT])
        K.ramp = keep("ramp", [P, SLOTS + 1])
        K.part = keep("part", [P, 1])
        K.strict_twice = keep("strict_twice", [P, 2, N_EXPERTS])
        K.part_share = keep("part_share", [P, 1])
        K.minus_slots = keep("minus_slots", [P, P])
        K.full_rounds = keep("full_rounds", [P, ROUNDS])
        K.table = keep("block_table", [P, BLOCK_COLS], I32)
        K.last_turn = keep("last_turn", [P, DEPTH], I32)
        K.first_turn = keep("first_turn", [P, DEPTH + 1], I32)
        K.first_turn_f = keep("first_turn_f", [P, DEPTH + 1])
        psum = ctx.enter_context(nc.psum_tensor("banks", [P, BANKS, 512], F32))
        K.psum = [psum[:, b] for b in range(BANKS)]
        first_block(nc, A, K)
        second_block(nc, A, K, out)


INPUTS = [
    "x", "c", "positions", "w_mod", "b_mod", "norm_mix_g", "norm_ffn_g", "w_in", "qn_g", "kn_g", "lam_q1", "lam_k1",
    "lam_q2", "lam_k2", "subln_g", "w_proj_a", "w_dw", "b_dw", "conv_ln_g", "conv_ln_b", "w_proj_b", "b_proj_b",
    "w_proj_c", "w_out", "w_router", "b_router", "w1", "w3", "w2", "ws1", "ws3", "ws2", "positions_2", "norm_g_2",
    "w_in_2", "mla_q_norm_g_2", "mla_w_uq_2", "mla_kv_norm_g_2", "mla_w_ukv_2", "mla_q_g_2", "mla_k_nope_g_2",
    "mla_k_rope_g_2", "conv_w_2", "sg_ln_g_2", "sg_ln_b_2", "sg_w_2", "sg_b_2", "moba_q_g_2", "moba_k_g_2", "w_out_2",
]


def kernel(**inputs):
    from concourse import bacc
    from concourse.bass_utils import run_bass_kernel_spmd

    nc = bacc.Bacc("TRN2", target_bir_lowering=False, num_devices=1)
    arrays, A = {}, {}
    for name in INPUTS:
        a = np.ascontiguousarray(inputs[name])
        arrays[f"in_{name}"] = a
        A[name] = nc.dram_tensor(f"in_{name}", a.shape, mybir.dt.from_np(a.dtype), kind="ExternalInput").ap()
    out = nc.dram_tensor("out", (1, SEQ, D), F32, kind="ExternalOutput").ap()
    build(nc, A, out)
    result = run_bass_kernel_spmd(nc, [arrays], core_ids=[0])
    return result.results[0]["out"]
```
